# Optimizing a Trainium2 kernel written in Bass

```python
import math
import jax, jax.numpy as jnp
from jax import lax
import numpy as np

D_MODEL = 1024
BATCH = 1
SEQ = 1024
DEPTH = 1

CTX_LEN = 256
GRID_W = 64
N_MOD = 6
D_FF = 4 * D_MODEL
CHUNK = 64
NORM_EPS = 1e-6

HY_C = D_MODEL // 4
HY_ORDER = 2
HY_SHORT = 3
HY_EMB = 33
HY_FH = 64
HY_DECAY_TARGET = 1e-2
HY_FAST_PCT = 0.3
HY_SLOW_PCT = 1.5

GLA_H = 4
GLA_VW = 3 * D_MODEL // 8
GLA_KW = GLA_VW // 2
GLA_DK = GLA_KW // GLA_H
GLA_DV = GLA_VW // GLA_H
GLA_RANK = 16
GLA_TAU = 16.0

GDN_H = 4
GDN_W = 3 * D_MODEL // 8
GDN_D = GDN_W // GDN_H
GDN_SHORT = 7

D_MIX = HY_C + GLA_VW + GDN_W
HY_IN = 3 * HY_C
GLA_IN = 2 * GLA_KW + 2 * GLA_VW + 2 * GLA_RANK
GDN_IN = 4 * GDN_W + 4 * GDN_H
IN_SIZES = (HY_IN, GLA_IN, GDN_IN)
N_IN = HY_IN + GLA_IN + GDN_IN


F32 = jnp.float32

def split_last(t, sizes):
    return jnp.split(t, np.cumsum(sizes)[:-1].tolist(), axis=-1)

def rmsnorm(x, g):
    xf = x.astype(F32)
    y = xf * lax.rsqrt(jnp.mean(xf * xf, axis=-1, keepdims=True) + NORM_EPS)
    return (y * g.astype(F32)).astype(x.dtype)

def modulate(x, g, shift, scale):
    return rmsnorm(x, g) * (1 + scale) + shift

def to_heads(t, n_heads):
    b, l, _ = t.shape
    return t.reshape(b, l, n_heads, -1).transpose(0, 2, 1, 3)

def from_heads(t):
    b, h, l, d = t.shape
    return t.transpose(0, 2, 1, 3).reshape(b, l, h * d)

def l2norm(t):
    return t * lax.rsqrt(jnp.sum(t * t, axis=-1, keepdims=True) + NORM_EPS)

def short_conv(u, w, n_seg, seg_len):
    b, l, ch = u.shape
    k = w.shape[0]
    us = u.reshape(b * n_seg, seg_len, ch)
    out = lax.conv_general_dilated(us, w[:, None, :].astype(u.dtype), window_strides=(1,),
                                   padding=[(k // 2, k // 2)], dimension_numbers=('NWC', 'WIO', 'NWC'),
                                   feature_group_count=ch)
    return out.reshape(b, l, ch)

def hyena_filters(length, w1, b1, w2, b2, w3, sin_freq):
    t = jnp.linspace(0.0, 1.0, length, dtype=F32)[:, None]
    bands = (HY_EMB - 1) // 2
    f = jnp.linspace(1e-4, bands - 1, bands, dtype=F32)
    w = 2 * math.pi * jnp.arange(length, dtype=F32) / length
    ang = w[:, None] * f[None, :]
    z = jnp.concatenate([t, jnp.cos(ang), -jnp.sin(ang)], axis=-1)
    h = jnp.sin(sin_freq[0].astype(F32) * (z @ w1.astype(F32) + b1.astype(F32)))
    h = jnp.sin(sin_freq[1].astype(F32) * (h @ w2.astype(F32) + b2.astype(F32)))
    h = (h @ w3.astype(F32)).reshape(length, HY_ORDER, 2, HY_C)
    deltas = jnp.abs(jnp.linspace(math.log(HY_DECAY_TARGET) / HY_SLOW_PCT,
                                  math.log(HY_DECAY_TARGET) / HY_FAST_PCT, HY_C, dtype=F32))
    h = h * jnp.exp(-t * deltas[None, :])[:, None, None, :]
    h_fwd, h_bwd = h[:, :, 0], h[:, :, 1]
    return jnp.concatenate([h_fwd, jnp.zeros_like(h_fwd[:1]), h_bwd[:0:-1]], axis=0)

def hyena_mix(z, n_seg, seg_len, conv_w, conv_b, filt, d_skip):
    u = (short_conv(z, conv_w, n_seg, seg_len) + conv_b).astype(F32)
    v, x1, x2 = jnp.split(u, 3, axis=-1)
    l = u.shape[1]
    filt_f = jnp.fft.rfft(filt, axis=0)
    y = v
    for o, gate in enumerate((x1, x2)):
        conv = jnp.fft.irfft(jnp.fft.rfft(y, n=2 * l, axis=1) * filt_f[None, :, o], n=2 * l, axis=1)[:, :l]
        y = gate * (conv + d_skip[o].astype(F32) * y)
    return y.astype(z.dtype)

def to_chunks(t, n):
    return jnp.moveaxis(t.reshape(t.shape[:2] + (n, CHUNK) + t.shape[3:]), 2, 0)

def from_chunks(t):
    t = jnp.moveaxis(t, 0, 2)
    return t.reshape(t.shape[:2] + (-1,) + t.shape[4:])

def gla_chunk_scan(q, k, v, log_a, s0):
    n = q.shape[2] // CHUNK
    mask = jnp.tril(jnp.ones((CHUNK, CHUNK), bool))[:, :, None]

    def step(s, xs):
        qc, kc, vc, ac = xs
        b = jnp.cumsum(ac, axis=2)
        diff = b[:, :, :, None, :] - b[:, :, None, :, :]
        decay = jnp.exp(jnp.where(mask, diff, -jnp.inf))
        attn = jnp.einsum('bhid,bhjd,bhijd->bhij', qc, kc, decay)
        o = jnp.einsum('bhid,bhde->bhie', qc * jnp.exp(b), s) + jnp.einsum('bhij,bhje->bhie', attn, vc)
        b_last = b[:, :, -1:, :]
        s_new = jnp.exp(b_last[:, :, 0, :])[..., None] * s + jnp.einsum(
            'bhjd,bhje->bhde', kc * jnp.exp(b_last - b), vc)
        return s_new, o

    s_fin, o = lax.scan(step, s0, (to_chunks(q, n), to_chunks(k, n), to_chunks(v, n), to_chunks(log_a, n)))
    return from_chunks(o), s_fin

def gdn_chunk_scan(q, k, v, g, beta, s0):
    n = q.shape[2] // CHUNK
    dk = q.shape[-1]
    strict = jnp.tril(jnp.ones((CHUNK, CHUNK), bool), -1)
    incl = jnp.tril(jnp.ones((CHUNK, CHUNK), bool))
    eye = jnp.eye(CHUNK, dtype=F32)

    def step(s, xs):
        qc, kc, vc, gc, bc = xs
        gcum = jnp.cumsum(gc, axis=-1)
        diff = gcum[..., :, None] - gcum[..., None, :]
        kb = kc * bc[..., None]
        a = -jnp.einsum('bhid,bhjd->bhij', kb, kc) * jnp.exp(jnp.where(strict, diff, -jnp.inf))
        rhs = jnp.concatenate([kb * jnp.exp(gcum)[..., None], vc * bc[..., None]], axis=-1)
        sol = lax.linalg.triangular_solve(eye - a, rhs, left_side=True, lower=True, unit_diagonal=True)
        w, u = sol[..., :dk], sol[..., dk:]
        v_new = u - w @ s
        attn = jnp.einsum('bhid,bhjd->bhij', qc, kc) * jnp.exp(jnp.where(incl, diff, -jnp.inf))
        o = (qc * jnp.exp(gcum)[..., None]) @ s + attn @ v_new
        g_last = gcum[..., -1:]
        s_new = jnp.exp(g_last)[..., None] * s + jnp.einsum(
            'bhjd,bhje->bhde', kc * jnp.exp(g_last - gcum)[..., None], v_new)
        return s_new, o

    s_fin, o = lax.scan(step, s0, (to_chunks(q, n), to_chunks(k, n), to_chunks(v, n),
                                   to_chunks(g, n), to_chunks(beta, n)))
    return from_chunks(o), s_fin

def bidir_scan(scan_fn, shared, fwd, bwd, s0_f, s0_b):
    o_f, s_f = scan_fn(*shared, *fwd, s0_f)
    flip = lambda a: jnp.flip(a, axis=2)
    o_b, s_b = scan_fn(*[flip(a) for a in shared], *[flip(a) for a in bwd], s0_b)
    return o_f + flip(o_b), s_f, s_b

def gated_head_norm(o, gate, g_norm):
    y = o * lax.rsqrt(jnp.mean(o * o, axis=-1, keepdims=True) + NORM_EPS) * g_norm.astype(F32)
    return from_heads(y) * jax.nn.silu(gate.astype(F32))

def gla_prep(z, w_a2, b_a):
    zf = z.astype(F32)
    q, k, v, gate, a_f, a_b = split_last(zf, (GLA_KW, GLA_KW, GLA_VW, GLA_VW, GLA_RANK, GLA_RANK))
    log_a = [to_heads(jax.nn.log_sigmoid(a @ w_a2[d].astype(F32) + b_a[d].astype(F32)) / GLA_TAU, GLA_H)
             for d, a in enumerate((a_f, a_b))]
    shared = (to_heads(q, GLA_H) * GLA_DK ** -0.5, to_heads(k, GLA_H), to_heads(v, GLA_H))
    return shared, (log_a[0],), (log_a[1],), gate

def gla_branch(z_lat, z_ctx, with_ctx_out, w_a2, b_a, norm_g):
    sh_c, fw_c, bw_c, gate_c = gla_prep(z_ctx, w_a2, b_a)
    s0 = jnp.zeros((z_ctx.shape[0], GLA_H, GLA_DK, GLA_DV), F32)
    o_c, s_f, s_b = bidir_scan(gla_chunk_scan, sh_c, fw_c, bw_c, s0, s0)
    sh_l, fw_l, bw_l, gate_l = gla_prep(z_lat, w_a2, b_a)
    o_l, _, _ = bidir_scan(gla_chunk_scan, sh_l, fw_l, bw_l, s_f, s_b)
    out_lat = gated_head_norm(o_l, gate_l, norm_g).astype(z_lat.dtype)
    out_ctx = gated_head_norm(o_c, gate_c, norm_g).astype(z_ctx.dtype) if with_ctx_out else None
    return out_lat, out_ctx

def gdn_prep(z, conv_w, a_log, dt_bias, n_seg, seg_len):
    qkv, gate, a_f, a_b, b_f, b_b = split_last(z, (3 * GDN_W, GDN_W, GDN_H, GDN_H, GDN_H, GDN_H))
    qkv = jax.nn.silu(short_conv(qkv, conv_w, n_seg, seg_len)).astype(F32)
    q, k, v = jnp.split(qkv, 3, axis=-1)
    shared = (l2norm(to_heads(q, GDN_H)) * GDN_D ** -0.5, l2norm(to_heads(k, GDN_H)), to_heads(v, GDN_H))

    def log_decay(a, d):
        return (-jnp.exp(a_log[d].astype(F32)) *
                jax.nn.softplus(a.astype(F32) + dt_bias[d].astype(F32))).transpose(0, 2, 1)

    def write_gate(b):
        return jax.nn.sigmoid(b.astype(F32)).transpose(0, 2, 1)

    return shared, (log_decay(a_f, 0), write_gate(b_f)), (log_decay(a_b, 1), write_gate(b_b)), gate

def gdn_branch(z_lat, z_ctx, rows, with_ctx_out, conv_w, a_log, dt_bias, norm_g):
    sh_c, fw_c, bw_c, gate_c = gdn_prep(z_ctx, conv_w, a_log, dt_bias, 1, z_ctx.shape[1])
    s0 = jnp.zeros((z_ctx.shape[0], GDN_H, GDN_D, GDN_D), F32)
    o_c, s_f, s_b = bidir_scan(gdn_chunk_scan, sh_c, fw_c, bw_c, s0, s0)
    sh_l, fw_l, bw_l, gate_l = gdn_prep(z_lat, conv_w, a_log, dt_bias, rows, GRID_W)
    o_l, _, _ = bidir_scan(gdn_chunk_scan, sh_l, fw_l, bw_l, s_f, s_b)
    out_lat = gated_head_norm(o_l, gate_l, norm_g).astype(z_lat.dtype)
    out_ctx = gated_head_norm(o_c, gate_c, norm_g).astype(z_ctx.dtype) if with_ctx_out else None
    return out_lat, out_ctx

def mixer(h, hc, rows, with_ctx_out, w_in, w_out, hy_conv_w, hy_conv_b, hy_filter, hy_d,
          gla_w_a2, gla_b_a, gla_norm_g, gdn_conv_w, gdn_a_log, gdn_dt_bias, gdn_norm_g):
    zl_hy, zl_gla, zl_gdn = split_last(h @ w_in, IN_SIZES)
    zc_hy, zc_gla, zc_gdn = split_last(hc @ w_in, IN_SIZES)
    hy_lat = hyena_mix(zl_hy, rows, GRID_W, hy_conv_w, hy_conv_b, hyena_filters(h.shape[1], *hy_filter), hy_d)
    gla_lat, gla_ctx = gla_branch(zl_gla, zc_gla, with_ctx_out, gla_w_a2, gla_b_a, gla_norm_g)
    gdn_lat, gdn_ctx = gdn_branch(zl_gdn, zc_gdn, rows, with_ctx_out, gdn_conv_w, gdn_a_log, gdn_dt_bias, gdn_norm_g)
    y_lat = jnp.concatenate([hy_lat, gla_lat, gdn_lat], axis=-1) @ w_out
    if not with_ctx_out:
        return y_lat, None
    hy_ctx = hyena_mix(zc_hy, 1, hc.shape[1], hy_conv_w, hy_conv_b, hyena_filters(hc.shape[1], *hy_filter), hy_d)
    y_ctx = jnp.concatenate([hy_ctx, gla_ctx, gdn_ctx], axis=-1) @ w_out
    return y_lat, y_ctx

def sq_relu_mlp(h, w1, w2):
    return jnp.square(jax.nn.relu(h @ w1)) @ w2

def first_inputs(seed: int = 0) -> dict:
    key = jax.random.key(seed)
    ks = iter(jax.random.split(key, 32))
    nrm = lambda shape, std: std * jax.random.normal(next(ks), shape, F32)
    dt = jnp.exp(jax.random.uniform(next(ks), (DEPTH, 2, GDN_H), F32, math.log(1e-3), math.log(1e-1)))
    return {
        'x': nrm((BATCH, SEQ, D_MODEL), 1.0),
        'c': nrm((BATCH, D_MODEL), 1.0),
        'ctx': nrm((BATCH, CTX_LEN, D_MODEL), 1.0),
        'c_ctx': nrm((D_MODEL,), 1.0),
        'norm1_g': 1.0 + nrm((DEPTH, D_MODEL), 0.05),
        'norm2_g': 1.0 + nrm((DEPTH, D_MODEL), 0.05),
        'w_mod': nrm((DEPTH, D_MODEL, N_MOD * D_MODEL), D_MODEL ** -0.5),
        'b_mod': nrm((DEPTH, N_MOD * D_MODEL), 0.02),
        'w_in': nrm((DEPTH, D_MODEL, N_IN), D_MODEL ** -0.5),
        'w_out': nrm((DEPTH, D_MIX, D_MODEL), D_MIX ** -0.5),
        'hy_conv_w': nrm((DEPTH, HY_SHORT, HY_IN), HY_SHORT ** -0.5),
        'hy_conv_b': nrm((DEPTH, HY_IN), 0.02),
        'hy_f_w1': nrm((DEPTH, HY_EMB, HY_FH), HY_EMB ** -0.5),
        'hy_f_b1': nrm((DEPTH, HY_FH), 0.02),
        'hy_f_w2': nrm((DEPTH, HY_FH, HY_FH), HY_FH ** -0.5),
        'hy_f_b2': nrm((DEPTH, HY_FH), 0.02),
        'hy_f_w3': nrm((DEPTH, HY_FH, HY_ORDER * 2 * HY_C), 0.05 * HY_FH ** -0.5),
        'hy_sin_freq': 1.0 + nrm((DEPTH, 2, HY_FH), 0.05),
        'hy_d': nrm((DEPTH, HY_ORDER, HY_C), 1.0),
        'gla_w_a2': nrm((DEPTH, 2, GLA_RANK, GLA_KW), GLA_RANK ** -0.5),
        'gla_b_a': nrm((DEPTH, 2, GLA_KW), 0.02),
        'gla_norm_g': 1.0 + nrm((DEPTH, GLA_DV), 0.05),
        'gdn_conv_w': nrm((DEPTH, GDN_SHORT, 3 * GDN_W), GDN_SHORT ** -0.5),
        'gdn_a_log': jnp.log(jax.random.uniform(next(ks), (DEPTH, 2, GDN_H), F32, 1.0, 16.0)),
        'gdn_dt_bias': dt + jnp.log(-jnp.expm1(-dt)),
        'gdn_norm_g': 1.0 + nrm((DEPTH, GDN_D), 0.05),
        'w_mlp1': nrm((DEPTH, D_MODEL, D_FF), D_MODEL ** -0.5),
        'w_mlp2': nrm((DEPTH, D_FF, D_MODEL), D_FF ** -0.5),
        'final_norm_g': 1.0 + nrm((D_MODEL,), 0.05),
    }

def first_block(x, c, ctx, c_ctx, norm1_g, norm2_g, w_mod, b_mod, w_in, w_out, hy_conv_w, hy_conv_b,
              hy_f_w1, hy_f_b1, hy_f_w2, hy_f_b2, hy_f_w3, hy_sin_freq, hy_d, gla_w_a2, gla_b_a, gla_norm_g,
              gdn_conv_w, gdn_a_log, gdn_dt_bias, gdn_norm_g, w_mlp1, w_mlp2, final_norm_g):
    rows = x.shape[1] // GRID_W
    silu_c = jax.nn.silu(c)
    silu_cc = jax.nn.silu(c_ctx)
    for l in range(DEPTH):
        with_ctx_out = l < DEPTH - 1
        sh1, sc1, g1, sh2, sc2, g2 = jnp.split((silu_c @ w_mod[l] + b_mod[l])[:, None, :], N_MOD, axis=-1)
        csh1, csc1, cg1, csh2, csc2, cg2 = jnp.split(silu_cc @ w_mod[l] + b_mod[l], N_MOD, axis=-1)
        h = modulate(x, norm1_g[l], sh1, sc1)
        hc = modulate(ctx, norm1_g[l], csh1, csc1)
        hy_filter = (hy_f_w1[l], hy_f_b1[l], hy_f_w2[l], hy_f_b2[l], hy_f_w3[l], hy_sin_freq[l])
        y, yc = mixer(h, hc, rows, with_ctx_out, w_in[l], w_out[l], hy_conv_w[l], hy_conv_b[l], hy_filter,
                      hy_d[l], gla_w_a2[l], gla_b_a[l], gla_norm_g[l], gdn_conv_w[l], gdn_a_log[l],
                      gdn_dt_bias[l], gdn_norm_g[l])
        x = x + g1 * y
        x = x + g2 * sq_relu_mlp(modulate(x, norm2_g[l], sh2, sc2), w_mlp1[l], w_mlp2[l])
        if with_ctx_out:
            ctx = ctx + cg1 * yc
            ctx = ctx + cg2 * sq_relu_mlp(modulate(ctx, norm2_g[l], csh2, csc2), w_mlp1[l], w_mlp2[l])
    return rmsnorm(x, final_norm_g)


DEPTH_2 = 2

ATT_HEADS = 8
ATT_KV_HEADS = 2
ATT_HEAD_DIM = 64
ATT_WIDTH = ATT_HEADS * ATT_HEAD_DIM
KV_WIDTH = ATT_KV_HEADS * ATT_HEAD_DIM
WINDOW = 128
BLOCK = 128
ROPE_BASE = 10000.0
M_HEADS = 4
M_HEAD_DIM = 128
M_WIDTH = M_HEADS * M_HEAD_DIM
CONV_K = 5
CHUNK_2 = 128
N_DIR = 2
MIX_WIDTH = ATT_WIDTH + M_WIDTH
EPS = 1e-6
SPLIT_SIZES = (ATT_WIDTH, KV_WIDTH, KV_WIDTH, ATT_WIDTH, M_WIDTH, M_WIDTH, M_WIDTH, M_WIDTH, M_WIDTH, N_DIR * M_HEADS, N_DIR * M_HEADS)
IN_COLS = 2 * ATT_WIDTH + 2 * KV_WIDTH + 5 * M_WIDTH + 2 * N_DIR * M_HEADS


def rmsnorm_2(x, g):
    xf = x.astype(jnp.float32)
    y = xf * lax.rsqrt(jnp.mean(xf * xf, axis=-1, keepdims=True) + EPS)
    return (y * g.astype(jnp.float32)).astype(x.dtype)

def project(xn, w_in):
    idx = np.cumsum(SPLIT_SIZES)[:-1].tolist()
    return jnp.split(xn @ w_in, idx, axis=-1)

def axial_rope_tables(T):
    rows = T // GRID_W
    row = jnp.repeat(jnp.arange(rows), GRID_W).astype(jnp.float32)
    col = jnp.tile(jnp.arange(GRID_W), rows).astype(jnp.float32)
    half = ATT_HEAD_DIM // 2
    inv = ROPE_BASE ** (-jnp.arange(0, half, 2, dtype=jnp.float32) / half)
    ang_r = row[:, None] * inv
    ang_c = col[:, None] * inv
    return (jnp.cos(ang_r)[:, None, :], jnp.sin(ang_r)[:, None, :],
            jnp.cos(ang_c)[:, None, :], jnp.sin(ang_c)[:, None, :])

def rope_2d(u, tables):
    cos_r, sin_r, cos_c, sin_c = [t.astype(u.dtype) for t in tables]

    def rot(a, cos, sin):
        a1, a2 = jnp.split(a, 2, axis=-1)
        return jnp.concatenate([a1 * cos - a2 * sin, a2 * cos + a1 * sin], axis=-1)

    ur, uc = jnp.split(u, 2, axis=-1)
    return jnp.concatenate([rot(ur, cos_r, sin_r), rot(uc, cos_c, sin_c)], axis=-1)

def window_ctx_attention(q, k, v, kc, vc, sink):
    B, T, H, dh = q.shape
    G = H // ATT_KV_HEADS
    NB = T // BLOCK
    scale = dh ** -0.5
    qb = q.reshape(B, NB, BLOCK, ATT_KV_HEADS, G, dh)
    pad = ((0, 0), (BLOCK, BLOCK), (0, 0), (0, 0))
    kp = jnp.pad(k, pad).reshape(B, NB + 2, BLOCK, ATT_KV_HEADS, dh)
    vp = jnp.pad(v, pad).reshape(B, NB + 2, BLOCK, ATT_KV_HEADS, dh)
    kw = jnp.concatenate([kp[:, :-2], kp[:, 1:-1], kp[:, 2:]], axis=2)
    vw = jnp.concatenate([vp[:, :-2], vp[:, 1:-1], vp[:, 2:]], axis=2)
    s_win = jnp.einsum('bnqhgd,bnkhd->bhgnqk', qb, kw).astype(jnp.float32) * scale
    qpos = jnp.arange(NB)[:, None, None] * BLOCK + jnp.arange(BLOCK)[None, :, None]
    kpos = (jnp.arange(NB)[:, None, None] - 1) * BLOCK + jnp.arange(3 * BLOCK)[None, None, :]
    valid = (jnp.abs(qpos - kpos) <= WINDOW) & (kpos >= 0) & (kpos < T)
    s_win = jnp.where(valid, s_win, -jnp.inf)
    s_ctx = jnp.einsum('bnqhgd,bchd->bhgnqc', qb, kc).astype(jnp.float32) * scale
    s_sink = jnp.broadcast_to(sink.astype(jnp.float32).reshape(1, ATT_KV_HEADS, G, 1, 1, 1),
                              s_win.shape[:-1] + (1,))
    p = jax.nn.softmax(jnp.concatenate([s_win, s_ctx, s_sink], axis=-1), axis=-1)
    Lw = 3 * BLOCK
    Lc = kc.shape[1]
    p_win = p[..., :Lw].astype(v.dtype)
    p_ctx = p[..., Lw:Lw + Lc].astype(v.dtype)
    out = (jnp.einsum('bhgnqk,bnkhd->bnqhgd', p_win, vw)
           + jnp.einsum('bhgnqc,bchd->bnqhgd', p_ctx, vc))
    return out.reshape(B, T, H * dh)

def ctx_attention(qc, kc, vc, sink):
    B, Lc, H, dh = qc.shape
    G = H // ATT_KV_HEADS
    qg = qc.reshape(B, Lc, ATT_KV_HEADS, G, dh)
    s = jnp.einsum('bqhgd,bkhd->bhgqk', qg, kc).astype(jnp.float32) * dh ** -0.5
    s_sink = jnp.broadcast_to(sink.astype(jnp.float32).reshape(1, ATT_KV_HEADS, G, 1, 1),
                              s.shape[:-1] + (1,))
    p = jax.nn.softmax(jnp.concatenate([s, s_sink], axis=-1), axis=-1)
    out = jnp.einsum('bhgqk,bkhd->bqhgd', p[..., :Lc].astype(vc.dtype), vc)
    return out.reshape(B, Lc, H * dh)

def dwconv(u, w, b):
    C = u.shape[-1]
    y = lax.conv_general_dilated(u, w[:, None, :].astype(u.dtype), window_strides=(1,),
                                 padding=[(CONV_K // 2, CONV_K // 2)],
                                 dimension_numbers=('NWC', 'WIO', 'NWC'), feature_group_count=C)
    return y + b.astype(u.dtype)

def mlstm_init_state(B):
    N = N_DIR * B * M_HEADS
    return (jnp.zeros((N, M_HEAD_DIM, M_HEAD_DIM), jnp.float32),
            jnp.zeros((N, M_HEAD_DIM), jnp.float32),
            jnp.full((N,), -jnp.inf, jnp.float32))

def mlstm_chunkwise(q, k, v, i_pre, f_pre, state):
    N, T, dh = q.shape
    NC = T // CHUNK_2
    f32 = jnp.float32

    def chunks(u):
        return u.astype(f32).reshape((N, NC, CHUNK_2) + u.shape[2:]).swapaxes(0, 1)

    qc = chunks(q)
    kc = chunks(k) * dh ** -0.5
    vc = chunks(v)
    lf = chunks(jax.nn.log_sigmoid(f_pre.astype(f32)))
    ic = chunks(i_pre)
    lower = jnp.tril(jnp.ones((CHUNK_2, CHUNK_2), bool))

    def step(carry, inp):
        C, n, m = carry
        qq, kk, vv, lfc, ii = inp
        b = jnp.cumsum(lfc, axis=-1)
        dmat = jnp.where(lower, b[:, :, None] - b[:, None, :] + ii[:, None, :], -jnp.inf)
        inter = b + m[:, None]
        m_t = jnp.maximum(inter, jnp.max(dmat, axis=-1))
        w_inter = jnp.exp(inter - m_t)
        qk = jnp.einsum('ntd,nsd->nts', qq, kk) * jnp.exp(dmat - m_t[:, :, None])
        num = (w_inter[..., None] * jnp.einsum('nvd,ntd->ntv', C, qq)
               + jnp.einsum('nts,nsv->ntv', qk, vv))
        den = w_inter * jnp.einsum('nd,ntd->nt', n, qq) + qk.sum(-1)
        h = num / jnp.maximum(jnp.abs(den), jnp.exp(-m_t))[..., None]
        bL = b[:, -1]
        g = bL[:, None] - b + ii
        m_new = jnp.maximum(bL + m, jnp.max(g, axis=-1))
        a = jnp.exp(bL + m - m_new)
        w = jnp.exp(g - m_new[:, None])
        C_new = a[:, None, None] * C + jnp.einsum('ns,nsv,nsd->nvd', w, vv, kk)
        n_new = a[:, None] * n + jnp.einsum('ns,nsd->nd', w, kk)
        return (C_new, n_new, m_new), h

    state, h = lax.scan(step, state, (qc, kc, vc, lf, ic))
    h = h.swapaxes(0, 1).reshape(N, T, dh)
    return h.astype(q.dtype), state

def mlstm_bidir(q, k, v, i_pre, f_pre, state):
    B, T, _ = q.shape

    def heads(u):
        u = u.reshape(B, T, M_HEADS, M_HEAD_DIM).transpose(0, 2, 1, 3)
        return jnp.stack([u, jnp.flip(u, axis=2)]).reshape(N_DIR * B * M_HEADS, T, M_HEAD_DIM)

    def gates(gt):
        gt = gt.reshape(B, T, N_DIR, M_HEADS).transpose(2, 0, 3, 1)
        return jnp.stack([gt[0], jnp.flip(gt[1], axis=-1)]).reshape(N_DIR * B * M_HEADS, T)

    h, state = mlstm_chunkwise(heads(q), heads(k), heads(v), gates(i_pre), gates(f_pre), state)
    h = h.reshape(N_DIR, B, M_HEADS, T, M_HEAD_DIM)
    h = h[0] + jnp.flip(h[1], axis=2)
    return h.transpose(0, 2, 1, 3).reshape(B, T, M_WIDTH), state

def mlstm_post(h, o_pre, z, head_g):
    B, T, _ = h.shape
    h = jax.nn.sigmoid(o_pre) * h
    hh = rmsnorm_2(h.reshape(B, T, M_HEADS, M_HEAD_DIM), head_g.reshape(M_HEADS, M_HEAD_DIM))
    return hh.reshape(B, T, M_WIDTH) * jax.nn.silu(z)

def mlstm_qk(mq, mk, conv_w, conv_b):
    qk = jax.nn.silu(dwconv(jnp.concatenate([mq, mk], axis=-1), conv_w, conv_b))
    return jnp.split(qk, 2, axis=-1)

def hybrid_layer(x, ctx, mod_x, mod_c, tables, norm_g, w_in, conv_w, conv_b, gate_b, sink,
                 head_g, w_out, last):
    shift_x, scale_x, gate_x = mod_x
    shift_c, scale_c, gate_c = mod_c
    B, T, _ = x.shape
    Lc = ctx.shape[1]
    b_i, b_f = jnp.split(gate_b, 2)
    xn = rmsnorm_2(x, norm_g) * (1 + scale_x) + shift_x
    cn = rmsnorm_2(ctx, norm_g) * (1 + scale_c) + shift_c
    aq, ak, av, az, mq, mk, mv, mo, mz, mi, mf = project(xn, w_in)
    caq, cak, cav, caz, cmq, cmk, cmv, cmo, cmz, cmi, cmf = project(cn, w_in)

    q = rope_2d(aq.reshape(B, T, ATT_HEADS, ATT_HEAD_DIM), tables)
    k = rope_2d(ak.reshape(B, T, ATT_KV_HEADS, ATT_HEAD_DIM), tables)
    v = av.reshape(B, T, ATT_KV_HEADS, ATT_HEAD_DIM)
    kc = cak.reshape(B, Lc, ATT_KV_HEADS, ATT_HEAD_DIM)
    vc = cav.reshape(B, Lc, ATT_KV_HEADS, ATT_HEAD_DIM)
    att_x = window_ctx_attention(q, k, v, kc, vc, sink) * jax.nn.silu(az)

    cq, ck = mlstm_qk(cmq, cmk, conv_w, conv_b)
    xq, xk = mlstm_qk(mq, mk, conv_w, conv_b)
    h_ctx, ctx_state = mlstm_bidir(cq, ck, cmv, cmi + b_i, cmf + b_f, mlstm_init_state(B))
    h_lat, _ = mlstm_bidir(xq, xk, mv, mi + b_i, mf + b_f, ctx_state)
    m_x = mlstm_post(h_lat, mo, mz, head_g)

    out_x = jnp.concatenate([att_x, m_x], axis=-1) @ w_out
    x = x + gate_x * out_x
    if not last:
        qc = caq.reshape(B, Lc, ATT_HEADS, ATT_HEAD_DIM)
        att_c = ctx_attention(qc, kc, vc, sink) * jax.nn.silu(caz)
        m_c = mlstm_post(h_ctx, cmo, cmz, head_g)
        out_c = jnp.concatenate([att_c, m_c], axis=-1) @ w_out
        ctx = ctx + gate_c * out_c
    return x, ctx

def second_inputs(seed: int = 0) -> dict:
    key = jax.random.key(seed)
    ks = jax.random.split(key, 16)
    f32 = jnp.float32
    nrm = lambda k, s: jax.random.normal(k, s, f32)
    f_bias = jnp.tile(jnp.linspace(3.0, 6.0, M_HEADS), N_DIR)
    gate_b = jnp.concatenate([0.1 * nrm(ks[8], (DEPTH_2, N_DIR * M_HEADS)),
                              f_bias[None, :] + 0.1 * nrm(ks[9], (DEPTH_2, N_DIR * M_HEADS))], axis=-1)
    return {
        "x": nrm(ks[0], (BATCH, SEQ, D_MODEL)),
        "c": nrm(ks[1], (BATCH, D_MODEL)),
        "ctx": nrm(ks[2], (BATCH, CTX_LEN, D_MODEL)),
        "c_ctx": nrm(ks[3], (D_MODEL,)),
        "w_ada": 0.5 * D_MODEL ** -0.5 * nrm(ks[4], (DEPTH_2, D_MODEL, 3 * D_MODEL)),
        "b_ada": 0.01 * nrm(ks[5], (DEPTH_2, 3 * D_MODEL)),
        "norm_g": 1.0 + 0.02 * nrm(ks[6], (DEPTH_2, D_MODEL)),
        "w_in": D_MODEL ** -0.5 * nrm(ks[7], (DEPTH_2, D_MODEL, IN_COLS)),
        "conv_w": CONV_K ** -0.5 * nrm(ks[10], (DEPTH_2, CONV_K, 2 * M_WIDTH)),
        "conv_b": 0.01 * nrm(ks[11], (DEPTH_2, 2 * M_WIDTH)),
        "gate_b": gate_b,
        "sink": 0.5 * nrm(ks[12], (DEPTH_2, ATT_HEADS)),
        "head_g": 1.0 + 0.02 * nrm(ks[13], (DEPTH_2, M_WIDTH)),
        "w_out": MIX_WIDTH ** -0.5 * nrm(ks[14], (DEPTH_2, MIX_WIDTH, D_MODEL)),
        "final_g": 1.0 + 0.02 * nrm(ks[15], (D_MODEL,)),
    }

def second_block(x, c, ctx, c_ctx, w_ada, b_ada, norm_g, w_in, conv_w, conv_b, gate_b, sink,
              head_g, w_out, final_g):
    T = x.shape[1]
    tables = axial_rope_tables(T)
    sc = jax.nn.silu(c)
    scc = jax.nn.silu(c_ctx)
    for l in range(DEPTH_2):
        mod_x = jnp.split((sc @ w_ada[l] + b_ada[l])[:, None, :], 3, axis=-1)
        mod_c = jnp.split(scc @ w_ada[l] + b_ada[l], 3, axis=-1)
        x, ctx = hybrid_layer(x, ctx, mod_x, mod_c, tables, norm_g[l], w_in[l], conv_w[l],
                              conv_b[l], gate_b[l], sink[l], head_g[l], w_out[l],
                              last=(l == DEPTH_2 - 1))
    return rmsnorm_2(x, final_g)


def setup_inputs(seed=0):
    out = dict(first_inputs(seed))
    for name, value in second_inputs(seed + 1).items():
        if name != "x":
            out[name + "_2"] = value
    return out


def reference(
    x, c, ctx, c_ctx, norm1_g, norm2_g, w_mod, b_mod, w_in, w_out, hy_conv_w, hy_conv_b,
    hy_f_w1, hy_f_b1, hy_f_w2, hy_f_b2, hy_f_w3, hy_sin_freq, hy_d, gla_w_a2, gla_b_a,
    gla_norm_g, gdn_conv_w, gdn_a_log, gdn_dt_bias, gdn_norm_g, w_mlp1, w_mlp2, final_norm_g,
    c_2, ctx_2, c_ctx_2, w_ada_2, b_ada_2, norm_g_2, w_in_2, conv_w_2, conv_b_2, gate_b_2,
    sink_2, head_g_2, w_out_2, final_g_2,
):
    x = first_block(
        x, c, ctx, c_ctx, norm1_g, norm2_g, w_mod, b_mod, w_in, w_out, hy_conv_w, hy_conv_b,
        hy_f_w1, hy_f_b1, hy_f_w2, hy_f_b2, hy_f_w3, hy_sin_freq, hy_d, gla_w_a2, gla_b_a,
        gla_norm_g, gdn_conv_w, gdn_a_log, gdn_dt_bias, gdn_norm_g, w_mlp1, w_mlp2,
        final_norm_g,
    )
    return second_block(
        x, c_2, ctx_2, c_ctx_2, w_ada_2, b_ada_2, norm_g_2, w_in_2, conv_w_2, conv_b_2,
        gate_b_2, sink_2, head_g_2, w_out_2, final_g_2,
    )


_drawn_inputs = setup_inputs


def setup_inputs(seed=0):
    import zlib

    import numpy as np

    out = dict(_drawn_inputs(seed))
    spreads = {}
    factors = {'hy_conv_b': 2.907,
     'hy_sin_freq': 2.827,
     'gla_b_a': 8.0,
     'gla_norm_g': 4.985,
     'gdn_norm_g': 4.729,
     'b_ada_2': 6.131,
     'norm_g_2': 8.0,
     'conv_b_2': 64.0,
     'sink_2': 8.0,
     'head_g_2': 8.0,
     'final_g_2': 8.17}
    for name, (base, spread) in spreads.items():
        noise = np.random.default_rng([zlib.crc32(name.encode()), seed]).standard_normal(out[name].shape)
        drawn = base * np.exp(spread * noise) if base else spread * noise
        out[name] = __import__('jax').numpy.asarray(drawn.astype(out[name].dtype))
    for name, factor in factors.items():
        out[name] = (out[name] * factor).astype(out[name].dtype)
    return out
```

```python
import math
from contextlib import ExitStack

import numpy as np
import concourse.bass as bass
from concourse import mybir

F32 = mybir.dt.float32
I32 = mybir.dt.int32
ALU = mybir.AluOpType
ACT = mybir.ActivationFunctionType
AXX = mybir.AxisListType.X

T, TC, TT = 1024, 256, 1280
D = 1024
NEG = -1.0e30
BLKS = [(0, 512), (512, 512), (1024, 256)]
ENGINES = ("pe", "act", "dve", "pool", "sp")


class Item:

    __slots__ = ("eng", "fn", "after", "need", "val", "lane")

    def __init__(self, eng, fn, after, lane=None):
        self.eng, self.fn, self.after, self.lane = eng, fn, after, lane
        self.need, self.val = False, 0


class Calls:

    def matmul(self, *a, **k):
        return lambda e: e.matmul(*a, **k)

    def transpose(self, *a, **k):
        return lambda e: e.transpose(*a, **k)

    def activation(self, *a, **k):
        return lambda e: e.activation(*a, **k)

    def tensor_copy(self, *a, **k):
        return lambda e: e.tensor_copy(*a, **k)

    def tensor_tensor(self, *a, **k):
        return lambda e: e.tensor_tensor(*a, **k)

    def tensor_scalar(self, *a, **k):
        return lambda e: e.tensor_scalar(*a, **k)

    def scalar_tensor_tensor(self, *a, **k):
        return lambda e: e.scalar_tensor_tensor(*a, **k)

    def tensor_reduce(self, *a, **k):
        return lambda e: e.tensor_reduce(*a, **k)

    def tensor_tensor_scan(self, *a, **k):
        return lambda e: e.tensor_tensor_scan(*a, **k)

    def copy_predicated(self, *a, **k):
        return lambda e: e.copy_predicated(*a, **k)

    def reciprocal(self, *a, **k):
        return lambda e: e.reciprocal(*a, **k)

    def memset(self, *a, **k):
        return lambda e: e.memset(*a, **k)

    def dma_start(self, *a, **k):
        return lambda e: e.dma_start(*a, **k)


CALLS = Calls()


class Prog:

    def __init__(self, nc, ctx):
        self.nc, self.ctx = nc, ctx
        self.q = {e: [] for e in ENGINES}
        self.sem = {e: ctx.enter_context(nc.semaphore(f"s_{e}")) for e in ENGINES if e != "sp"}
        self.lanes = {}
        self.fence = {e: [] for e in ENGINES}
        self.outs = []

    def add(self, eng, fn, after, lane=None):
        flat = []
        for a in after:
            if isinstance(a, (list, tuple)):
                flat += [x for x in a if x is not None]
            elif a is not None:
                flat.append(a)
        flat += self.fence[eng]
        self.fence[eng] = []
        it = Item(eng, fn(CALLS), flat, lane)
        for a in flat:
            a.need = True
        self.q[eng].append(it)
        return it

    def pe(self, fn, *after):
        return self.add("pe", fn, after)

    def act(self, fn, *after):
        return self.add("act", fn, after + tuple(self.q["act"][-1:]))

    def dve(self, fn, *after):
        return self.add("dve", fn, after + tuple(x for x in self.q["dve"][-1:]))

    def pool(self, fn, *after):
        return self.add("pool", fn, after + tuple(self.q["pool"][-1:]))

    def dma(self, lane, fn, *after, eng="sp"):
        if lane not in self.lanes:
            self.lanes[lane] = [self.ctx.enter_context(self.nc.semaphore(f"l_{lane}")), 0]
        it = self.add(eng, fn, after, lane)
        self.lanes[lane][1] += 16
        it.val = self.lanes[lane][1]
        return it

    def barrier(self):
        last = []
        for e in ENGINES:
            comp = [x for x in self.q[e] if x.lane is None]
            last += comp[-1:]
        last += [x for x in self.pending if x is not None]
        self.pending = []
        for e in ENGINES:
            self.fence[e] = self.fence[e] + last

    pending = []

    def emit(self, block):
        for e in ENGINES:
            n = 0
            for it in self.q[e]:
                if it.lane is None and it.need:
                    n += 1
                    it.val = n

        def run(e, eng):
            seen = {}
            for it in self.q[e]:
                for a in it.after:
                    key = ("lane", a.lane) if a.lane is not None else a.eng
                    if seen.get(key, 0) >= a.val:
                        continue
                    seen[key] = a.val
                    sem = self.lanes[a.lane][0] if a.lane is not None else self.sem[a.eng]
                    eng.wait_ge(sem, a.val)
                ins = it.fn(eng)
                if it.lane is not None:
                    ins.then_inc(self.lanes[it.lane][0], 16)
                elif it.need:
                    ins.then_inc(self.sem[e], 1)
            if e == "sp":
                for a in self.outs:
                    eng.wait_ge(self.lanes[a.lane][0], a.val)

        block.tensor(lambda eng: run("pe", eng))
        block.scalar(lambda eng: run("act", eng))
        block.vector(lambda eng: run("dve", eng))
        block.gpsimd(lambda eng: run("pool", eng))
        block.sync(lambda eng: run("sp", eng))


class Slot:

    def __init__(self, ap, lane=None):
        self.ap, self.free, self.lane, self.held = ap, [], lane, False

    def take(self):
        assert not self.held, "taken twice"
        self.held = True
        f, self.free = self.free, []
        return f

    def give(self, *toks):
        assert self.held
        self.held = False
        self.free = [t for t in toks if t is not None]


class Ring:
    def __init__(self, slots):
        self.slots, self.n = slots, 0

    def next(self):
        s = self.slots[self.n % len(self.slots)]
        self.n += 1
        return s, s.take()


def interleave(gens):
    gens = list(gens)
    while gens:
        for g in list(gens):
            try:
                next(g)
            except StopIteration:
                gens.remove(g)


def constants():
    c = {}
    f = np.float32
    c["c_ident"] = np.eye(128, dtype=f)
    sel = np.zeros((128, 8, 128), f)
    for d in range(2):
        for h in range(4):
            sel[32 * d + h, 4 * d + h, :] = 1.0
    c["c_sel"] = sel.reshape(128, 1024)
    rst = np.ones((128, 2, TT), f)
    rst[:, 0, 0::128] = 0.0
    rst[:, 1, 127::128] = 0.0
    c["c_rst"] = rst.reshape(128, 2 * TT)
    j, i = np.meshgrid(np.arange(128), np.arange(128), indexing="ij")
    mt = np.zeros((128, 2, 128), f)
    mt[:, 0] = np.where(i >= j, 0.0, NEG)
    mt[:, 1] = np.where(i <= j, 0.0, NEG)
    c["c_mt"] = mt.reshape(128, 256)
    lv = np.zeros((128, 2, 7, 128), f)
    for n in range(7):
        s = 1 << n
        same = (i // (2 * s)) == (j // (2 * s))
        lv[:, 0, n] = same & (j % (2 * s) < s) & (i % (2 * s) >= s)
        lv[:, 1, n] = same & (j % (2 * s) >= s) & (i % (2 * s) < s)
    c["c_lv"] = lv.reshape(128, 2 * 7 * 128)
    pm = np.zeros((128, 2, 4, 128), np.int32)
    pm[:, 0] = (i >= j)[:, None, :]
    pm[:, 1] = (i <= j)[:, None, :]
    c["c_pm"] = pm.reshape(128, 1024)
    sg = np.ones((128, 1), f)
    sg[64:] = -1.0
    c["c_sgn"] = sg
    q = np.arange(128)[:, None]
    k = np.arange(384)[None, :] - 128
    c["c_wm"] = np.where(np.abs(q - k) <= 128, 0.0, NEG).astype(f)
    inv = (10000.0 ** (-np.arange(0, 32, 2, dtype=f) / f(32))).astype(f)
    row = np.repeat(np.arange(T // 64), 64).astype(f)
    col = np.tile(np.arange(64), T // 64).astype(f)
    cos = np.zeros((128, T), f)
    sin = np.zeros((128, T), f)
    rt = np.zeros((128, 128), f)
    for p in range(128):
        dd = p % 64
        pos = row if dd < 32 else col
        ang = (pos * inv[dd % 16]).astype(f)
        cos[p], sin[p] = np.cos(ang), np.sin(ang)
        if dd % 32 < 16:
            rt[p + 16, p] = -1.0
        else:
            rt[p - 16, p] = 1.0
    c["c_cos"], c["c_sin"], c["c_rot"] = cos, sin, rt
    tt = np.linspace(0.0, 1.0, T, dtype=f)[:, None]
    fr = np.linspace(1e-4, 15, 16, dtype=f)
    w = (f(2 * math.pi) * np.arange(T, dtype=f) / f(T)).astype(f)
    ang = (w[:, None] * fr[None, :]).astype(f)
    z = np.concatenate([tt, np.cos(ang), -np.sin(ang)], axis=-1).astype(f)
    c["c_z"] = np.ascontiguousarray(z.T)
    deltas = np.abs(np.linspace(math.log(1e-2) / 1.5, math.log(1e-2) / 0.3, 256, dtype=f))
    dec = np.exp((-tt * deltas[None, :]).astype(f)).astype(f)
    perm = np.concatenate([np.arange(0, T, 2), np.arange(1, T, 2)])
    c["c_dec"] = np.ascontiguousarray(dec[perm])
    kk = np.arange(512)[None, :].astype(np.float64)
    tm = np.zeros((4, 512, 512))
    for e in range(2):
        t = (2 * np.arange(512) + e)[:, None].astype(np.float64)
        a = math.pi * (2 * kk + 1) * t / 2048.0
        tm[2 * e], tm[2 * e + 1] = np.cos(a), np.sin(a)
    c["c_dft"] = tm.astype(f)
    c["c_idft"] = (tm.transpose(0, 2, 1) / 1024.0).astype(f)
    return {k: np.ascontiguousarray(v) for k, v in c.items()}


SMALL_ROWS = {
    0: [("b_mod", 48), ("norm1_g", 8), ("norm2_g", 8), ("final_norm_g", 8), ("hy_conv_b", 6), ("c", 8),
        ("c_ctx", 8), ("c_2", 8), ("c_ctx_2", 8)],
    1: [("b_ada_2", 48), ("norm_g_2", 16), ("conv_b_2", 16), ("final_g_2", 8)],
    2: [("hy_conv_w", 18), ("conv_w_2", 80)],
    3: [("gdn_conv_w", 63)],
}


def build(nc, A, out):
    ctx = ExitStack()
    with ctx:
        P = Prog(nc, ctx)
        P.pending = []
        emit_all(nc, ctx, P, A, out)
        with nc.Block() as block:
            P.emit(block)


class Arena:
    def __init__(self, t, lo, hi):
        self.t, self.lo, self.hi, self.at = t, lo, hi, lo

    def reset(self, at=None):
        self.at = self.lo if at is None else at

    def get(self, *dims, parts=128, dt=F32):
        n = int(np.prod(dims))
        assert self.at + n <= self.hi, ("arena", self.at, n, self.hi)
        ap = self.t[0:parts, self.at:self.at + n]
        self.at += n
        if dt is not F32:
            ap = ap.bitcast(dt)
        if len(dims) == 2:
            ap = ap.rearrange("p (a b) -> p a b", a=dims[0])
        elif len(dims) == 3:
            ap = ap.rearrange("p (a b c) -> p a b c", a=dims[0], b=dims[1])
        return ap


def emit_all(nc, ctx, P, A, out):
    pe, act, dve, pool = P.pe, P.act, P.dve, P.pool

    total = 52800
    big = ctx.enter_context(nc.sbuf_tensor("big", [128, total], F32))
    psum = [ctx.enter_context(nc.psum_tensor(f"ps{i}", [128, 512], F32)) for i in range(8)]
    PSL = [Slot(p) for p in psum]
    xs = nc.dram_tensor("xs_scratch", [128, 8, TT], F32, kind="Internal").ap()
    hs = nc.dram_tensor("hs_scratch", [128, 8, TT], F32, kind="Internal").ap()

    CON = Arena(big, 0, 5900)
    ringm = Arena(big, 5900, 5900 + 4 * 2048)
    M0 = 14092
    R1 = Arena(big, total - 10240, total)
    CAT = Arena(big, M0, M0 + 10240)
    BR = Arena(big, M0 + 10240, total - 10240)

    W = Ring([Slot(ringm.get(2048), lane=f"w{i}") for i in range(4)])

    def wload(src, kt, n, parts=128):
        s, free = W.next()
        view = s.ap[0:parts, 0:kt * n].rearrange("p (k n) -> p k n", k=kt)
        tok = P.dma(s.lane, lambda e: e.dma_start(view, src), *free)
        return s, view, tok

    def wcols(w, c0, n, kt=8):
        return w.rearrange("(k p) n -> p k n", p=128)[:, 0:kt, c0:c0 + n]

    def load(lane, dst, src, *after):
        return P.dma(lane, lambda e: e.dma_start(dst, src), *after, eng="pool")

    def store(lane, dst, src, *after):
        it = P.dma(lane, lambda e: e.dma_start(dst, src), *after, eng="pool")
        P.pending.append(it)
        return it

    ident = CON.get(128)
    ones = CON.get(128)
    sel = CON.get(8, 128)
    rst = CON.get(2, TT)
    mt = CON.get(2, 128)
    sgn = CON.get(1)
    vec = [CON.get(128) for _ in range(4)]
    modc = CON.get(48, 2)
    adac = CON.get(2, 24, 2)
    nA = CON.get(2, 8)
    nB = CON.get(2, 8)
    sc = CON.get(2, 8, 2)
    cst = [load("cst", ident, A["c_ident"]), load("cst", sel, A["c_sel"].rearrange("p (a b) -> p a b", a=8)),
           load("cst", rst, A["c_rst"].rearrange("p (a b) -> p a b", a=2)),
           load("cst", mt, A["c_mt"].rearrange("p (a b) -> p a b", a=2)), load("cst", sgn, A["c_sgn"])]
    stage = [BR.get(128) for _ in range(4)]
    z = [dve(lambda e, s=s: e.memset(s, 0.0)) for s in stage]
    offs = {}
    for n, rows in SMALL_ROWS.items():
        r = 0
        for name, k in rows:
            src = A[name]
            flat = src.rearrange(" ".join("abcd"[:len(src.shape)]) + " -> (" + " ".join("abcd"[:len(src.shape)]) + ")") \
                if len(src.shape) > 1 else src
            cst.append(load("cst", stage[n][r:r + k, :], flat.rearrange("(r q) -> r q", q=128), z[n]))
            offs[name] = (n, r)
            r += k
    ok = cst[-1]
    dve(lambda e: e.memset(ones, 1.0))
    vt = []
    for n in range(4):
        t = pe(lambda e, n=n: e.transpose(psum[n][:, 0:128], stage[n], ident), ok)
        vt.append(dve(lambda e, n=n: e.tensor_copy(vec[n], psum[n][:, 0:128]), t))

    def col(name, j, n=1):
        k, r = offs[name]
        return vec[k][:, r + j:r + j + n]

    for b, names in enumerate((("c", "c_ctx"), ("c_2", "c_ctx_2"))):
        for k, nm in enumerate(names):
            sctok = act(lambda e, b=b, k=k, nm=nm: e.activation(sc[:, b, :, k], col(nm, 0, 8), ACT.Silu), vt)
    P.barrier()
    BR.reset()

    def modulation(w, b, n, bias, dst, bank):
        for j in range(0, n, 2):
            s, wv, tok = wload(wcols(w, 128 * j, 256), 8, 256)
            for m in range(2):
                for k in range(8):
                    last = pe(lambda e, m=m, k=k, j=j, wv=wv: e.matmul(
                        bank[:, 2 * (j + m):2 * (j + m) + 2], wv[:, k, 128 * m:128 * m + 128], sc[:, b, k, :],
                        start=(k == 0), stop=(k == 7)), tok, sctok)
            s.give(last)
        pv = bank[:, 0:2 * n].rearrange("p (j c) -> p j c", c=2)
        for k in range(2):
            last = dve(lambda e, k=k: e.tensor_tensor(dst[:, :, k], pv[:, :, k], bias, ALU.add), last)
        return last

    def seq_mod():
        return modulation(A["w_mod"][0], 0, 48, col("b_mod", 0, 48), modc, psum[6])

    XT = BR.get(8, TT)

    def load_xT(dst, src_list):
        st = Ring([Slot(R1.get(1024), lane=f"x{i}") for i in range(3)])
        pr = Ring([PSL[i] for i in range(4)])
        n = 0
        for src, t0 in src_list:
            for i in range(src.shape[0] // 128):
                s, free = st.next()
                tok = load(s.lane, s.ap, src[128 * i:128 * i + 128, :], free)
                rd = []
                for half in range(2):
                    b, bf = pr.next()
                    for k in range(4):
                        last = pe(lambda e, s=s, b=b, k=k, half=half: e.transpose(
                            b.ap[:, 128 * k:128 * k + 128],
                            s.ap[:, 512 * half + 128 * k:512 * half + 128 * k + 128], ident), tok, bf)
                    o = dst[:, 4 * half:4 * half + 4, t0 + 128 * i:t0 + 128 * i + 128]
                    bv = b.ap[:, :].rearrange("p (k t) -> p k t", k=4)
                    if n % 2:
                        ev = dve(lambda e, o=o, bv=bv: e.tensor_copy(o, bv), last)
                    else:
                        ev = act(lambda e, o=o, bv=bv: e.activation(o, bv, ACT.Copy), last)
                    n += 1
                    b.give(ev)
                    rd.append(last)
                s.give(*rd)

    load_xT(XT, [(A["x"][0], 0), (A["ctx"][0], 1024)])
    mod1 = seq_mod()
    P.barrier()
    R1.reset()

    def norm_cols(g, gi, sc_x, sh_x, sc_c=None, sh_c=None):
        gc = col(g, gi, 8)
        dve(lambda e: e.scalar_tensor_tensor(nA[:, 0, :], sc_x, 1.0, gc, ALU.add, ALU.mult))
        dve(lambda e: e.tensor_copy(nB[:, 0, :], sh_x))
        if sc_c is not None:
            dve(lambda e: e.scalar_tensor_tensor(nA[:, 1, :], sc_c, 1.0, gc, ALU.add, ALU.mult))
            dve(lambda e: e.tensor_copy(nB[:, 1, :], sh_c))
        return P.q["dve"][-1]

    def rms(x, dst, blks, tmp, cols, g_only=None):
        sq = Ring([Slot(tmp.get(512)) for _ in range(3)])
        rs = Ring([Slot(tmp.get(512)) for _ in range(2)])
        pr = Ring([PSL[i] for i in range(2)])
        for (t0, n) in blks:
            w = 1 if t0 >= T else 0
            b, bf = pr.next()
            for k in range(8):
                s, sf = sq.next()
                q = act(lambda e, s=s, k=k: e.activation(s.ap[:, 0:n], x[:, k, t0:t0 + n], ACT.Square), sf)
                m = pe(lambda e, s=s, k=k, b=b: e.matmul(b.ap[:, 0:n], ones, s.ap[:, 0:n], start=(k == 0),
                                                        stop=(k == 7)), q, bf)
                s.give(m)
            r, rf = rs.next()
            v = dve(lambda e, r=r, b=b: e.tensor_scalar(r.ap[:, 0:n], b.ap[:, 0:n], 1.0 / D, 1e-6, ALU.mult,
                                                       ALU.add), m, rf)
            b.give(v)
            act(lambda e, r=r: e.activation(r.ap[:, 0:n], r.ap[:, 0:n], ACT.Ln), v)
            rr = act(lambda e, r=r: e.activation(r.ap[:, 0:n], r.ap[:, 0:n], ACT.Exp, scale=-0.5))
            for k in range(8):
                sa = nA[:, w, k:k + 1] if g_only is None else g_only[:, k:k + 1]
                y = dve(lambda e, k=k, r=r, sa=sa: e.scalar_tensor_tensor(
                    dst[:, k, t0:t0 + n], x[:, k, t0:t0 + n], sa, r.ap[:, 0:n], ALU.mult, ALU.mult), rr, cols)
                if g_only is None:
                    y2 = act(lambda e, k=k: e.activation(dst[:, k, t0:t0 + n], dst[:, k, t0:t0 + n], ACT.Identity,
                                                         bias=nB[:, w, k:k + 1]), y)
            r.give(y)

    def m6(i, k=0):
        return modc[:, 8 * i:8 * i + 8, k]

    hT = R1.get(8, TT)
    P.hT = hT
    c1 = norm_cols("norm1_g", 0, m6(1), m6(0), m6(1, 1), m6(0, 1))
    rms(XT, hT, BLKS, CAT, c1)
    P.barrier()
    CAT.reset()
    P.hT_live = True
    h_sp = store("hs", hs, hT)
    x_sp = store("xs", xs, XT)
    P.barrier()
    BR.reset()

    def proj_cm(w, c0, ntile, sink, blks=BLKS, banks=(0, 1, 2, 3), pieces=None):
        pr = proj_cm.rings.setdefault(banks, Ring([PSL[i] for i in banks]))
        hv_ = P.hT
        for j in range(0, ntile, 2):
            nt = min(2, ntile - j)
            s, wv, tok = wload(wcols(w, c0 + 128 * j, 128 * nt), 8, 128 * nt)
            for m in range(nt):
                for (t0, n) in blks:
                    b, bf = pr.next()
                    for k in range(8):
                        last = pe(lambda e, m=m, k=k, b=b, wv=wv, t0=t0, n=n: e.matmul(
                            b.ap[:, 0:n], wv[:, k, 128 * m:128 * m + 128], hv_[:, k, t0:t0 + n],
                            start=(k == 0), stop=(k == 7)), tok, bf)
                    b.give(sink(j + m, t0, n, b.ap, last))
            s.give(last)
    proj_cm.rings = {}

    def proj_tm(w, c0, ncol, sink, tiles, banks=(4, 5, 6, 7)):
        hv_ = P.hT
        pr = Ring([PSL[i] for i in banks])
        for c in range(0, ncol, 256):
            nn = min(256, ncol - c)
            s, wv, tok = wload(wcols(w, c0 + c, nn), 8, nn)
            for t in tiles:
                b, bf = pr.next()
                for k in range(8):
                    last = pe(lambda e, k=k, b=b, wv=wv, t=t, nn=nn: e.matmul(
                        b.ap[:, 0:nn], hv_[:, k, 128 * t:128 * t + 128], wv[:, k, 0:nn],
                        start=(k == 0), stop=(k == 7)), tok, bf)
                b.give(sink(t, c, nn, b.ap, last))
            s.give(last)

    def rows_proj(w, groups, dst, banks=(4, 5)):
        hv_ = P.hT
        s, free = W.next()
        view = s.ap[:, 0:1024].rearrange("p (k n) -> p k n", k=8)
        zz = dve(lambda e: e.memset(view, 0.0), free)
        for q, (c0, n) in groups.items():
            tok = P.dma(s.lane, lambda e, q=q, c0=c0, n=n: e.dma_start(view[:, :, 32 * q:32 * q + n], wcols(w, c0, n)), zz)
        pr = Ring([PSL[i] for i in banks])
        for (t0, n) in BLKS:
            b, bf = pr.next()
            for k in range(8):
                last = pe(lambda e, k=k, b=b, t0=t0, n=n: e.matmul(
                    b.ap[:, 0:n], view[:, k, :], hv_[:, k, t0:t0 + n], start=(k == 0), stop=(k == 7)), tok, bf)
            ev = dve(lambda e, b=b, t0=t0, n=n: e.tensor_copy(dst[:, t0:t0 + n], b.ap[:, 0:n]), last)
            b.give(ev)
        s.give(last)
        return ev

    def softplus(y, t, e1, engine_out=None):
        a = act(lambda e: e.activation(t, y, ACT.Abs), P.q["dve"][-1])
        a = act(lambda e: e.activation(e1, t, ACT.Exp, scale=-1.0), a)
        a = act(lambda e: e.activation(e1, e1, ACT.Ln, bias=1.0))
        return dve(lambda e: e.scalar_tensor_tensor(y, y, 0.0, e1, ALU.max, ALU.add), a)

    def bc(c4, n):
        return c4.unsqueeze(2).to_broadcast([c4.shape[0], c4.shape[1], n])

    def h4(ap, n):
        return ap.rearrange("p (h x) -> p h x", x=n)

    def region(a, b):
        return Arena(big, a, b)

    OFF = {"hy": 0, "gla": 768, "gdn": 768 + 1184}

    def conv_channels(w, c0, ntile, taps, seg, wcol, bcol, zring, outs, fn=None, blks=BLKS, banks=(0, 1, 2, 3)):
        pad = taps // 2
        rows = T // seg
        wl = rows * (seg + 2 * pad)
        state = {}

        def sink(m, t0, n, b, tok):
            if t0 == 0:
                state["z"], state["zf"] = zring.next()
            zs, zf = state["z"], state["zf"]
            if t0 < T:
                zv = zs.ap[:, 0:wl].rearrange("p (r s) -> p r s", s=seg + 2 * pad)
                if seg <= 512:
                    r0 = t0 // seg
                    o = zv[:, r0:r0 + n // seg, pad:pad + seg]
                    src = b[:, 0:n].rearrange("p (r s) -> p r s", s=seg)
                else:
                    o, src = zs.ap[:, pad + t0:pad + t0 + n], b[:, 0:n]
            else:
                o, src = zs.ap[:, wl + pad:wl + pad + n], b[:, 0:n]
            ev = act(lambda e: e.activation(o, src, ACT.Copy), tok, zf)
            if t0 == blks[-1][0]:
                zlat = zs.ap[:, 0:wl].rearrange("p (r s) -> p r s", s=seg + 2 * pad)
                c_on = len(blks) == 3
                zctx = zs.ap[:, wl:wl + 2 * pad + TC] if c_on else None
                dst, waits, fin = outs(m)
                last = dve(lambda e: e.tensor_scalar(
                    dst[:, 0:T].rearrange("p (r s) -> p r s", s=seg), zlat[:, :, 0:seg], wcol(m, 0),
                    0.0 if bcol is None else bcol(m), ALU.mult, ALU.add), ev, waits)
                if c_on:
                    dve(lambda e: e.tensor_scalar(dst[:, T:TT], zctx[:, 0:TC], wcol(m, 0),
                                                  0.0 if bcol is None else bcol(m), ALU.mult, ALU.add))
                for tap in range(1, taps):
                    last = dve(lambda e, tap=tap: e.scalar_tensor_tensor(
                        dst[:, 0:T].rearrange("p (r s) -> p r s", s=seg), zlat[:, :, tap:tap + seg],
                        wcol(m, tap), dst[:, 0:T].rearrange("p (r s) -> p r s", s=seg), ALU.mult, ALU.add))
                    if c_on:
                        last = dve(lambda e, tap=tap: e.scalar_tensor_tensor(
                            dst[:, T:TT], zctx[:, tap:tap + TC], wcol(m, tap), dst[:, T:TT], ALU.mult, ALU.add))
                zs.give(last)
                if fn is not None:
                    nn = TT if c_on else T
                    last = act(lambda e: e.activation(dst[:, 0:nn], dst[:, 0:nn], fn), last)
                fin(m, last)
            return ev

        proj_cm(w, c0, ntile, sink, blks=blks, banks=banks)

    def tr4(pieces, dst, pr, after, parts=128, eng="act"):
        b, bf = pr.next()
        for i, p in enumerate(pieces):
            k = p.shape[0]
            m = p.shape[1]
            last = pe(lambda e, i=i, p=p, k=k, m=m: e.transpose(b.ap[0:m, 128 * i:128 * i + k], p, ident[0:k, 0:k]),
                      after, bf)
        return b, last

    def gdn():
        w = A["w_in"][0]
        c0 = OFF["gdn"]
        cat = CAT.t[:, M0 + 5 * T:M0 + 8 * T].rearrange("p (m t) -> p m t", m=3)
        C1 = region(M0, M0 + 8192)
        B1 = region(M0 + 8192, total - 10240)
        hreg = (total - 10240, total)
        gate, G = C1.get(8, 384), C1.get(TT)
        qT, kT = B1.get(4, TT, parts=96), B1.get(4, TT, parts=96)
        ktm, vtm = B1.get(10, 384), B1.get(10, 384)
        CX = region(CON.at, CON.hi)
        colg, ngc, kdE, egc = CX.get(10, 16), CX.get(10, 8), CX.get(10, 8), CX.get(10, 8)
        GL, eGL, par, ss = CX.get(8, 10), CX.get(8, 10), CX.get(4), CX.get(10, 4)
        s1 = B1.t[:, M0 + 8192:M0 + 8192 + TT]
        e1 = B1.t[:, M0 + 8192 + TT:M0 + 8192 + 2 * TT]
        rows_proj(w, {0: (c0 + 1536, 4), 1: (c0 + 1540, 4), 2: (c0 + 1544, 4), 3: (c0 + 1548, 4)}, G)
        z0 = dve(lambda e: e.memset(par, 0.0))
        for d in range(2):
            load("gpar", par[32 * d:32 * d + 4, 0:1], A["gdn_dt_bias"][0, d].rearrange("(a b) -> a b", b=1), z0)
            pl = load("gpar", par[32 * d:32 * d + 4, 1:2], A["gdn_a_log"][0, d].rearrange("(a b) -> a b", b=1), z0)
        ea = act(lambda e: e.activation(par[:, 2:3], par[:, 1:2], ACT.Exp), pl)
        dve(lambda e: e.tensor_scalar(G, G, par[:, 0:1], sgn, ALU.add, ALU.mult), pl)
        softplus(G, s1, e1)
        dve(lambda e: e.tensor_scalar(G[0:64, :], G[0:64, :], par[0:64, 2:3], -1.0, ALU.mult, ALU.mult), ea)
        beta = act(lambda e: e.activation(G[64:128, :], G[64:128, :], ACT.Exp, scale=-1.0), P.q["dve"][-1])
        for d in range(2):
            src, ms, o = G[32 * d:32 * d + 32, :], rst[32 * d:32 * d + 32, d, :], s1[32 * d:32 * d + 32, :]
            if d:
                src, ms, o = src[:, ::-1], ms[:, ::-1], o[:, ::-1]
            dve(lambda e, src=src, ms=ms, o=o: e.tensor_tensor_scan(o, ms, src, 0.0, ALU.mult, ALU.add))
        gcr = dve(lambda e: e.tensor_copy(G[0:64, :], s1[0:64, :]), beta)
        ev = [None, None]
        for c in range(10):
            b = psum[c % 2]
            t = pe(lambda e, c=c, b=b: e.transpose(b[:, 0:128], G[:, 128 * c:128 * c + 128], ident), gcr, ev[c % 2])
            src = b[:, 0:128].rearrange("p (q r) -> p q r", q=4)[:, :, 0:4]
            ev[c % 2] = dve(lambda e, c=c, src=src: e.tensor_copy(
                colg[:, c, :].rearrange("p (q r) -> p q r", q=4), src), t)
        for d in range(2):
            for h in range(4):
                ends = G[:, (127 if d == 0 else 0):TT:128]
                t = pe(lambda e, d=d, h=h, ends=ends: e.matmul(
                    psum[2][:, (4 * d + h) * 16:(4 * d + h) * 16 + 10], sel[:, 4 * d + h, :], ends, start=True,
                    stop=True), gcr)
        dve(lambda e: e.tensor_copy(GL, psum[2][:, 0:128].rearrange("p (a b) -> p a b", a=8)[:, :, 0:10]), t)
        gc8 = colg[:, :, 0:8]
        dve(lambda e: e.tensor_scalar(ngc, gc8, -1.0, None, ALU.mult))
        a0 = dve(lambda e: e.tensor_tensor(kdE, ngc, GL.rearrange("p a b -> p b a"), ALU.add))
        act(lambda e: e.activation(kdE, kdE, ACT.Exp), a0)
        act(lambda e: e.activation(egc, gc8, ACT.Exp))
        act(lambda e: e.activation(eGL, GL, ACT.Exp))
        P.barrier()

        zw = 16 * 70 + 262
        zr = Ring([Slot(C1.get(zw)) for _ in range(2)])
        for s in zr.slots:
            zt = dve(lambda e, s=s: e.memset(s.ap, 0.0))
            s.free = [zt]
        cr = Ring([Slot(B1.get(TT))])
        pr = Ring([PSL[i] for i in (4, 5, 6, 7)])
        gw, gr = offs["gdn_conv_w"]

        def branch(base, dsttm):
            def outs(m):
                s, f = cr.next()

                def fin(m, tok):
                    ts = []
                    for t0 in (0, 4, 8):
                        k = min(4, 10 - t0)
                        b, last = tr4([s.ap[:, 128 * (t0 + i):128 * (t0 + i) + 128] for i in range(k)], None, pr, tok)
                        o = dsttm[:, t0:t0 + k, 128 * m:128 * m + 128]
                        ev = dve(lambda e, o=o, b=b, k=k: e.tensor_copy(
                            o, b.ap[:, 0:128 * k].rearrange("p (t c) -> p t c", t=k)), last)
                        b.give(ev)
                    s.give(last)
                return s.ap, f, fin

            conv_channels(w, c0 + 128 * base, 3, 7, 64, lambda m, tap: vec[gw][:, gr + tap * 9 + base + m:
                          gr + tap * 9 + base + m + 1], None, zr, outs, fn=ACT.Silu)

        def normalize(tm, dstT, scale):
            for t in range(10):
                dve(lambda e, t=t: e.tensor_tensor(nt, tm[:, t, :], tm[:, t, :], ALU.mult))
                dve(lambda e, t=t: e.tensor_reduce(ss[:, t, :], h4(nt, 96), AXX, ALU.add))
            a = dve(lambda e: e.tensor_scalar(ss, ss, 1e-6, None, ALU.add))
            act(lambda e: e.activation(ss, ss, ACT.Ln), a)
            a = act(lambda e: e.activation(ss, ss, ACT.Exp, scale=-0.5))
            if scale != 1.0:
                a = dve(lambda e: e.tensor_scalar(ss, ss, scale, None, ALU.mult), a)
            for t in range(10):
                n = dve(lambda e, t=t: e.tensor_tensor(h4(tm[:, t, :], 96), h4(tm[:, t, :], 96),
                                                       bc(ss[:, t, :], 96), ALU.mult), a)
                b, last = tr4([tm[:, t, 96 * h:96 * h + 96] for h in range(4)], None, pr, n)
                ev = act(lambda e, t=t, b=b: e.activation(
                    dstT[:, :, 128 * t:128 * t + 128], b.ap[0:96, :].rearrange("p (h t) -> p h t", h=4), ACT.Copy),
                    last)
                b.give(ev)
            return ev

        nt = C1.get(384)
        branch(0, vtm)
        P.barrier()
        normalize(vtm, qT, 96 ** -0.5)
        P.barrier()
        branch(3, ktm)
        P.barrier()
        normalize(ktm, kT, 1.0)
        branch(6, vtm)

        def gsink(t, c, n, b, tok):
            return act(lambda e: e.activation(gate[:, t, c:c + n], b[:, 0:n], ACT.Silu), tok)

        proj_tm(w, c0 + 1152, 384, gsink, range(8), banks=(0, 1, 2, 3))
        P.hT_live = False
        P.barrier()

        H1 = region(*hreg)
        C2 = region(C1.at - 384, M0 + 8192)
        C2.at = C2.lo = M0 + 3072 + TT
        lv = H1.get(2, 7, 128)
        lvt = load("gpar2", lv, A["c_lv"].rearrange("p (a b c) -> p a b c", a=2, b=7))
        oacc = H1.get(8, 384)
        odone = {}

        def scan(d, ar):
            DT, LT, C = ar.get(512), ar.get(512), ar.get(512)
            X, XT_, M1 = ar.get(512), ar.get(512), ar.get(512)
            qe = C2.get(512)[0:96, :]
            vn, S = C2.get(384), C2.get(384)[0:96, :]
            banks = [PSL[4 * d + i] for i in range(4)]
            pr = Ring(banks)
            st = dve(lambda e: e.memset(S, 0.0))
            order = [8, 9] + list(range(8)) if d == 0 else [9, 8] + list(range(7, -1, -1))
            pstate = [st]
            for c in order:
                lat = c < 8
                ts = slice(128 * c, 128 * c + 128)
                b, bf = pr.next()
                for h in range(4):
                    t = pe(lambda e, h=h, b=b: e.matmul(b.ap[:, 128 * h:128 * h + 128], sel[:, 4 * d + h, :], G[:, ts],
                                                       start=True, stop=True), bf)
                kb, kf = pr.next()
                for h in range(4):
                    tk = pe(lambda e, h=h, kb=kb: e.matmul(kb.ap[:, 128 * h:128 * h + 128], kT[:, h, ts], kT[:, h, ts],
                                                          start=True, stop=True), kf)
                yield
                for h in range(4):
                    last = dve(lambda e, h=h, b=b: e.scalar_tensor_tensor(
                        DT[:, 128 * h:128 * h + 128], b.ap[:, 128 * h:128 * h + 128],
                        ngc[:, c, 4 * d + h:4 * d + h + 1], mt[:, d, :], ALU.add, ALU.min), t)
                a1 = act(lambda e: e.activation(DT, DT, ACT.Exp), last)
                rel = [last]
                if lat:
                    a2 = act(lambda e, b=b: e.activation(qe, b.ap[0:96, :], ACT.Exp))
                    qed = pool(lambda e: e.tensor_tensor(h4(qe, 128), h4(qe, 128), qT[:, :, ts], ALU.mult), a2)
                    rel.append(a2)
                b.give(*rel)
                yield
                for h in range(4):
                    last = dve(lambda e, h=h, kb=kb: e.scalar_tensor_tensor(
                        LT[:, 128 * h:128 * h + 128], kb.ap[:, 128 * h:128 * h + 128],
                        colg[:, c, 8 + 4 * d + h:8 + 4 * d + h + 1], DT[:, 128 * h:128 * h + 128], ALU.mult,
                        ALU.mult), tk, a1)
                kb.give(last)
                for n in range(7):
                    cm = pool(lambda e, n=n: e.tensor_tensor(
                        h4(C, 128), h4(LT, 128), lv[:, d, n, :].unsqueeze(1).to_broadcast([128, 4, 128]), ALU.mult),
                        last, lvt, P.q["pe"][-1] if n else None)
                    b, bf = pr.next()
                    for h in range(4):
                        sl = slice(128 * h, 128 * h + 128)
                        rhs = ident if n == 0 else X[:, sl]
                        t = pe(lambda e, b=b, sl=sl, rhs=rhs: e.matmul(b.ap[:, sl], C[:, sl], rhs, start=True,
                                                                       stop=True), cm, bf, last)
                    idb = ident.unsqueeze(1).to_broadcast([128, 4, 128])
                    if n == 0:
                        x1 = dve(lambda e, b=b: e.tensor_tensor(h4(X, 128), idb, h4(b.ap[:, :], 128), ALU.subtract), t)
                        last = dve(lambda e: e.tensor_tensor(h4(XT_, 128), idb, h4(C, 128), ALU.subtract))
                        b.give(x1)
                        yield
                        continue
                    m1 = act(lambda e, b=b: e.activation(M1, b.ap[:, :], ACT.Copy), t)
                    b.give(m1)
                    yield
                    b2, bf2 = pr.next()
                    for h in range(4):
                        sl = slice(128 * h, 128 * h + 128)
                        t2 = pe(lambda e, b2=b2, sl=sl: e.matmul(b2.ap[:, sl], M1[:, sl], XT_[:, sl], start=True,
                                                                 stop=True), m1, bf2)
                    if n < 6:
                        b3, bf3 = pr.next()
                        for h in range(4):
                            sl = slice(128 * h, 128 * h + 128)
                            t3 = pe(lambda e, b3=b3, sl=sl: e.matmul(b3.ap[:, sl], XT_[:, sl], M1[:, sl], start=True,
                                                                     stop=True), bf3)
                        x1 = dve(lambda e, b3=b3: e.tensor_tensor(X, X, b3.ap[:, :], ALU.subtract), t3)
                        b3.give(x1)
                    last = dve(lambda e, b2=b2: e.tensor_tensor(XT_, XT_, b2.ap[:, :], ALU.subtract), t2,
                               P.q["pe"][-1])
                    b2.give(last)
                    yield
                ke, nw = M1[:, 0:384], LT[0:96, :]
                k1 = dve(lambda e: e.tensor_tensor(h4(ke, 96), h4(ktm[:, c, :], 96),
                                                   bc(egc[:, c, 4 * d:4 * d + 4], 96), ALU.mult))
                b, bf = pr.next()
                for h in range(4):
                    t = pe(lambda e, b=b, h=h: e.matmul(b.ap[0:96, 128 * h:128 * h + 128], ke[:, 96 * h:96 * h + 96],
                                                       XT_[:, 128 * h:128 * h + 128], start=True, stop=True),
                           k1, last, bf)
                n1 = act(lambda e, b=b: e.activation(nw, b.ap[0:96, :], ACT.Copy, scale=-1.0), t)
                b.give(n1)
                if lat:
                    qb, qf = pr.next()
                    for h in range(4):
                        tq = pe(lambda e, qb=qb, h=h: e.matmul(qb.ap[:, 128 * h:128 * h + 128], kT[:, h, ts],
                                                              qT[:, h, ts], start=True, stop=True), qf)
                    at = dve(lambda e, qb=qb: e.tensor_tensor(C, qb.ap[:, :], DT, ALU.mult), tq)
                    qb.give(at)
                kd = X[:, 0:384]
                kdt = dve(lambda e: e.tensor_tensor(h4(kd, 96), h4(ktm[:, c, :], 96),
                                                    bc(kdE[:, c, 4 * d:4 * d + 4], 96), ALU.mult))
                yield
                b, bf = pr.next()
                for h in range(4):
                    pe(lambda e, b=b, h=h: e.matmul(b.ap[:, 96 * h:96 * h + 96], XT_[:, 128 * h:128 * h + 128],
                                                    vtm[:, c, 96 * h:96 * h + 96], start=True, stop=False), bf)
                    t = pe(lambda e, b=b, h=h: e.matmul(b.ap[:, 96 * h:96 * h + 96], nw[:, 128 * h:128 * h + 128],
                                                       S[:, 96 * h:96 * h + 96], start=False, stop=True),
                           n1, pstate[0])
                v1 = dve(lambda e, b=b: e.tensor_tensor(h4(vn, 96), h4(b.ap[:, 0:384], 96),
                                                        bc(colg[:, c, 8 + 4 * d:12 + 4 * d], 96), ALU.mult), t)
                b.give(v1)
                yield
                b, bf = pr.next()
                for h in range(4):
                    ts_ = pe(lambda e, b=b, h=h: e.matmul(b.ap[0:96, 96 * h:96 * h + 96], kd[:, 96 * h:96 * h + 96],
                                                         vn[:, 96 * h:96 * h + 96], start=True, stop=True), v1, kdt,
                             bf)
                if lat:
                    ob, of = pr.next()
                    for h in range(4):
                        pe(lambda e, ob=ob, h=h: e.matmul(ob.ap[:, 96 * h:96 * h + 96], C[:, 128 * h:128 * h + 128],
                                                          vn[:, 96 * h:96 * h + 96], start=True, stop=False), at, of)
                        to = pe(lambda e, ob=ob, h=h: e.matmul(
                            ob.ap[:, 96 * h:96 * h + 96], qe[:, 128 * h:128 * h + 128], S[:, 96 * h:96 * h + 96],
                            start=False, stop=True), qed)
                    if c not in odone:
                        o1 = act(lambda e, ob=ob: e.activation(oacc[:, c, :], ob.ap[:, 0:384], ACT.Copy), to)
                        odone[c] = o1
                    else:
                        o1 = dve(lambda e, ob=ob: e.tensor_tensor(oacc[:, c, :], oacc[:, c, :], ob.ap[:, 0:384],
                                                                  ALU.add), to, odone[c])
                    ob.give(o1)
                dve(lambda e: e.tensor_tensor(h4(S, 96), h4(S, 96), bc(eGL[0:96, 4 * d:4 * d + 4, c], 96), ALU.mult),
                    P.q["pe"][-1])
                s1_ = dve(lambda e, b=b: e.tensor_tensor(S, S, b.ap[0:96, 0:384], ALU.add), ts_)
                b.give(s1_)
                pstate[0] = s1_
                yield

        interleave([scan(0, ScanAr([H1, B1, C2])), scan(1, ScanAr([H1, B1, C2]))])
        P.barrier()
        head_out(oacc, gate, "gdn_norm_g", 4, 96, cat, region(H1.lo + 1792 + 3072, H1.hi), CX)

    class ScanAr:
        def __init__(self, ars):
            self.ars = ars

        def get(self, n):
            for a in self.ars:
                if a.at + n <= a.hi:
                    return a.get(n)
            raise AssertionError("no room")

    def head_out(oacc, gate, gname, nh, dv, cat, ar, CX):
        nn = nh * dv
        gb = ar.get(dv)
        gl = load("gb", gb, A[gname][0].partition_broadcast(128))
        sq = ar.get(nn)
        s8 = CX.get(8, nh)
        for t in range(8):
            dve(lambda e, t=t: e.tensor_tensor(sq, oacc[:, t, :], oacc[:, t, :], ALU.mult))
            dve(lambda e, t=t: e.tensor_reduce(s8[:, t, :], h4(sq, dv), AXX, ALU.add))
        a = dve(lambda e: e.tensor_scalar(s8, s8, 1.0 / dv, 1e-6, ALU.mult, ALU.add))
        act(lambda e: e.activation(s8, s8, ACT.Ln), a)
        a = act(lambda e: e.activation(s8, s8, ACT.Exp, scale=-0.5))
        pr = Ring([PSL[i] for i in range(4)])
        for t in range(8):
            dve(lambda e, t=t: e.tensor_tensor(h4(oacc[:, t, :], dv), h4(oacc[:, t, :], dv), bc(s8[:, t, :], dv),
                                               ALU.mult), a)
            dve(lambda e, t=t: e.tensor_tensor(h4(oacc[:, t, :], dv), h4(oacc[:, t, :], dv),
                                               gb.unsqueeze(1).to_broadcast([128, nh, dv]), ALU.mult), gl)
            n = dve(lambda e, t=t: e.tensor_tensor(oacc[:, t, :], oacc[:, t, :], gate[:, t, :], ALU.mult))
            b, last = tr4([oacc[:, t, 128 * i:128 * i + 128] for i in range(nn // 128)], None, pr, n)
            ev = act(lambda e, t=t, b=b: e.activation(
                cat[:, :, 128 * t:128 * t + 128], b.ap[:, 0:nn].rearrange("p (m t) -> p m t", t=128), ACT.Copy), last)
            b.give(ev)
        P.barrier()

    def gla():
        w = A["w_in"][0]
        c0 = OFF["gla"]
        cat = CAT.t[:, M0 + 2 * T:M0 + 5 * T].rearrange("p (m t) -> p m t", m=3)
        C1 = region(M0, M0 + 5 * T)
        B1 = region(M0 + 8192, total - 10240)
        H1 = region(total - 10240, total)
        CX = region(CON.at, CON.hi)
        gate = B1.get(8, 384)
        qT, kT = B1.get(4, TT, parts=48), B1.get(4, TT, parts=48)
        vtm = B1.get(10, 384)
        aT = [B1.get(TT, parts=16), B1.get(TT, parts=16)]
        wa = C1.get(2, 192, parts=16)
        nba = CX.get(2, 4)[0:48, :, :]
        pl = load("gl1", wa, A["gla_w_a2"][0].rearrange("d r n -> r d n"))
        for d in range(2):
            for h in range(4):
                pl = load("gl1", nba[:, d, h:h + 1],
                          A["gla_b_a"][0, d, 48 * h:48 * h + 48].rearrange("(a b) -> a b", b=1))
        hx = None if P.hT_live else load("hsl", hT, hs)
        P.hT_live = True
        P.fence["pe"] = P.fence["pe"] + ([hx] if hx else [])
        pr = Ring([PSL[i] for i in range(4)])

        def headed(c, m, nh, dst):
            hv_ = P.hT
            s, wv, tok = wload(wcols(w, c, m * nh), 8, m * nh)
            for g in range(nh):
                for (t0, n) in BLKS:
                    b, bf = pr.next()
                    for k in range(8):
                        last = pe(lambda e, g=g, k=k: e.matmul(b.ap[0:m, 0:n], wv[:, k, m * g:m * g + m],
                                                               hv_[:, k, t0:t0 + n], start=(k == 0), stop=(k == 7)),
                                  tok, bf)
                    o = dst(g, t0, n)
                    ev = act(lambda e: e.activation(o, b.ap[0:m, 0:n], ACT.Copy), last)
                    b.give(ev)
            s.give(last)

        headed(c0, 48, 4, lambda g, t0, n: qT[:, g, t0:t0 + n])
        headed(c0 + 192, 48, 4, lambda g, t0, n: kT[:, g, t0:t0 + n])
        headed(c0 + 1152, 16, 2, lambda g, t0, n: aT[g][:, t0:t0 + n])

        def vsink(t, c, n, b, tok):
            return dve(lambda e: e.tensor_copy(vtm[:, t, c:c + n], b[:, 0:n]), tok)

        proj_tm(w, c0 + 384, 384, vsink, range(10))

        def gsink(t, c, n, b, tok):
            return act(lambda e: e.activation(gate[:, t, c:c + n], b[:, 0:n], ACT.Silu), tok)

        proj_tm(w, c0 + 768, 384, gsink, range(8))
        P.barrier()
        P.hT_live = False
        oacc = H1.get(8, 384)
        pm = H1.get(2, 512)
        H1.get(768)
        pmt = load("gl2", pm, A["c_pm"].bitcast(F32).rearrange("p (d x) -> p d x", d=2))
        odone = {}
        rem = ScanAr([H1, B1, C1])

        def scan(d):
            g48 = lambda: rem.get(512)[0:48, :]
            la, bb, e1, e2, qs, kd = g48(), g48(), g48(), g48(), g48(), g48()
            qd, kk = g48(), g48()
            At = rem.get(512)
            kdt, S = CX.get(192), CXS(CX, d)[0:48, :]
            pr = Ring([PSL[4 * d + i] for i in range(4)])
            dve(lambda e: e.memset(At, 0.0))
            st = dve(lambda e: e.memset(S, 0.0))
            order = [8, 9] + list(range(8)) if d == 0 else [9, 8] + list(range(7, -1, -1))
            fin_pe = None
            for c in order:
                lat = c < 8
                ts = slice(128 * c, 128 * c + 128)
                b, bf = pr.next()
                for h in range(4):
                    t = pe(lambda e, h=h: e.matmul(b.ap[0:48, 128 * h:128 * h + 128], wa[:, d, 48 * h:48 * h + 48],
                                                  aT[d][:, ts], start=True, stop=True), bf, pl)
                y = dve(lambda e: e.tensor_tensor(h4(la, 128), h4(b.ap[0:48, :], 128),
                                                  bc(nba[:, d, :], 128), ALU.add), t, pl)
                b.give(y)
                yield
                a1 = act(lambda e: e.activation(e1, la, ACT.Abs), y)
                act(lambda e: e.activation(e1, e1, ACT.Exp, scale=-1.0))
                a1 = act(lambda e: e.activation(e1, e1, ACT.Ln, bias=1.0))
                yield
                dve(lambda e: e.scalar_tensor_tensor(la, la, 0.0, e1, ALU.min, ALU.subtract), a1)
                dve(lambda e: e.tensor_scalar(la, la, 1.0 / 16.0, None, ALU.mult))
                ms = rst[0:48, d, 0:512]
                if d == 0:
                    dve(lambda e: e.tensor_tensor_scan(bb, ms, la, 0.0, ALU.mult, ALU.add))
                else:
                    dve(lambda e: e.tensor_tensor_scan(bb[:, ::-1], ms[:, ::-1], la[:, ::-1], 0.0, ALU.mult, ALU.add))
                b4 = h4(bb, 128)
                end = 127 if d == 0 else 0
                f1 = dve(lambda e: e.tensor_tensor(h4(e2, 128), b4[:, :, end:end + 1].to_broadcast([48, 4, 128]), b4,
                                                  ALU.subtract), fin_pe)
                a2 = act(lambda e: e.activation(e2, e2, ACT.Exp), f1)
                eL = act(lambda e: e.activation(e1[:, 0:4], b4[:, :, end], ACT.Exp))
                kdd = pool(lambda e: e.tensor_tensor(h4(kd, 128), h4(e2, 128), kT[:, :, ts], ALU.mult), a2,
                           fin_pe)
                yield
                kb, kf = pr.next()
                for h in range(4):
                    tk = pe(lambda e, h=h: e.transpose(kb.ap[:, 48 * h:48 * h + 48], kd[:, 128 * h:128 * h + 128],
                                                      ident[0:48, 0:48]), kdd, kf)
                kt1 = act(lambda e: e.activation(kdt, kb.ap[:, 0:192], ACT.Copy), tk)
                kb.give(kt1)
                sb_, sf = pr.next()
                for h in range(4):
                    tsn = pe(lambda e, h=h: e.matmul(sb_.ap[0:48, 96 * h:96 * h + 96], kdt[:, 48 * h:48 * h + 48],
                                                     vtm[:, c, 96 * h:96 * h + 96], start=True, stop=True), kt1, sf)
                if lat:
                    a3 = act(lambda e: e.activation(qs, bb, ACT.Exp))
                    q1 = pool(lambda e: e.tensor_tensor(h4(qs, 128), h4(qs, 128), qT[:, :, ts], ALU.mult), a3)
                    b5 = bb.rearrange("p (h f x) -> p (h f) x", h=4, f=2)
                    mid = b5[:, :, 31:32].to_broadcast([48, 8, 64])
                    dve(lambda e: e.tensor_tensor(qd.rearrange("p (g x) -> p g x", g=8), b5, mid, ALU.subtract),
                        fin_pe)
                    f2 = dve(lambda e: e.tensor_scalar(qd, qd, 80.0, -80.0, ALU.min, ALU.max))
                    act(lambda e: e.activation(kk, qd, ACT.Exp, scale=-1.0), f2)
                    a4 = act(lambda e: e.activation(qd, qd, ACT.Exp))
                    pool(lambda e: e.tensor_tensor(h4(kk, 128), h4(kk, 128), kT[:, :, ts], ALU.mult), a4)
                    q2 = pool(lambda e: e.tensor_tensor(h4(qd, 128), h4(qd, 128), qT[:, :, ts], ALU.mult), a4)
                    yield
                    ab, af = pr.next()
                    for h in range(4):
                        t1 = pe(lambda e, h=h: e.matmul(ab.ap[:, 128 * h:128 * h + 128], kk[:, 128 * h:128 * h + 128],
                                                       qd[:, 128 * h:128 * h + 128], start=True, stop=True), q2, af)
                    r = 63 if d == 0 else 64
                    qh = slice(64, 128) if d == 0 else slice(0, 64)
                    kh = slice(0, 64) if d == 0 else slice(64, 128)
                    ref = b4[:, :, r:r + 1].to_broadcast([48, 4, 64])
                    q4, k4 = h4(qd, 128), h4(kk, 128)
                    dve(lambda e: e.tensor_tensor(q4[:, :, qh], b4[:, :, qh], ref, ALU.subtract), t1)
                    f3 = dve(lambda e: e.tensor_tensor(k4[:, :, kh], ref, b4[:, :, kh], ALU.subtract))
                    act(lambda e: e.activation(q4[:, :, qh], q4[:, :, qh], ACT.Exp), f3)
                    a5 = act(lambda e: e.activation(k4[:, :, kh], k4[:, :, kh], ACT.Exp))
                    pool(lambda e: e.tensor_tensor(q4[:, :, qh], q4[:, :, qh],
                                                   qT[:, :, 128 * c + qh.start:128 * c + qh.stop], ALU.mult), a5)
                    q3 = pool(lambda e: e.tensor_tensor(k4[:, :, kh], k4[:, :, kh],
                                                        kT[:, :, 128 * c + kh.start:128 * c + kh.stop], ALU.mult))
                    yield
                    for h in range(4):
                        o = ab.ap[kh, 128 * h + qh.start:128 * h + qh.stop]
                        t2 = pe(lambda e, h=h, o=o: e.matmul(o, k4[:, h, kh], q4[:, h, qh], start=True, stop=True),
                                q3)
                    pmi = pm[:, d, :].bitcast(I32)
                    cp = dve(lambda e: e.copy_predicated(At, pmi, ab.ap[:, :]), t2, pmt, fin_pe)
                    ab.give(cp)
                    ob, of = pr.next()
                    for h in range(4):
                        pe(lambda e, h=h: e.matmul(ob.ap[:, 96 * h:96 * h + 96], At[:, 128 * h:128 * h + 128],
                                                   vtm[:, c, 96 * h:96 * h + 96], start=True, stop=False), cp, of)
                        to = pe(lambda e, h=h: e.matmul(ob.ap[:, 96 * h:96 * h + 96], qs[:, 128 * h:128 * h + 128],
                                                       S[:, 96 * h:96 * h + 96], start=False, stop=True), q1, st)
                    if c not in odone:
                        o1 = act(lambda e: e.activation(oacc[:, c, :], ob.ap[:, 0:384], ACT.Copy,
                                                        scale=48 ** -0.5), to)
                        odone[c] = o1
                    else:
                        o1 = dve(lambda e: e.scalar_tensor_tensor(oacc[:, c, :], ob.ap[:, 0:384], 48 ** -0.5,
                                                                  oacc[:, c, :], ALU.mult, ALU.add), to, odone[c])
                    ob.give(o1)
                fin_pe = P.q["pe"][-1]
                dve(lambda e: e.tensor_tensor(h4(S, 96), h4(S, 96), bc(e1[:, 0:4], 96), ALU.mult), fin_pe, eL)
                st = dve(lambda e: e.tensor_tensor(S, S, sb_.ap[0:48, 0:384], ALU.add), tsn)
                sb_.give(st)
                yield

        interleave([scan(0), scan(1)])
        P.barrier()
        head_out(oacc, gate, "gla_norm_g", 4, 96, cat, region(H1.lo + 3072, H1.hi), CX)

    def CXS(CX, d):
        return big[:, total - 10240 + 3072 + 1024 + 384 * d:total - 10240 + 3072 + 1024 + 384 * (d + 1)]

    def hyena():
        w = A["w_in"][0]
        cat = CAT.t[:, M0:M0 + 2 * T].rearrange("p (m t) -> p m t", m=2)
        B1 = region(M0 + 8192, total - 10240)
        H1 = region(total - 10240, total)
        hx = None if P.hT_live else load("hsl", hT, hs)
        P.hT_live = True
        P.fence["pe"] = P.fence["pe"] + ([hx] if hx else [])
        u = B1.get(8, 768)
        mark = B1.at
        zr = Ring([Slot(B1.get(16 * 66)) for _ in range(2)])
        for s in zr.slots:
            s.free = [dve(lambda e, s=s: e.memset(s.ap, 0.0))]
        cr = Ring([Slot(B1.get(T)) for _ in range(2)])
        pr = Ring([PSL[i] for i in (4, 5, 6, 7)])
        hw, hr = offs["hy_conv_w"]

        def outs(m):
            s, f = cr.next()

            def fin(m, tok):
                sv = s.ap.rearrange("p (t two) -> p two t", two=2)
                for par in range(2):
                    b, last = tr4([sv[:, par, 128 * i:128 * i + 128] for i in range(4)], None, pr, tok)
                    ev = act(lambda e, b=b, par=par: e.activation(
                        u[:, 4 * par:4 * par + 4, 128 * m:128 * m + 128],
                        b.ap[:, :].rearrange("p (t c) -> p t c", t=4), ACT.Copy), last)
                    b.give(ev)
                s.give(last)
            return s.ap, f, fin

        conv_channels(w, 0, 6, 3, 64, lambda m, tap: vec[hw][:, hr + tap * 6 + m:hr + tap * 6 + m + 1],
                      lambda m: col("hy_conv_b", m, 1), zr, outs, fn=None, blks=BLKS[0:2])
        P.barrier()
        P.hT_live = False
        B1.at = mark
        CX = region(CON.at, CON.hi)
        hm = H1.at
        zc = H1.get(T)[0:33, :]
        fw1, fw2 = H1.get(64)[0:33, :], H1.get(64)[0:64, :]
        fw3 = H1.get(1024)[0:64, :]
        h1, rr, kf = H1.get(T)[0:64, :], H1.get(T)[0:64, :], H1.get(T)[0:64, :]
        fp = CX.get(8)[0:64, :]
        for dst, src in ((zc, A["c_z"]), (fw1, A["hy_f_w1"][0]), (fw2, A["hy_f_w2"][0]), (fw3, A["hy_f_w3"][0]),
                         (fp[:, 0:1], A["hy_f_b1"][0].rearrange("(a b) -> a b", b=1)),
                         (fp[:, 1:2], A["hy_f_b2"][0].rearrange("(a b) -> a b", b=1)),
                         (fp[:, 2:3], A["hy_sin_freq"][0, 0].rearrange("(a b) -> a b", b=1)),
                         (fp[:, 3:4], A["hy_sin_freq"][0, 1].rearrange("(a b) -> a b", b=1))):
            ld = load("hyl", dst, src)
        MAGIC = 12582912.0
        C1_, C2_ = 6.28125, 2 * math.pi - 6.28125
        prev = ld
        for n, (wt, inp) in enumerate(((fw1, zc), (fw2, h1))):
            evs = []
            for i in range(2):
                t = pe(lambda e, i=i: e.matmul(psum[i][0:64, :], wt, inp[:, 512 * i:512 * i + 512], start=True,
                                               stop=True), prev, ld)
                evs.append(dve(lambda e, i=i: e.tensor_scalar(rr[:, 512 * i:512 * i + 512], psum[i][0:64, :],
                                                             fp[:, n:n + 1], fp[:, 2 + n:3 + n], ALU.add, ALU.mult),
                               t))
            dve(lambda e: e.tensor_scalar(kf, rr, 1.0 / (2 * math.pi), MAGIC, ALU.mult, ALU.add))
            dve(lambda e: e.tensor_scalar(kf, kf, MAGIC, None, ALU.subtract))
            dve(lambda e: e.scalar_tensor_tensor(rr, kf, -C1_, rr, ALU.mult, ALU.add))
            dve(lambda e: e.scalar_tensor_tensor(rr, kf, -C2_, rr, ALU.mult, ALU.add))
            a = dve(lambda e: e.tensor_scalar(rr, rr, 3.1415925, -3.1415925, ALU.min, ALU.max))
            prev = act(lambda e: e.activation(h1, rr, ACT.Sin), a)
        dec = Ring([Slot(H1.get(256), lane=f"dec{i}") for i in range(2)])
        R2 = H1.at
        fr = Ring([Slot(B1.get(1024)) for _ in range(2)])
        hsm = B1.get(8, 512)
        hdf_ = B1.get(8, 512)
        pr = Ring([PSL[i] for i in range(2, 8)])
        hv = h1.rearrange("p (t two) -> p two t", two=2)
        for tt_ in range(8):
            par, i = tt_ // 4, tt_ % 4
            s, sf = dec.next()
            dl = load(s.lane, s.ap, A["c_dec"][128 * tt_:128 * tt_ + 128, :], sf)
            f, ff = fr.next()
            for half in range(2):
                b, bf = pr.next()
                t = pe(lambda e, half=half: e.matmul(b.ap[:, :], hv[:, par, 128 * i:128 * i + 128],
                                                     fw3[:, 512 * half:512 * half + 512], start=True, stop=True),
                       prev, bf)
                ev = dve(lambda e, half=half: e.tensor_tensor(
                    f.ap[:, 512 * half:512 * half + 512].rearrange("p (a c) -> p a c", a=2),
                    b.ap[:, :].rearrange("p (a c) -> p a c", a=2), s.ap.unsqueeze(1).to_broadcast([128, 2, 256]),
                    ALU.mult), t, dl, ff)
                b.give(ev)
            s.give(ev)
            fv = f.ap.rearrange("p (o d c) -> p o d c", o=2, d=2)
            if tt_ == 0:
                dve(lambda e: e.memset(fv[0:1, :, 1, :], 0.0))
            o1 = hsm[:, tt_, :].rearrange("p (o c) -> p o c", o=2)
            o2 = hdf_[:, tt_, :].rearrange("p (o c) -> p o c", o=2)
            dve(lambda e: e.tensor_tensor(o1, fv[:, :, 0, :], fv[:, :, 1, :], ALU.add))
            last = dve(lambda e: e.tensor_tensor(o2, fv[:, :, 0, :], fv[:, :, 1, :], ALU.subtract))
            f.give(last)
        fdone = last

        def mat(name, n):
            return wload(A[name][n].rearrange("(k p) n -> p k n", p=128), 4, 512)

        def dft(src_c, src_s, ncol, dst, ready, banks):
            for k_ in range(2):
                src = src_c if k_ == 0 else src_s
                re, rep = (dst[0], dst[2]) if k_ == 0 else (dst[1], dst[3])
                slE, vE, tE = mat("c_dft", k_)
                slO, vO, tO = mat("c_dft", 2 + k_)
                pe_last = None
                for k in range(4):
                    be, bef = banks.next()
                    bo, bof = banks.next()
                    for half, (b, bf, v, tk) in enumerate(((be, bef, vE, tE), (bo, bof, vO, tO))):
                        for t in range(4):
                            last = pe(lambda e, b=b, v=v, t=t, half=half: e.matmul(
                                b.ap[:, 0:ncol], v[:, t, 128 * k:128 * k + 128], src[:, 4 * half + t, :],
                                start=(t == 0), stop=(t == 3)), tk, bf, ready)
                    e1 = act(lambda e: e.activation(re[:, k, :], be.ap[:, 0:ncol], ACT.Copy), last)
                    be.give(e1)
                    d2 = dve(lambda e: e.tensor_tensor(rep[:, k, :], re[:, k, :], bo.ap[:, 0:ncol], ALU.subtract), e1,
                             last)
                    d1 = dve(lambda e: e.tensor_tensor(re[:, k, :], re[:, k, :], bo.ap[:, 0:ncol], ALU.add))
                    bo.give(d1)
                slE.give(last)
                slO.give(last)
            return dve(lambda e: e.tensor_scalar(dst[1], dst[1], -1.0, None, ALU.mult))

        banks = Ring([PSL[i] for i in range(8)])
        P.barrier()
        H1.at = hm
        HF = [H1.get(4, 512) for _ in range(4)]
        fh = dft(hsm, hdf_, 512, HF, fdone, banks)
        P.barrier()
        B1.at = mark
        Y = [B1.get(4, 256) for _ in range(4)]
        Z = [B1.get(4, 256) for _ in range(4)]
        tmp, tmp2 = H1.get(1024).rearrange("p (a b) -> p a b", a=4), H1.get(1024).rearrange("p (a b) -> p a b", a=4)
        dsk = B1.get(2, 256)
        dl = load("hyl", dsk, A["hy_d"][0].partition_broadcast(128))
        y = u[:, :, 0:256]
        ready = None
        for o in range(2):
            ready = dft(y, y, 256, Y, ready, banks)
            H = [x[:, :, 256 * o:256 * o + 256] for x in HF]
            for q in range(2):
                ar, ai, hr_, hi = Y[2 * q], Y[2 * q + 1], H[2 * q], H[2 * q + 1]
                zr_, zi = Z[2 * q], Z[2 * q + 1]
                dve(lambda e: e.tensor_tensor(zr_, ar, hr_, ALU.mult), ready)
                p1 = pool(lambda e: e.tensor_tensor(tmp, ai, hi, ALU.mult), ready, P.q["dve"][-2])
                dve(lambda e: e.tensor_tensor(zi, ar, hi, ALU.mult))
                p2 = pool(lambda e: e.tensor_tensor(tmp2, ai, hr_, ALU.mult))
                dve(lambda e: e.tensor_tensor(zr_, zr_, tmp, ALU.subtract), p1)
                dve(lambda e: e.tensor_tensor(zi, zi, tmp2, ALU.add), p2)
            dve(lambda e: e.tensor_tensor(Y[0], Z[0], Z[2], ALU.add))
            dve(lambda e: e.tensor_tensor(Y[1], Z[3], Z[1], ALU.subtract))
            dve(lambda e: e.tensor_tensor(Y[2], Z[0], Z[2], ALU.subtract))
            dve(lambda e: e.tensor_tensor(Y[3], Z[1], Z[3], ALU.add))
            rdy = dve(lambda e: e.tensor_scalar(Y[3], Y[3], -1.0, None, ALU.mult))
            gate = u[:, :, 256 * (o + 1):256 * (o + 2)]
            for par in range(2):
                slc, vc, tc = mat("c_idft", 2 * par)
                sls, vs, ts_ = mat("c_idft", 2 * par + 1)
                for i in range(4):
                    b, bf = banks.next()
                    for v, yy, tk in ((vc, Y[2 * par], tc), (vs, Y[2 * par + 1], ts_)):
                        for k in range(4):
                            last = pe(lambda e, v=v, yy=yy, k=k: e.matmul(
                                b.ap[:, 0:256], v[:, k, 128 * i:128 * i + 128], yy[:, k, :],
                                start=(v is vc and k == 0), stop=(v is vs and k == 3)), tk, bf, rdy)
                    tt_ = 4 * par + i
                    yv = y[:, tt_, :]
                    t_ = tmp[:, 0, :]
                    dve(lambda e: e.tensor_tensor(t_, yv, dsk[:, o, :], ALU.mult), dl)
                    dve(lambda e: e.tensor_tensor(t_, t_, b.ap[:, 0:256], ALU.add), last)
                    b.give(P.q["dve"][-1])
                    ready = dve(lambda e: e.tensor_tensor(y[:, tt_, :], t_, gate[:, tt_, :], ALU.mult))
                slc.give(last)
                sls.give(last)
        for m in range(2):
            cv = cat[:, m, :].rearrange("p (t two) -> p two t", two=2)
            for par in range(2):
                b, last = tr4([y[:, 4 * par + i, 128 * m:128 * m + 128] for i in range(4)], None, banks, ready)
                ev = act(lambda e: e.activation(cv[:, par, :], b.ap[:, :], ACT.Copy), last)
                b.give(ev)
        P.barrier()

    def out_proj(w, XT, cat, gates, blks):
        pr = Ring(PSL)
        for j in range(0, 8, 2):
            s, wv, tok = wload(wcols(w, 128 * j, 256), 8, 256)
            for m in range(2):
                for bi, (t0, n) in enumerate(blks):
                    b, bf = pr.next()
                    for k in range(8):
                        last = pe(lambda e: e.matmul(b.ap[:, 0:n], wv[:, k, 128 * m:128 * m + 128],
                                                     cat[:, k, t0:t0 + n], start=(k == 0), stop=(k == 7)), tok, bf)
                    g = gates[1 if t0 >= T else 0][:, j + m:j + m + 1]
                    x = XT[:, j + m, t0:t0 + n]
                    ev = dve(lambda e: e.scalar_tensor_tensor(x, b.ap[:, 0:n], g, x, ALU.mult, ALU.add), last)
                    b.give(ev)
            s.give(last)
        P.barrier()

    def restore_xT():
        BR.reset()
        x = BR.get(8, TT)
        it = load("xsl", x, xs)
        P.fence["dve"] = P.fence["dve"] + [it]
        P.fence["act"] = P.fence["act"] + [it]
        return x

    def mlp(XT):
        gcol = m6(5)
        hr = Ring([Slot(CAT.t[:, M0 + 4096 * i:M0 + 4096 * i + 4096].rearrange("p (a b) -> p a b", a=4))
                   for i in range(2)])
        pr = Ring(PSL)
        w1, w2 = A["w_mlp1"][0], A["w_mlp2"][0]
        hv_ = P.hT
        held = []

        def second(g, s, done):
            w2v = w2.rearrange("(k p) n -> p k n", p=128)
            for half in range(2):
                ws, wv, tok = wload(w2v[:, 4 * g:4 * g + 4, 512 * half:512 * half + 512], 4, 512)
                for m in range(4):
                    for (t0, n) in BLKS[0:2]:
                        b, bf = pr.next()
                        for k in range(4):
                            last = pe(lambda e: e.matmul(b.ap[:, :], wv[:, k, 128 * m:128 * m + 128],
                                                         s.ap[:, k, t0:t0 + n], start=(k == 0), stop=(k == 3)), tok,
                                      bf, done)
                        x = XT[:, 4 * half + m, t0:t0 + n]
                        g_ = gcol[:, 4 * half + m:4 * half + m + 1]
                        ev = dve(lambda e: e.scalar_tensor_tensor(x, b.ap[:, :], g_, x, ALU.mult, ALU.add), last)
                        b.give(ev)
                ws.give(last)
            s.give(last)

        for g in range(8):
            s, sf = hr.next()
            for half in range(2):
                ws, wv, tok = wload(wcols(w1, 512 * g + 256 * half, 256), 8, 256)
                for m in range(2):
                    for (t0, n) in BLKS[0:2]:
                        b, bf = pr.next()
                        for k in range(8):
                            last = pe(lambda e: e.matmul(b.ap[:, :], wv[:, k, 128 * m:128 * m + 128],
                                                         hv_[:, k, t0:t0 + n], start=(k == 0), stop=(k == 7)), tok,
                                      bf)
                        r1 = act(lambda e: e.activation(s.ap[:, 2 * half + m, t0:t0 + n], b.ap[:, :], ACT.Relu),
                                 last, sf)
                        b.give(r1)
                        done = pool(lambda e: e.tensor_tensor(
                            s.ap[:, 2 * half + m, t0:t0 + n], s.ap[:, 2 * half + m, t0:t0 + n],
                            s.ap[:, 2 * half + m, t0:t0 + n], ALU.mult), r1)
                ws.give(last)
            held.append((g, s, done))
            if len(held) == 2:
                second(*held.pop(0))
        second(*held.pop(0))
        P.barrier()

    def block1_end():
        CATV = CAT.t[:, M0:M0 + 8 * T].rearrange("p (a b) -> p a b", a=8)
        XT = restore_xT()
        out_proj(A["w_out"][0], XT, CATV, (m6(2), None), BLKS[0:2])
        c2 = norm_cols("norm2_g", 0, m6(4), m6(3))
        tmp = region(BR.lo + 10240, BR.hi)
        rms(XT, hT, BLKS[0:2], tmp, c2)
        P.barrier()
        mlp(XT)
        tmp.reset()
        rms(XT, XT, BLKS[0:2], tmp, None, g_only=col("final_norm_g", 0, 8))
        P.barrier()
        return XT

    C2 = {"aq": 0, "ak": 512, "av": 640, "az": 768, "mq": 1280, "mk": 1792, "mv": 2304, "mo": 2816, "mz": 3328,
          "mi": 3840, "mf": 3848}

    def mlstm(l):
        w = A["w_in_2"][l]
        last_layer = l == 1
        lat_tiles = range(8) if last_layer else range(10)
        B1 = region(M0 + 10240, total - 10240)
        C1 = region(M0, M0 + 10240)
        CX = region(CON.at, CON.hi)
        vtm = C1.get(10, 4 * 129)
        U = C1.get(TT)
        colm, AB, par = CX.get(10, 4, 8), CX.get(8, 10), CX.get(2)
        G, I, Bc, M, t1 = B1.get(TT), B1.get(TT), B1.get(TT), B1.get(TT), B1.get(TT)
        R2, MP, EN, BL = B1.get(TT), B1.get(10), B1.get(10), B1.get(10)
        R3 = B1.get(TT)
        rows_proj(w, {0: (C2["mf"], 4), 1: (C2["mf"] + 4, 4), 2: (C2["mi"], 4), 3: (C2["mi"] + 4, 4)}, G)
        z0 = dve(lambda e: e.memset(par, 0.0))
        for q, off in enumerate((8, 12, 0, 4)):
            pl = load("mpar", par[32 * q:32 * q + 4, 0:1],
                      A["gate_b_2"][l, off:off + 4].rearrange("(a b) -> a b", b=1), z0)
        dve(lambda e: e.tensor_scalar(G, G, par[:, 0:1], None, ALU.add), pl)
        dve(lambda e: e.tensor_copy(I[0:64, :], G[64:128, :]))
        F = G[0:64, :]
        dve(lambda e: e.tensor_scalar(F, F, -1.0, None, ALU.mult))
        softplus(F, t1[0:64, :], Bc[0:64, :])
        dve(lambda e: e.tensor_scalar(F, F, -1.0, None, ALU.mult), P.q["act"][-1])
        for d in range(2):
            q = slice(32 * d, 32 * d + 32)
            s = (lambda x: x[:, ::-1]) if d else (lambda x: x)
            dve(lambda e: e.tensor_tensor_scan(s(Bc[q, :]), s(rst[q, d, :]), s(G[q, :]), 0.0, ALU.mult, ALU.add))
            dve(lambda e: e.tensor_tensor_scan(s(M[q, T:TT]), s(G[q, T:TT]), s(I[q, T:TT]), NEG, ALU.add, ALU.max))
            e0 = TT - 1 if d == 0 else T
            dve(lambda e: e.tensor_tensor_scan(s(M[q, 0:T]), s(G[q, 0:T]), s(I[q, 0:T]), M[q, e0:e0 + 1], ALU.add,
                                               ALU.max))
            end = 127 if d == 0 else 0
            dve(lambda e: e.tensor_copy(EN[q, :], M[q, end:TT:128]))
            dve(lambda e: e.tensor_copy(BL[q, :], Bc[q, end:TT:128]))
            if d == 0:
                dve(lambda e: e.tensor_copy(MP[q, 1:10], EN[q, 0:9]))
                dve(lambda e: e.tensor_copy(MP[q, 0:1], EN[q, 9:10]))
                dve(lambda e: e.memset(MP[q, 8:9], NEG))
            else:
                dve(lambda e: e.tensor_copy(MP[q, 0:9], EN[q, 1:10]))
                dve(lambda e: e.memset(MP[q, 9:10], NEG))
        H = slice(0, 64)
        v10 = lambda x: x.rearrange("p (c t) -> p c t", c=10)
        b10 = lambda x: x.unsqueeze(2).to_broadcast([64, 10, 128])
        dve(lambda e: e.memset(U, 0.0))
        dve(lambda e: e.tensor_tensor(U[H, :], Bc[H, :], M[H, :], ALU.subtract))
        dve(lambda e: e.tensor_tensor(R2[H, :], I[H, :], Bc[H, :], ALU.subtract))
        dve(lambda e: e.tensor_tensor(v10(R2[64:128, :]), v10(U[H, :]), b10(MP[H, :]), ALU.add))
        dve(lambda e: e.tensor_scalar(R3[H, :], M[H, :], -1.0, None, ALU.mult))
        dve(lambda e: e.tensor_tensor(BL[H, :], BL[H, :], EN[H, :], ALU.subtract))
        dve(lambda e: e.tensor_tensor(v10(R3[64:128, :]), v10(R2[H, :]), b10(BL[H, :]), ALU.add))
        dve(lambda e: e.memset(EN, 0.0))
        rd = dve(lambda e: e.tensor_tensor(EN[H, :], BL[H, :], MP[H, :], ALU.add))
        pr = Ring(PSL)
        for c in range(10):
            b, bf = pr.next()
            pe(lambda e: e.transpose(b.ap[:, 0:128], R2[:, 128 * c:128 * c + 128], ident), rd, bf)
            t = pe(lambda e: e.transpose(b.ap[:, 128:256], R3[:, 128 * c:128 * c + 128], ident))
            src = b.ap[:, 0:256].rearrange("p (q r) -> p q r", q=8)[:, :, 0:4]
            ev = dve(lambda e: e.tensor_copy(colm[:, c, :, :].rearrange("p a b -> p (a b)").rearrange(
                "p (q r) -> p q r", q=8), src), t)
            b.give(ev)
        ex = act(lambda e: e.activation(colm[:, :, 1:4, :], colm[:, :, 1:4, :], ACT.Exp), ev)
        dve(lambda e: e.tensor_scalar(colm[:, :, 3, :], colm[:, :, 3, :], 128 ** -0.5, None, ALU.mult), ex)
        b, bf = pr.next()
        for r in range(8):
            t = pe(lambda e: e.matmul(b.ap[:, 16 * r:16 * r + 10], sel[:, r, :], EN, start=True, stop=True), rd, bf)
        ab = act(lambda e: e.activation(AB, b.ap[:, 0:128].rearrange("p (a b) -> p a b", a=8)[:, :, 0:10], ACT.Exp), t)
        b.give(ab)
        P.barrier()
        B1.reset()
        qT, kT, ktm = B1.get(4, TT), B1.get(4, TT), B1.get(10, 512)
        zr = Ring([Slot(B1.get(1028 + 260)) for _ in range(2)])
        for s in zr.slots:
            s.free = [dve(lambda e: e.memset(s.ap, 0.0))]
        cw, cwr = offs["conv_w_2"]
        pt = Ring([PSL[i] for i in (4, 5, 6, 7)])

        def outs(m):
            dst = (qT if m < 4 else kT)[:, m % 4, :]

            def fin(m, tok):
                if m < 4:
                    return
                for t0 in (0, 4, 8):
                    k = min(4, 10 - t0)
                    b, last = tr4([dst[:, 128 * (t0 + i):128 * (t0 + i) + 128] for i in range(k)], None, pt, tok)
                    o = ktm[:, t0:t0 + k, 128 * (m - 4):128 * (m - 4) + 128]
                    ev = dve(lambda e: e.tensor_copy(o, b.ap[:, 0:128 * k].rearrange("p (t c) -> p t c", t=k)), last)
                    b.give(ev)
            return dst, None, fin

        conv_channels(w, C2["mq"], 8, 5, T, lambda m, tap: vec[cw][:, cwr + 40 * l + 8 * tap + m:
                      cwr + 40 * l + 8 * tap + m + 1], lambda m: col("conv_b_2", 8 * l + m, 1), zr, outs,
                      fn=ACT.Silu)
        v5 = vtm.rearrange("p t (h x) -> p t h x", h=4)
        dve(lambda e: e.memset(v5[:, :, :, 128:129].rearrange("p t h x -> p (t h) x"), 1.0))

        def vsink(t, c, n, b, tok):
            o = v5[:, t, c // 128:c // 128 + 2, 0:128]
            return dve(lambda e: e.tensor_copy(o, b[:, 0:n].rearrange("p (h x) -> p h x", h=2)), tok)

        proj_tm(w, C2["mv"], 512, vsink, range(10))
        P.barrier()
        H1 = region(total - 10240, total)
        hacc = H1.get(10, 512)
        B1.at = B1.lo + 3 * 5120
        hdone = {}

        def scan(d):
            E, Pm, wv, hn = H1.get(512), H1.get(512), H1.get(516), H1.get(516)
            Cs, dn = B1.get(516), B1.get(8)
            pr = Ring([PSL[4 * d + i] for i in range(4)])
            st = dve(lambda e: e.memset(Cs, 0.0))
            order = [8, 9] + list(range(8)) if d == 0 else [9, 8] + list(range(7, -1, -1))
            pe_last = None
            for c in order:
                want = c < 8 or not last_layer
                ts = slice(128 * c, 128 * c + 128)
                cc = lambda g, h, c=c: colm[:, c, g, 4 * d + h:4 * d + h + 1]
                wvd = pool(lambda e: e.tensor_tensor(h4(wv, 129), v5[:, c, :, :],
                                                     bc(colm[:, c, 3, 4 * d:4 * d + 4], 129), ALU.mult), pe_last)
                if want:
                    b, bf = pr.next()
                    for h in range(4):
                        t = pe(lambda e: e.matmul(b.ap[:, 128 * h:128 * h + 128], sel[:, 4 * d + h, :], U[:, ts],
                                                  start=True, stop=True), bf)
                    sb_, sf = pr.next()
                    for h in range(4):
                        t_s = pe(lambda e: e.matmul(sb_.ap[:, 128 * h:128 * h + 128], kT[:, h, ts], qT[:, h, ts],
                                                    start=True, stop=True), sf)
                    yield
                    for h in range(4):
                        a = dve(lambda e: e.scalar_tensor_tensor(
                            E[:, 128 * h:128 * h + 128], b.ap[:, 128 * h:128 * h + 128], cc(0, h), mt[:, d, :],
                            ALU.add, ALU.min), t)
                    b.give(a)
                    ex = act(lambda e: e.activation(E, E, ACT.Exp), a)
                    yield
                    pm_ = dve(lambda e: e.scalar_tensor_tensor(Pm, sb_.ap[:, :], 128 ** -0.5, E, ALU.mult, ALU.mult),
                              t_s, ex, pe_last)
                    sb_.give(pm_)
                    for hh in range(2):
                        xb, xf = pr.next()
                        yb, yf = pr.next()
                        for j in range(2):
                            h = 2 * hh + j
                            sl = slice(129 * h, 129 * h + 129)
                            tx = pe(lambda e: e.matmul(xb.ap[:, 129 * j:129 * j + 129], Pm[:, 128 * h:128 * h + 128],
                                                       vtm[:, c, sl], start=True, stop=True), pm_, xf)
                            ty = pe(lambda e: e.matmul(yb.ap[:, 129 * j:129 * j + 129], qT[:, h, ts], Cs[:, sl],
                                                       start=True, stop=True), st, yf)
                        cp = act(lambda e: e.activation(hn[:, 258 * hh:258 * hh + 258], xb.ap[:, 0:258], ACT.Copy),
                                 tx)
                        xb.give(cp)
                        for j in range(2):
                            h = 2 * hh + j
                            o = hn[:, 129 * h:129 * h + 129]
                            a = dve(lambda e: e.scalar_tensor_tensor(o, yb.ap[:, 129 * j:129 * j + 129], cc(1, h), o,
                                                                     ALU.mult, ALU.add), ty, cp)
                        yb.give(a)
                    yield
                    den = h4(hn, 129)[:, :, 128]
                    dve(lambda e: e.scalar_tensor_tensor(dn[:, 0:4], den, -1.0, den, ALU.mult, ALU.max))
                    dve(lambda e: e.tensor_tensor(dn[:, 0:4], dn[:, 0:4], colm[:, c, 2, 4 * d:4 * d + 4], ALU.max))
                    dve(lambda e: e.reciprocal(dn[:, 4:8], dn[:, 0:4]))
                    o = h4(hacc[:, c, :], 128)
                    num = h4(hn, 129)[:, :, 0:128]
                    if c not in hdone:
                        hdone[c] = dve(lambda e: e.tensor_tensor(o, num, bc(dn[:, 4:8], 128), ALU.mult))
                    else:
                        dve(lambda e: e.tensor_tensor(num, num, bc(dn[:, 4:8], 128), ALU.mult))
                        hdone[c] = dve(lambda e: e.tensor_tensor(o, o, num, ALU.add), hdone[c])
                yield
                bs = []
                for hh in range(2):
                    b, bf = pr.next()
                    for j in range(2):
                        h = 2 * hh + j
                        t = pe(lambda e: e.matmul(b.ap[:, 129 * j:129 * j + 129], ktm[:, c, 128 * h:128 * h + 128],
                                                  wv[:, 129 * h:129 * h + 129], start=True, stop=True), wvd, bf)
                    bs.append((b, t))
                pe_last = t
                for hh in range(2):
                    b, t = bs[hh]
                    for j in range(2):
                        h = 2 * hh + j
                        o = Cs[:, 129 * h:129 * h + 129]
                        st = dve(lambda e: e.scalar_tensor_tensor(o, o, AB[:, 4 * d + h, c:c + 1],
                                                                  b.ap[:, 129 * j:129 * j + 129], ALU.mult, ALU.add),
                                 t, pe_last)
                    b.give(st)
                yield

        interleave([scan(0), scan(1)])
        P.barrier()
        B1.reset()
        P.hT = B1.get(8, TT)
        hl = load("hsl", P.hT, hs)
        P.fence["pe"] = P.fence["pe"] + [hl]
        gb = B1.get(512)
        gl = load("gb", gb, A["head_g_2"][l].partition_broadcast(128))
        tr = Ring([Slot(B1.get(256)) for _ in range(4)])
        sq, s10 = B1.get(512), B1.get(10, 4)

        def osink(t, c, n, b, tok):
            s, sf = tr.next()
            a = act(lambda e: e.activation(s.ap, b[:, 0:n], ACT.Sigmoid), tok, sf)
            y = pool(lambda e: e.tensor_tensor(hacc[:, t, c:c + n], hacc[:, t, c:c + n], s.ap, ALU.mult), a)
            s.give(y)
            return a

        proj_tm(w, C2["mo"], 512, osink, lat_tiles)
        pl = P.q["pool"][-1]
        for t in lat_tiles:
            dve(lambda e: e.tensor_tensor(sq, hacc[:, t, :], hacc[:, t, :], ALU.mult), pl)
            a = dve(lambda e: e.tensor_reduce(s10[:, t, :], h4(sq, 128), AXX, ALU.add))
        nt = len(lat_tiles)
        a = dve(lambda e: e.tensor_scalar(s10[:, 0:nt, :], s10[:, 0:nt, :], 1.0 / 128, 1e-6, ALU.mult, ALU.add))
        act(lambda e: e.activation(s10[:, 0:nt, :], s10[:, 0:nt, :], ACT.Ln), a)
        a = act(lambda e: e.activation(s10[:, 0:nt, :], s10[:, 0:nt, :], ACT.Exp, scale=-0.5))
        for t in lat_tiles:
            dve(lambda e: e.tensor_tensor(h4(hacc[:, t, :], 128), h4(hacc[:, t, :], 128), bc(s10[:, t, :], 128),
                                          ALU.mult), a)
            nd = dve(lambda e: e.tensor_tensor(hacc[:, t, :], hacc[:, t, :], gb, ALU.mult), gl)
        catm = CAT.t[:, M0 + 5120:M0 + 10240].rearrange("p (m t) -> p m t", m=4)
        pt = Ring([PSL[i] for i in range(4)])

        def zsink(t, c, n, b, tok):
            s, sf = tr.next()
            a = act(lambda e: e.activation(s.ap, b[:, 0:n], ACT.Silu), tok, sf)
            y = pool(lambda e: e.tensor_tensor(s.ap, hacc[:, t, c:c + n], s.ap, ALU.mult), a, nd)
            b2, last = tr4([s.ap[:, 0:128], s.ap[:, 128:256]], None, pt, y)
            s.give(last)
            o = catm[:, c // 128:c // 128 + 2, 128 * t:128 * t + 128]
            ev = dve(lambda e: e.tensor_copy(o, b2.ap[:, 0:256].rearrange("p (m t) -> p m t", m=2)), last)
            b2.give(ev)
            return a

        proj_tm(w, C2["mz"], 512, zsink, lat_tiles)
        P.barrier()

    def attention(l):
        w = A["w_in_2"][l]
        last_layer = l == 1
        H1 = region(total - 10240, total)
        B1 = region(M0 + 10240 + 10240, total - 10240)
        cata = CAT.t[:, M0:M0 + 5120].rearrange("p (m t) -> p m t", m=4)
        hv_ = P.hT
        qT, kT, vtm = H1.get(4, TT), H1.get(TT), H1.get(10, 128)
        cos, sin, rot, wm = H1.get(T), H1.get(T), H1.get(128), H1.get(384)
        CX = region(CON.at, CON.hi)
        snk = CX.get(8)
        for dst, src in ((cos, A["c_cos"]), (sin, A["c_sin"]), (rot, A["c_rot"]), (wm, A["c_wm"]),
                         (snk, A["sink_2"][l].partition_broadcast(128))):
            cl = load("att", dst, src)
        t1 = Ring([Slot(B1.get(512)) for _ in range(2)])
        t2 = Ring([Slot(B1.get(512)) for _ in range(2)])
        pr = Ring([PSL[i] for i in range(4)])
        p2 = Ring([PSL[i] for i in range(4, 8)])

        def rope_sink(dst, t0, n, b, tok):
            if t0 >= T:
                return act(lambda e: e.activation(dst, b.ap[:, 0:n], ACT.Copy), tok)
            s, sf = t1.next()
            a = act(lambda e: e.activation(s.ap, b.ap[:, :], ACT.Copy), tok, sf)
            b2, bf2 = p2.next()
            r = pe(lambda e: e.matmul(b2.ap[:, :], rot, s.ap, start=True, stop=True), a, bf2, cl)
            u, uf = t2.next()
            rs = dve(lambda e: e.tensor_tensor(u.ap, b2.ap[:, :], sin[:, t0:t0 + n], ALU.mult), r, uf, cl)
            b2.give(rs)
            m = pool(lambda e: e.tensor_tensor(s.ap, s.ap, cos[:, t0:t0 + n], ALU.mult), r, a, cl)
            f = dve(lambda e: e.tensor_tensor(dst, s.ap, u.ap, ALU.add), m)
            s.give(f)
            u.give(f)
            return a

        for j in range(0, 6, 2):
            s, free = W.next()
            nt = 2 if j < 4 else 1
            view = s.ap[:, 0:8 * 128 * nt].rearrange("p (k n) -> p k n", k=8)
            if j < 4:
                for m in range(2):
                    for hf in range(2):
                        c0 = 64 * (j + m + 4 * hf)
                        tok = P.dma(s.lane, lambda e: e.dma_start(
                            view[:, :, 128 * m + 64 * hf:128 * m + 64 * hf + 64], wcols(w, c0, 64)), free)
            else:
                tok = P.dma(s.lane, lambda e: e.dma_start(view, wcols(w, C2["ak"], 128)), free)
            for m in range(nt):
                for (t0, n) in BLKS:
                    b, bf = pr.next()
                    for k in range(8):
                        last = pe(lambda e: e.matmul(b.ap[:, 0:n], view[:, k, 128 * m:128 * m + 128],
                                                     hv_[:, k, t0:t0 + n], start=(k == 0), stop=(k == 7)), tok, bf)
                    dst = qT[:, j + m, t0:t0 + n] if j < 4 else kT[:, t0:t0 + n]
                    b.give(rope_sink(dst, t0, n, b, last))
            s.give(last)

        def vsink(t, c, n, b, tok):
            return act(lambda e: e.activation(vtm[:, t, :], b[:, 0:n], ACT.Copy), tok)

        proj_tm(w, C2["av"], 128, vsink, range(10))
        P.barrier()
        B1.reset()
        zs = [wload(wcols(w, C2["az"] + 256 * i, 256), 8, 256) for i in range(2)]
        Sr = Ring([Slot(B1.get(4, 640)) for _ in range(2)])
        Pr = Ring([Slot(B1.get(640)) for _ in range(2)])
        og, zg = B1.get(512), H1.t[:, H1.lo + 7680:H1.lo + 8192]
        st = CX.get(2, 24)
        sb_ = Ring([PSL[i] for i in (0, 1, 2, 3)])
        tb = Ring([PSL[i] for i in (4, 5)])
        ob = Ring([PSL[i] for i in (6, 7)])
        scale = 64 ** -0.5
        og_free = zg_free = None
        blocks = range(8) if last_layer else range(10)
        for n in blocks:
            ctx = n >= 8
            kb = [] if ctx else [k for k in (n - 1, n, n + 1) if 0 <= k < 8]
            lo = 384 if ctx else (128 if n == 0 else 0)
            o_, of = ob.next()
            for g in range(2):
                S, Sf = Sr.next()
                for h in range(4):
                    q = qT[64 * g:64 * g + 64, h, 128 * n:128 * n + 128]
                    ev1 = None
                    if kb:
                        b, bf = sb_.next()
                        c0, c1 = 128 * (kb[0] - n + 1), 128 * (kb[-1] - n + 2)
                        t = pe(lambda e: e.matmul(b.ap[:, c0:c1], q, kT[64 * g:64 * g + 64,
                                                                       128 * kb[0]:128 * kb[-1] + 128],
                                                  start=True, stop=True), bf)
                        ev1 = dve(lambda e: e.scalar_tensor_tensor(S.ap[:, h, c0:c1], b.ap[:, c0:c1], scale,
                                                                   wm[:, c0:c1], ALU.mult, ALU.add), t, Sf)
                        b.give(ev1)
                        if n == 7:
                            dve(lambda e: e.memset(S.ap[:, h, 256:384], NEG))
                    b, bf = sb_.next()
                    t = pe(lambda e: e.matmul(b.ap[:, 0:256], q, kT[64 * g:64 * g + 64, T:TT], start=True,
                                              stop=True), bf)
                    ev2 = act(lambda e: e.activation(S.ap[:, h, 384:640], b.ap[:, 0:256], ACT.Copy, scale=scale), t,
                              Sf)
                    b.give(ev2)
                mx, nm, sm, es = (st[:, g, 4 * i:4 * i + 4] for i in range(4))
                dve(lambda e: e.tensor_reduce(mx, S.ap[:, :, lo:640], AXX, ALU.max), ev2)
                dve(lambda e: e.tensor_tensor(mx, mx, snk[:, 4 * g:4 * g + 4], ALU.max), cl)
                dve(lambda e: e.tensor_scalar(nm, mx, -1.0, None, ALU.mult))
                dd = dve(lambda e: e.tensor_tensor(es, snk[:, 4 * g:4 * g + 4], mx, ALU.subtract))
                exs = []
                for h in range(4):
                    exs.append(act(lambda e: e.activation(S.ap[:, h, lo:640], S.ap[:, h, lo:640], ACT.Exp,
                                                          bias=nm[:, h:h + 1], accum_out=sm[:, h:h + 1]), dd))
                ea = act(lambda e: e.activation(es, es, ACT.Exp))
                dve(lambda e: e.tensor_tensor(sm, sm, es, ALU.add), ea)
                dve(lambda e: e.reciprocal(sm, sm))
                kt = [(k - n + 1, k) for k in kb] + [(3, 8), (4, 9)]
                for h in range(4):
                    p, pf = Pr.next()
                    evs = []
                    for i0 in range(0, len(kt), 4):
                        b, bf = tb.next()
                        grp = kt[i0:i0 + 4]
                        for i, (slot, k) in enumerate(grp):
                            t = pe(lambda e: e.transpose(b.ap[:, 128 * i:128 * i + 128],
                                                         S.ap[:, h, 128 * slot:128 * slot + 128], ident), exs[h], bf)
                        o = p.ap[:, 128 * i0:128 * (i0 + len(grp))]
                        if i0 == 0:
                            ev = dve(lambda e: e.tensor_copy(o, b.ap[:, 0:128 * len(grp)]), t, pf)
                        else:
                            ev = act(lambda e: e.activation(o, b.ap[:, 0:128 * len(grp)], ACT.Copy), t, pf)
                        b.give(ev)
                        evs.append(ev)
                    hd = 4 * g + h
                    for i, (slot, k) in enumerate(kt):
                        t = pe(lambda e: e.matmul(o_.ap[:, 64 * hd:64 * hd + 64], p.ap[:, 128 * i:128 * i + 128],
                                                  vtm[:, k, 64 * g:64 * g + 64], start=(i == 0),
                                                  stop=(i == len(kt) - 1)), evs, of)
                    p.give(t)
                S.give(t)
                o4 = o_.ap[:, 256 * g:256 * g + 256].rearrange("p (h x) -> p h x", h=4)
                ev = dve(lambda e: e.tensor_tensor(h4(og[:, 256 * g:256 * g + 256], 64), o4, bc(sm, 64), ALU.mult), t,
                         og_free)
            o_.give(ev)
            for i in range(2):
                b, bf = sb_.next()
                wv, tok = zs[i][1], zs[i][2]
                for k in range(8):
                    t = pe(lambda e: e.matmul(b.ap[:, 0:256], hv_[:, k, 128 * n:128 * n + 128], wv[:, k, :],
                                              start=(k == 0), stop=(k == 7)), tok, bf)
                a = act(lambda e: e.activation(zg[:, 256 * i:256 * i + 256], b.ap[:, 0:256], ACT.Silu), t, zg_free)
                b.give(a)
            m = dve(lambda e: e.tensor_tensor(og, og, zg, ALU.mult), a)
            zg_free = m
            b, last = tr4([og[:, 128 * i:128 * i + 128] for i in range(4)], None, tb, m)
            og_free = last
            ev = act(lambda e: e.activation(cata[:, :, 128 * n:128 * n + 128],
                                            b.ap[:, :].rearrange("p (m t) -> p m t", m=4), ACT.Copy), last)
            b.give(ev)
        for z_ in zs:
            z_[0].give(t)
        P.barrier()

    def block2(XT):
        R1.reset()
        load_xT(XT, [(A["ctx_2"][0], T)])
        P.barrier()
        for l in range(2):
            md = adac[:, l, :, :]
            modulation(A["w_ada_2"][l], 1, 24, col("b_ada_2", 24 * l, 24), md, psum[6])
            c = norm_cols("norm_g_2", 8 * l, md[:, 8:16, 0], md[:, 0:8, 0], md[:, 8:16, 1], md[:, 0:8, 1])
            tmp = region(BR.lo + 10240, BR.hi)
            P.barrier()
            P.hT = hT
            rms(XT, hT, BLKS, tmp, c)
            P.barrier()
            store("hs", hs, hT)
            store("xs", xs, XT)
            P.barrier()
            mlstm(l)
            attention(l)
            XT = restore_xT()
            CATV = CAT.t[:, M0:M0 + 8 * TT].rearrange("p (a b) -> p a b", a=8)
            out_proj(A["w_out_2"][l], XT, CATV, (md[:, 16:24, 0], md[:, 16:24, 1]), BLKS if l == 0 else BLKS[0:2])
        tmp = region(BR.lo + 10240, BR.hi)
        rms(XT, XT, BLKS[0:2], tmp, None, g_only=col("final_g_2", 0, 8))
        P.barrier()
        st = Ring([Slot(R1.t[:, R1.lo + 1024 * i:R1.lo + 1024 * i + 1024], lane=f"o{i}") for i in range(3)])
        pr = Ring(PSL)
        for t in range(8):
            s, sf = st.next()
            evs = []
            for half in range(2):
                b, last = tr4([XT[:, 4 * half + k, 128 * t:128 * t + 128] for k in range(4)], None, pr, None)
                dst = s.ap[:, 512 * half:512 * half + 512]
                if half:
                    ev = dve(lambda e: e.tensor_copy(dst, b.ap[:, :]), last, sf)
                else:
                    ev = act(lambda e: e.activation(dst, b.ap[:, :], ACT.Copy), last, sf)
                b.give(ev)
                evs.append(ev)
            it = P.dma(s.lane, lambda e: e.dma_start(out[0, 128 * t:128 * t + 128, :], s.ap), *evs, eng="pool")
            s.give(it)
            P.outs = [x for x in P.outs if x.lane != s.lane] + [it]

    gdn()
    gla()
    hyena()
    XT = block1_end()
    block2(XT)

_OUTS = [((1, 1024, 1024), "float32")]


def kernel(**inputs):
    import numpy as _np
    import concourse.bacc as _bacc
    from concourse import mybir as _mybir
    from concourse.bass_utils import run_bass_kernel_spmd as _run

    nc = _bacc.Bacc("TRN2", target_bir_lowering=False, num_devices=1)
    arrays = {f"in_{k}": _np.ascontiguousarray(v) for k, v in inputs.items()}
    arrays.update(constants())
    A = {}
    for name, a in arrays.items():
        A[name.removeprefix("in_")] = nc.dram_tensor(name, a.shape, _mybir.dt.from_np(a.dtype), kind="ExternalInput").ap()
    o = nc.dram_tensor("out_0", _OUTS[0][0], F32, kind="ExternalOutput").ap()
    build(nc, A, o)
    r = _run(nc, [arrays], core_ids=[0])
    return r.results[0]["out_0"]
```

```python
import math
from contextlib import ExitStack

import numpy as np
import concourse.bass as bass
from concourse import mybir

F32 = mybir.dt.float32
I32 = mybir.dt.int32
ALU = mybir.AluOpType
ACT = mybir.ActivationFunctionType
AXX = mybir.AxisListType.X

T, TC, TT = 1024, 256, 1280
D = 1024
NEG = -1.0e30
BLKS = [(0, 512), (512, 512), (1024, 256)]
ENGINES = ("pe", "act", "dve", "pool", "sp")


class Item:

    __slots__ = ("eng", "fn", "after", "need", "val", "lane")

    def __init__(self, eng, fn, after, lane=None):
        self.eng, self.fn, self.after, self.lane = eng, fn, after, lane
        self.need, self.val = False, 0


class Calls:

    def matmul(self, *a, **k):
        return lambda e: e.matmul(*a, **k)

    def transpose(self, *a, **k):
        return lambda e: e.transpose(*a, **k)

    def activation(self, *a, **k):
        return lambda e: e.activation(*a, **k)

    def tensor_copy(self, *a, **k):
        return lambda e: e.tensor_copy(*a, **k)

    def tensor_tensor(self, *a, **k):
        return lambda e: e.tensor_tensor(*a, **k)

    def tensor_scalar(self, *a, **k):
        return lambda e: e.tensor_scalar(*a, **k)

    def scalar_tensor_tensor(self, *a, **k):
        return lambda e: e.scalar_tensor_tensor(*a, **k)

    def tensor_reduce(self, *a, **k):
        return lambda e: e.tensor_reduce(*a, **k)

    def tensor_tensor_scan(self, *a, **k):
        return lambda e: e.tensor_tensor_scan(*a, **k)

    def copy_predicated(self, *a, **k):
        return lambda e: e.copy_predicated(*a, **k)

    def reciprocal(self, *a, **k):
        return lambda e: e.reciprocal(*a, **k)

    def memset(self, *a, **k):
        return lambda e: e.memset(*a, **k)

    def dma_start(self, *a, **k):
        return lambda e: e.dma_start(*a, **k)


CALLS = Calls()


class Prog:

    def __init__(self, nc, ctx):
        self.nc, self.ctx = nc, ctx
        self.q = {e: [] for e in ENGINES}
        self.sem = {e: ctx.enter_context(nc.semaphore(f"s_{e}")) for e in ENGINES if e != "sp"}
        self.lanes = {}
        self.fence = {e: [] for e in ENGINES}
        self.outs = []

    def add(self, eng, fn, after, lane=None):
        flat = []
        for a in after:
            if isinstance(a, (list, tuple)):
                flat += [x for x in a if x is not None]
            elif a is not None:
                flat.append(a)
        flat += self.fence[eng]
        self.fence[eng] = []
        it = Item(eng, fn(CALLS), flat, lane)
        for a in flat:
            a.need = True
        self.q[eng].append(it)
        return it

    def pe(self, fn, *after):
        return self.add("pe", fn, after)

    def act(self, fn, *after):
        return self.add("act", fn, after + tuple(self.q["act"][-1:]))

    def dve(self, fn, *after):
        return self.add("dve", fn, after + tuple(x for x in self.q["dve"][-1:]))

    def pool(self, fn, *after):
        return self.add("pool", fn, after + tuple(self.q["pool"][-1:]))

    def dma(self, lane, fn, *after, eng="sp"):
        if lane not in self.lanes:
            self.lanes[lane] = [self.ctx.enter_context(self.nc.semaphore(f"l_{lane}")), 0]
        it = self.add(eng, fn, after, lane)
        self.lanes[lane][1] += 16
        it.val = self.lanes[lane][1]
        return it

    def barrier(self):
        last = []
        for e in ENGINES:
            comp = [x for x in self.q[e] if x.lane is None]
            last += comp[-1:]
        last += [x for x in self.pending if x is not None]
        self.pending = []
        for e in ENGINES:
            if e != "sp":
                self.fence[e] = self.fence[e] + last

    pending = []

    def emit(self, block):
        for e in ENGINES:
            n = 0
            for it in self.q[e]:
                if it.lane is None and it.need:
                    n += 1
                    it.val = n

        def run(e, eng):
            seen = {}
            for it in self.q[e]:
                for a in it.after:
                    key = ("lane", a.lane) if a.lane is not None else a.eng
                    if seen.get(key, 0) >= a.val:
                        continue
                    seen[key] = a.val
                    sem = self.lanes[a.lane][0] if a.lane is not None else self.sem[a.eng]
                    eng.wait_ge(sem, a.val)
                ins = it.fn(eng)
                if it.lane is not None:
                    ins.then_inc(self.lanes[it.lane][0], 16)
                elif it.need:
                    ins.then_inc(self.sem[e], 1)
            if e == "sp":
                for a in self.outs:
                    eng.wait_ge(self.lanes[a.lane][0], a.val)

        block.tensor(lambda eng: run("pe", eng))
        block.scalar(lambda eng: run("act", eng))
        block.vector(lambda eng: run("dve", eng))
        block.gpsimd(lambda eng: run("pool", eng))
        block.sync(lambda eng: run("sp", eng))


class Slot:

    def __init__(self, ap, lane=None):
        self.ap, self.free, self.lane, self.held = ap, [], lane, False

    def take(self):
        assert not self.held, "taken twice"
        self.held = True
        f, self.free = self.free, []
        return f

    def give(self, *toks):
        assert self.held
        self.held = False
        self.free = [t for t in toks if t is not None]


class Ring:
    def __init__(self, slots):
        self.slots, self.n = slots, 0

    def next(self):
        s = self.slots[self.n % len(self.slots)]
        self.n += 1
        return s, s.take()


def interleave(gens):
    gens = list(gens)
    while gens:
        for g in list(gens):
            try:
                next(g)
            except StopIteration:
                gens.remove(g)


def constants():
    c = {}
    f = np.float32
    c["c_ident"] = np.eye(128, dtype=f)
    sel = np.zeros((128, 8, 128), f)
    for d in range(2):
        for h in range(4):
            sel[32 * d + h, 4 * d + h, :] = 1.0
    c["c_sel"] = sel.reshape(128, 1024)
    rst = np.ones((128, 2, TT), f)
    rst[:, 0, 0::128] = 0.0
    rst[:, 1, 127::128] = 0.0
    c["c_rst"] = rst.reshape(128, 2 * TT)
    j, i = np.meshgrid(np.arange(128), np.arange(128), indexing="ij")
    mt = np.zeros((128, 2, 128), f)
    mt[:, 0] = np.where(i >= j, 0.0, NEG)
    mt[:, 1] = np.where(i <= j, 0.0, NEG)
    c["c_mt"] = mt.reshape(128, 256)
    lv = np.zeros((128, 2, 7, 128), f)
    for n in range(7):
        s = 1 << n
        same = (i // (2 * s)) == (j // (2 * s))
        lv[:, 0, n] = same & (j % (2 * s) < s) & (i % (2 * s) >= s)
        lv[:, 1, n] = same & (j % (2 * s) >= s) & (i % (2 * s) < s)
    c["c_lv"] = lv.reshape(128, 2 * 7 * 128)
    pm = np.zeros((128, 2, 4, 128), np.int32)
    pm[:, 0] = (i >= j)[:, None, :]
    pm[:, 1] = (i <= j)[:, None, :]
    c["c_pm"] = pm.reshape(128, 1024)
    sg = np.ones((128, 1), f)
    sg[64:] = -1.0
    c["c_sgn"] = sg
    q = np.arange(128)[:, None]
    k = np.arange(384)[None, :] - 128
    c["c_wm"] = np.where(np.abs(q - k) <= 128, 0.0, NEG).astype(f)
    inv = (10000.0 ** (-np.arange(0, 32, 2, dtype=f) / f(32))).astype(f)
    row = np.repeat(np.arange(T // 64), 64).astype(f)
    col = np.tile(np.arange(64), T // 64).astype(f)
    cos = np.zeros((128, T), f)
    sin = np.zeros((128, T), f)
    rt = np.zeros((128, 128), f)
    for p in range(128):
        dd = p % 64
        pos = row if dd < 32 else col
        ang = (pos * inv[dd % 16]).astype(f)
        cos[p], sin[p] = np.cos(ang), np.sin(ang)
        if dd % 32 < 16:
            rt[p + 16, p] = -1.0
        else:
            rt[p - 16, p] = 1.0
    c["c_cos"], c["c_sin"], c["c_rot"] = cos, sin, rt
    tt = np.linspace(0.0, 1.0, T, dtype=f)[:, None]
    fr = np.linspace(1e-4, 15, 16, dtype=f)
    w = (f(2 * math.pi) * np.arange(T, dtype=f) / f(T)).astype(f)
    ang = (w[:, None] * fr[None, :]).astype(f)
    z = np.concatenate([tt, np.cos(ang), -np.sin(ang)], axis=-1).astype(f)
    c["c_z"] = np.ascontiguousarray(z.T)
    deltas = np.abs(np.linspace(math.log(1e-2) / 1.5, math.log(1e-2) / 0.3, 256, dtype=f))
    dec = np.exp((-tt * deltas[None, :]).astype(f)).astype(f)
    perm = np.concatenate([np.arange(0, T, 2), np.arange(1, T, 2)])
    c["c_dec"] = np.ascontiguousarray(dec[perm])
    kk = np.arange(512)[None, :].astype(np.float64)
    tm = np.zeros((4, 512, 512))
    for e in range(2):
        t = (2 * np.arange(512) + e)[:, None].astype(np.float64)
        a = math.pi * (2 * kk + 1) * t / 2048.0
        tm[2 * e], tm[2 * e + 1] = np.cos(a), np.sin(a)
    c["c_dft"] = tm.astype(f)
    c["c_idft"] = (tm.transpose(0, 2, 1) / 1024.0).astype(f)
    return {k: np.ascontiguousarray(v) for k, v in c.items()}


SMALL_ROWS = {
    0: [("b_mod", 48), ("norm1_g", 8), ("norm2_g", 8), ("final_norm_g", 8), ("hy_conv_b", 6), ("c", 8),
        ("c_ctx", 8), ("c_2", 8), ("c_ctx_2", 8)],
    1: [("b_ada_2", 48), ("norm_g_2", 16), ("conv_b_2", 16), ("final_g_2", 8)],
    2: [("hy_conv_w", 18), ("conv_w_2", 80)],
    3: [("gdn_conv_w", 63)],
}


def build(nc, A, out):
    ctx = ExitStack()
    with ctx:
        P = Prog(nc, ctx)
        P.pending = []
        emit_all(nc, ctx, P, A, out)
        with nc.Block() as block:
            P.emit(block)


class Arena:
    def __init__(self, t, lo, hi):
        self.t, self.lo, self.hi, self.at = t, lo, hi, lo

    def reset(self, at=None):
        self.at = self.lo if at is None else at

    def get(self, *dims, parts=128, dt=F32):
        n = int(np.prod(dims))
        assert self.at + n <= self.hi, ("arena", self.at, n, self.hi)
        ap = self.t[0:parts, self.at:self.at + n]
        self.at += n
        if dt is not F32:
            ap = ap.bitcast(dt)
        if len(dims) == 2:
            ap = ap.rearrange("p (a b) -> p a b", a=dims[0])
        elif len(dims) == 3:
            ap = ap.rearrange("p (a b c) -> p a b c", a=dims[0], b=dims[1])
        return ap


def emit_all(nc, ctx, P, A, out):
    pe, act, dve, pool = P.pe, P.act, P.dve, P.pool

    total = 52800
    big = ctx.enter_context(nc.sbuf_tensor("big", [128, total], F32))
    psum = [ctx.enter_context(nc.psum_tensor(f"ps{i}", [128, 512], F32)) for i in range(8)]
    PSL = [Slot(p) for p in psum]
    xs = nc.dram_tensor("xs_scratch", [128, 8, TT], F32, kind="Internal").ap()
    hs = nc.dram_tensor("hs_scratch", [128, 8, TT], F32, kind="Internal").ap()

    CON = Arena(big, 0, 5900)
    ringm = Arena(big, 5900, 5900 + 4 * 2048)
    M0 = 14092
    R1 = Arena(big, total - 10240, total)
    CAT = Arena(big, M0, M0 + 10240)
    BR = Arena(big, M0 + 10240, total - 10240)

    W = Ring([Slot(ringm.get(2048), lane=f"w{i}") for i in range(4)])

    def wload(src, kt, n, parts=128):
        s, free = W.next()
        view = s.ap[0:parts, 0:kt * n].rearrange("p (k n) -> p k n", k=kt)
        tok = P.dma(s.lane, lambda e: e.dma_start(view, src), *free)
        return s, view, tok

    def wcols(w, c0, n, kt=8):
        return w.rearrange("(k p) n -> p k n", p=128)[:, 0:kt, c0:c0 + n]

    def load(lane, dst, src, *after):
        return P.dma(lane, lambda e: e.dma_start(dst, src), *after, eng="pool")

    def store_late(lane, dst, src, *after):
        return P.dma(lane, lambda e: e.dma_start(dst, src), *after, eng="pool")

    def store(lane, dst, src, *after):
        it = P.dma(lane, lambda e: e.dma_start(dst, src), *after, eng="pool")
        P.pending.append(it)
        return it

    ident = CON.get(128)
    ones = CON.get(128)
    sel = CON.get(8, 128)
    rst = CON.get(2, TT)
    mt = CON.get(2, 128)
    sgn = CON.get(1)
    vec = [CON.get(128) for _ in range(4)]
    modc = CON.get(48, 2)
    adac = CON.get(2, 24, 2)
    nA = CON.get(2, 8)
    nB = CON.get(2, 8)
    sc = CON.get(2, 8, 2)
    cst = [load("cst", ident, A["c_ident"]), load("cst", sel, A["c_sel"].rearrange("p (a b) -> p a b", a=8)),
           load("cst", rst, A["c_rst"].rearrange("p (a b) -> p a b", a=2)),
           load("cst", mt, A["c_mt"].rearrange("p (a b) -> p a b", a=2)), load("cst", sgn, A["c_sgn"])]
    stage = [BR.get(128) for _ in range(4)]
    z = [dve(lambda e, s=s: e.memset(s, 0.0)) for s in stage]
    offs = {}
    for n, rows in SMALL_ROWS.items():
        r = 0
        for name, k in rows:
            src = A[name]
            flat = src.rearrange(" ".join("abcd"[:len(src.shape)]) + " -> (" + " ".join("abcd"[:len(src.shape)]) + ")") \
                if len(src.shape) > 1 else src
            cst.append(load("cst", stage[n][r:r + k, :], flat.rearrange("(r q) -> r q", q=128), z[n]))
            offs[name] = (n, r)
            r += k
    ok = cst[-1]
    dve(lambda e: e.memset(ones, 1.0))
    vt = []
    for n in range(4):
        t = pe(lambda e, n=n: e.transpose(psum[n][:, 0:128], stage[n], ident), ok)
        vt.append(dve(lambda e, n=n: e.tensor_copy(vec[n], psum[n][:, 0:128]), t))

    def col(name, j, n=1):
        k, r = offs[name]
        return vec[k][:, r + j:r + j + n]

    for b, names in enumerate((("c", "c_ctx"), ("c_2", "c_ctx_2"))):
        for k, nm in enumerate(names):
            sctok = act(lambda e, b=b, k=k, nm=nm: e.activation(sc[:, b, :, k], col(nm, 0, 8), ACT.Silu), vt)
    P.barrier()
    BR.reset()

    modrow = CON.get(256)[0:2, :]

    def modulation(w, b, j0, j1, bias, dst, banks, gap=0):
        pr = Ring([PSL[i] for i in banks])

        def turn(j, bk, cp):
            for m in range(2):
                t = pe(lambda e: e.transpose(bk.ap[:, 256 + 2 * m:258 + 2 * m], modrow[:, 128 * m:128 * m + 128],
                                             ident[0:2, 0:2]), cp)
            pv = bk.ap[:, 256:260].rearrange("p (m c) -> p m c", c=2)
            bb = bias[:, j:j + 2].unsqueeze(2).to_broadcast([128, 2, 2])
            bk.give(dve(lambda e: e.tensor_tensor(dst[:, j:j + 2, :], pv, bb, ALU.add), t))
            return t

        pend, tl = None, None
        for j in range(j0, j1, 2):
            s, wv, tok = wload(wcols(w, 128 * j, 256), 8, 256)
            bk, bf = pr.next()
            for k in range(8):
                last = pe(lambda e: e.matmul(bk.ap[0:2, 0:256], sc[:, b, k, :], wv[:, k, :], start=(k == 0),
                                             stop=(k == 7)), tok, sctok, bf)
            s.give(last)
            if pend is not None and len(banks) > 1:
                tl = turn(*pend)
            cp = act(lambda e: e.activation(modrow, bk.ap[0:2, 0:256], ACT.Copy), last, tl)
            pend = (j, bk, cp)
            yield
            if len(banks) == 1:
                tl = turn(*pend)
                pend = None
            for _ in range(gap):
                yield
        if pend is not None:
            turn(*pend)

    def ada(l, gap):
        return modulation(A["w_ada_2"][l], 1, 0, 24, col("b_ada_2", 24 * l, 24), adac[:, l, :, :], (7,), gap)

    XT = BR.get(8, TT)

    def load_xT(dst, src_list):
        st = Ring([Slot(R1.get(1024), lane=f"x{i}") for i in range(3)])
        pr = Ring([PSL[i] for i in range(4)])
        n = 0
        for src, t0 in src_list:
            for i in range(src.shape[0] // 128):
                s, free = st.next()
                tok = load(s.lane, s.ap, src[128 * i:128 * i + 128, :], free)
                rd = []
                for half in range(2):
                    b, bf = pr.next()
                    for k in range(4):
                        last = pe(lambda e, s=s, b=b, k=k, half=half: e.transpose(
                            b.ap[:, 128 * k:128 * k + 128],
                            s.ap[:, 512 * half + 128 * k:512 * half + 128 * k + 128], ident), tok, bf)
                    o = dst[:, 4 * half:4 * half + 4, t0 + 128 * i:t0 + 128 * i + 128]
                    bv = b.ap[:, :].rearrange("p (k t) -> p k t", k=4)
                    if n % 2:
                        ev = dve(lambda e, o=o, bv=bv: e.tensor_copy(o, bv), last)
                    else:
                        ev = act(lambda e, o=o, bv=bv: e.activation(o, bv, ACT.Copy), last)
                    n += 1
                    b.give(ev)
                    rd.append(last)
                s.give(*rd)

    load_xT(XT, [(A["x"][0], 0), (A["ctx"][0], 1024)])
    interleave([modulation(A["w_mod"][0], 0, 0, 16, col("b_mod", 0, 48), modc, (6, 7))])
    P.barrier()
    R1.reset()

    def norm_cols(g, gi, sc_x, sh_x, sc_c=None, sh_c=None):
        gc = col(g, gi, 8)
        dve(lambda e: e.scalar_tensor_tensor(nA[:, 0, :], sc_x, 1.0, gc, ALU.add, ALU.mult))
        dve(lambda e: e.tensor_copy(nB[:, 0, :], sh_x))
        if sc_c is not None:
            dve(lambda e: e.scalar_tensor_tensor(nA[:, 1, :], sc_c, 1.0, gc, ALU.add, ALU.mult))
            dve(lambda e: e.tensor_copy(nB[:, 1, :], sh_c))
        return P.q["dve"][-1]

    def rms(x, dst, blks, tmp, cols, g_only=None):
        sq = Ring([Slot(tmp.get(512)) for _ in range(3)])
        rs = [tmp.get(512) for _ in blks]
        pr = Ring([PSL[i] for i in range(3)])
        for (t0, n), r in zip(blks, rs):
            b, bf = pr.next()
            for k in range(8):
                s, sf = sq.next()
                q = act(lambda e, s=s, k=k: e.activation(s.ap[:, 0:n], x[:, k, t0:t0 + n], ACT.Square), sf)
                m = pe(lambda e, s=s, k=k, b=b: e.matmul(b.ap[:, 0:n], ones, s.ap[:, 0:n], start=(k == 0),
                                                        stop=(k == 7)), q, bf)
                s.give(m)
            v = dve(lambda e, r=r, b=b: e.tensor_scalar(r[:, 0:n], b.ap[:, 0:n], 1.0 / D, 1e-6, ALU.mult,
                                                       ALU.add), m)
            b.give(v)
        for (t0, n), r in zip(blks, rs):
            act(lambda e, r=r: e.activation(r[:, 0:n], r[:, 0:n], ACT.Ln), v)
        rr = [act(lambda e, r=r: e.activation(r[:, 0:n], r[:, 0:n], ACT.Exp, scale=-0.5))
              for (t0, n), r in zip(blks, rs)]
        for (t0, n), r, ra in zip(blks, rs, rr):
            w = 1 if t0 >= T else 0
            for k in range(8):
                sa = nA[:, w, k:k + 1] if g_only is None else g_only[:, k:k + 1]
                y = dve(lambda e, k=k, r=r, sa=sa: e.scalar_tensor_tensor(
                    dst[:, k, t0:t0 + n], x[:, k, t0:t0 + n], sa, r[:, 0:n], ALU.mult, ALU.mult), ra, cols)
                if g_only is None:
                    act(lambda e, k=k: e.activation(dst[:, k, t0:t0 + n], dst[:, k, t0:t0 + n], ACT.Identity,
                                                    bias=nB[:, w, k:k + 1]), y)

    def m6(i, k=0):
        return modc[:, 8 * i:8 * i + 8, k]

    hT = R1.get(8, TT)
    P.hT = hT
    c1 = norm_cols("norm1_g", 0, m6(1), m6(0), m6(1, 1), m6(0, 1))
    rms(XT, hT, BLKS, CAT, c1)
    P.barrier()
    CAT.reset()
    P.hT_live = True
    P.barrier()
    BR.reset()

    def load_hT(dst, blks=BLKS):
        P.hT = dst
        P.hx = [load(f"hsl{i}", dst[:, :, t0:t0 + n], hs[:, :, t0:t0 + n]) for i, (t0, n) in enumerate(blks)]

    def hx(t):
        return P.hx[min(t // 512, 2)] if P.hx else None

    P.hx = []

    def proj_cm(w, c0, ntile, sink, blks=BLKS, banks=(0, 1, 2, 3), pieces=None):
        pr = proj_cm.rings.setdefault(banks, Ring([PSL[i] for i in banks]))
        hv_ = P.hT
        for j in range(0, ntile, 2):
            nt = min(2, ntile - j)
            s, wv, tok = wload(wcols(w, c0 + 128 * j, 128 * nt), 8, 128 * nt)
            for m in range(nt):
                for (t0, n) in blks:
                    b, bf = pr.next()
                    for k in range(8):
                        last = pe(lambda e, m=m, k=k, b=b, wv=wv, t0=t0, n=n: e.matmul(
                            b.ap[:, 0:n], wv[:, k, 128 * m:128 * m + 128], hv_[:, k, t0:t0 + n],
                            start=(k == 0), stop=(k == 7)), tok, bf, hx(t0))
                    b.give(sink(j + m, t0, n, b.ap, last))
            s.give(last)
    proj_cm.rings = {}

    def proj_tm(w, c0, ncol, sink, tiles, banks=(4, 5, 6, 7)):
        hv_ = P.hT
        pr = Ring([PSL[i] for i in banks])
        for c in range(0, ncol, 256):
            nn = min(256, ncol - c)
            s, wv, tok = wload(wcols(w, c0 + c, nn), 8, nn)
            for t in tiles:
                b, bf = pr.next()
                for k in range(8):
                    last = pe(lambda e, k=k, b=b, wv=wv, t=t, nn=nn: e.matmul(
                        b.ap[:, 0:nn], hv_[:, k, 128 * t:128 * t + 128], wv[:, k, 0:nn],
                        start=(k == 0), stop=(k == 7)), tok, bf, hx(128 * t))
                b.give(sink(t, c, nn, b.ap, last))
            s.give(last)

    def rows_proj(w, groups, dst, banks=(4, 5)):
        hv_ = P.hT
        s, free = W.next()
        view = s.ap[:, 0:1024].rearrange("p (k n) -> p k n", k=8)
        zz = dve(lambda e: e.memset(view, 0.0), free)
        for q, (c0, n) in groups.items():
            tok = P.dma(s.lane, lambda e, q=q, c0=c0, n=n: e.dma_start(view[:, :, 32 * q:32 * q + n], wcols(w, c0, n)), zz)
        P.rows_tok = tok
        pr = Ring([PSL[i] for i in banks])
        for (t0, n) in BLKS:
            b, bf = pr.next()
            for k in range(8):
                last = pe(lambda e, k=k, b=b, t0=t0, n=n: e.matmul(
                    b.ap[:, 0:n], view[:, k, :], hv_[:, k, t0:t0 + n], start=(k == 0), stop=(k == 7)), tok, bf)
            ev = dve(lambda e, b=b, t0=t0, n=n: e.tensor_copy(dst[:, t0:t0 + n], b.ap[:, 0:n]), last)
            b.give(ev)
        s.give(last)
        return ev

    def softplus(y, t, e1, engine_out=None):
        a = act(lambda e: e.activation(t, y, ACT.Abs), P.q["dve"][-1])
        a = act(lambda e: e.activation(e1, t, ACT.Exp, scale=-1.0), a)
        a = act(lambda e: e.activation(e1, e1, ACT.Ln, bias=1.0))
        return dve(lambda e: e.scalar_tensor_tensor(y, y, 0.0, e1, ALU.max, ALU.add), a)

    def bc(c4, n):
        return c4.unsqueeze(2).to_broadcast([c4.shape[0], c4.shape[1], n])

    def h4(ap, n):
        return ap.rearrange("p (h x) -> p h x", x=n)

    def region(a, b):
        return Arena(big, a, b)

    OFF = {"hy": 0, "gla": 768, "gdn": 768 + 1184}

    def conv_channels(w, c0, ntile, taps, seg, wcol, bcol, zring, outs, fn=None, blks=BLKS, banks=(0, 1, 2, 3)):
        pad = taps // 2
        rows = T // seg
        wl = rows * (seg + 2 * pad)
        state = {}

        def sink(m, t0, n, b, tok):
            if t0 == 0:
                state["z"], state["zf"] = zring.next()
            zs, zf = state["z"], state["zf"]
            if t0 < T:
                zv = zs.ap[:, 0:wl].rearrange("p (r s) -> p r s", s=seg + 2 * pad)
                if seg <= 512:
                    r0 = t0 // seg
                    o = zv[:, r0:r0 + n // seg, pad:pad + seg]
                    src = b[:, 0:n].rearrange("p (r s) -> p r s", s=seg)
                else:
                    o, src = zs.ap[:, pad + t0:pad + t0 + n], b[:, 0:n]
            else:
                o, src = zs.ap[:, wl + pad:wl + pad + n], b[:, 0:n]
            ev = act(lambda e: e.activation(o, src, ACT.Copy), tok, zf)
            if t0 == blks[-1][0]:
                zlat = zs.ap[:, 0:wl].rearrange("p (r s) -> p r s", s=seg + 2 * pad)
                c_on = len(blks) == 3
                zctx = zs.ap[:, wl:wl + 2 * pad + TC] if c_on else None
                if "fin" in state:
                    state["fin"][0](*state["fin"][1])
                dst, waits, fin = outs(m)
                last = dve(lambda e: e.tensor_scalar(
                    dst[:, 0:T].rearrange("p (r s) -> p r s", s=seg), zlat[:, :, 0:seg], wcol(m, 0),
                    0.0 if bcol is None else bcol(m), ALU.mult, ALU.add), ev, waits)
                if c_on:
                    dve(lambda e: e.tensor_scalar(dst[:, T:TT], zctx[:, 0:TC], wcol(m, 0),
                                                  0.0 if bcol is None else bcol(m), ALU.mult, ALU.add))
                for tap in range(1, taps):
                    last = dve(lambda e, tap=tap: e.scalar_tensor_tensor(
                        dst[:, 0:T].rearrange("p (r s) -> p r s", s=seg), zlat[:, :, tap:tap + seg],
                        wcol(m, tap), dst[:, 0:T].rearrange("p (r s) -> p r s", s=seg), ALU.mult, ALU.add))
                    if c_on:
                        last = dve(lambda e, tap=tap: e.scalar_tensor_tensor(
                            dst[:, T:TT], zctx[:, tap:tap + TC], wcol(m, tap), dst[:, T:TT], ALU.mult, ALU.add))
                zs.give(last)
                if fn is not None:
                    nn = TT if c_on else T
                    last = act(lambda e: e.activation(dst[:, 0:nn], dst[:, 0:nn], fn), last)
                state["fin"] = (fin, (m, last))
            return ev

        proj_cm(w, c0, ntile, sink, blks=blks, banks=banks)
        state["fin"][0](*state["fin"][1])

    def tr4(pieces, dst, pr, after, parts=128, eng="act"):
        b, bf = pr.next()
        for i, p in enumerate(pieces):
            k = p.shape[0]
            m = p.shape[1]
            last = pe(lambda e, i=i, p=p, k=k, m=m: e.transpose(b.ap[0:m, 128 * i:128 * i + k], p, ident[0:k, 0:k]),
                      after, bf)
        return b, last

    def gdn():
        w = A["w_in"][0]
        c0 = OFF["gdn"]
        cat = CAT.t[:, M0 + 5 * T:M0 + 8 * T].rearrange("p (m t) -> p m t", m=3)
        C1 = region(M0, M0 + 8192)
        B1 = region(M0 + 8192, total - 10240)
        hreg = (total - 10240, total)
        gate, G = C1.get(8, 384), C1.get(TT)
        qT, kT = B1.get(4, TT, parts=96), B1.get(4, TT, parts=96)
        ktm, vtm = B1.get(10, 384), B1.get(10, 384)
        CX = region(CON.at, CON.hi)
        colg, ngc, kdE, egc = CX.get(10, 16), CX.get(10, 8), CX.get(10, 8), CX.get(10, 8)
        GL, eGL, par, ss = CX.get(8, 10), CX.get(8, 10), CX.get(4), CX.get(10, 4)
        s1, e1 = C1.t[:, C1.at:C1.at + TT], C1.t[:, C1.at + TT:C1.at + 2 * TT]
        rows_proj(w, {0: (c0 + 1536, 4), 1: (c0 + 1540, 4), 2: (c0 + 1544, 4), 3: (c0 + 1548, 4)}, G)
        z0 = dve(lambda e: e.memset(par, 0.0))
        for d in range(2):
            load("gpar", par[32 * d:32 * d + 4, 0:1], A["gdn_dt_bias"][0, d].rearrange("(a b) -> a b", b=1), z0)
            pl = load("gpar", par[32 * d:32 * d + 4, 1:2], A["gdn_a_log"][0, d].rearrange("(a b) -> a b", b=1), z0)
        x_sp = store_late("xs", xs, XT, pl, P.rows_tok)
        h_sp = store_late("hs", hs, hT)
        ea = act(lambda e: e.activation(par[:, 2:3], par[:, 1:2], ACT.Exp), pl)
        dve(lambda e: e.tensor_scalar(G, G, par[:, 0:1], sgn, ALU.add, ALU.mult), pl)
        softplus(G, s1, e1)
        dve(lambda e: e.tensor_scalar(G[0:64, :], G[0:64, :], par[0:64, 2:3], -1.0, ALU.mult, ALU.mult), ea)
        beta = act(lambda e: e.activation(G[64:128, :], G[64:128, :], ACT.Exp, scale=-1.0), P.q["dve"][-1])
        for d in range(2):
            src, ms, o = G[32 * d:32 * d + 32, :], rst[32 * d:32 * d + 32, d, :], s1[32 * d:32 * d + 32, :]
            if d:
                src, ms, o = src[:, ::-1], ms[:, ::-1], o[:, ::-1]
            dve(lambda e, src=src, ms=ms, o=o: e.tensor_tensor_scan(o, ms, src, 0.0, ALU.mult, ALU.add))
        gcr = dve(lambda e: e.tensor_copy(G[0:64, :], s1[0:64, :]), beta)
        P.fence["dve"] = P.fence["dve"] + [x_sp]

        def columns(pr):
            for c in range(10):
                b, bf = pr.next()
                t = pe(lambda e: e.transpose(b.ap[:, 0:128], G[:, 128 * c:128 * c + 128], ident), gcr, bf)
                src = b.ap[:, 0:128].rearrange("p (q r) -> p q r", q=4)[:, :, 0:4]
                b.give(dve(lambda e: e.tensor_copy(colg[:, c, :].rearrange("p (q r) -> p q r", q=4), src), t))
            b, bf = pr.next()
            for d in range(2):
                for h in range(4):
                    ends = G[:, (127 if d == 0 else 0):TT:128]
                    t = pe(lambda e: e.matmul(b.ap[:, (4 * d + h) * 16:(4 * d + h) * 16 + 10], sel[:, 4 * d + h, :],
                                              ends, start=True, stop=True), gcr, bf)
            b.give(dve(lambda e: e.tensor_copy(
                GL, b.ap[:, 0:128].rearrange("p (a b) -> p a b", a=8)[:, :, 0:10]), t))
            gc8 = colg[:, :, 0:8]
            dve(lambda e: e.tensor_scalar(ngc, gc8, -1.0, None, ALU.mult))
            a0 = dve(lambda e: e.tensor_tensor(kdE, ngc, GL.rearrange("p a b -> p b a"), ALU.add))
            act(lambda e: e.activation(kdE, kdE, ACT.Exp), a0)
            act(lambda e: e.activation(egc, gc8, ACT.Exp))
            act(lambda e: e.activation(eGL, GL, ACT.Exp))

        zw = 16 * 70 + 262
        zr = Ring([Slot(C1.get(zw)) for _ in range(2)])
        for s in zr.slots:
            zt = dve(lambda e, s=s: e.memset(s.ap, 0.0))
            s.free = [zt]
        cr = Ring([Slot(B1.get(TT))])
        pr = Ring([PSL[i] for i in (4, 5, 6, 7)])
        gw, gr = offs["gdn_conv_w"]

        def branch(base, dsttm):
            def outs(m):
                s, f = cr.next()

                def fin(m, tok):
                    ts = []
                    for t0 in (0, 4, 8):
                        k = min(4, 10 - t0)
                        b, last = tr4([s.ap[:, 128 * (t0 + i):128 * (t0 + i) + 128] for i in range(k)], None, pr, tok)
                        o = dsttm[:, t0:t0 + k, 128 * m:128 * m + 128]
                        ev = dve(lambda e, o=o, b=b, k=k: e.tensor_copy(
                            o, b.ap[:, 0:128 * k].rearrange("p (t c) -> p t c", t=k)), last)
                        b.give(ev)
                    s.give(last)
                return s.ap, f, fin

            conv_channels(w, c0 + 128 * base, 3, 7, 64, lambda m, tap: vec[gw][:, gr + tap * 9 + base + m:
                          gr + tap * 9 + base + m + 1], None, zr, outs, fn=ACT.Silu)

        def normalize(tm, dstT, scale):
            for t in range(10):
                dve(lambda e, t=t: e.tensor_tensor(nt, tm[:, t, :], tm[:, t, :], ALU.mult))
                dve(lambda e, t=t: e.tensor_reduce(ss[:, t, :], h4(nt, 96), AXX, ALU.add))
            a = dve(lambda e: e.tensor_scalar(ss, ss, 1e-6, None, ALU.add))
            act(lambda e: e.activation(ss, ss, ACT.Ln), a)
            a = act(lambda e: e.activation(ss, ss, ACT.Exp, scale=-0.5))
            if scale != 1.0:
                a = dve(lambda e: e.tensor_scalar(ss, ss, scale, None, ALU.mult), a)
            for t in range(10):
                n = dve(lambda e, t=t: e.tensor_tensor(h4(tm[:, t, :], 96), h4(tm[:, t, :], 96),
                                                       bc(ss[:, t, :], 96), ALU.mult), a)
                b, last = tr4([tm[:, t, 96 * h:96 * h + 96] for h in range(4)], None, pr, n)
                ev = act(lambda e, t=t, b=b: e.activation(
                    dstT[:, :, 128 * t:128 * t + 128], b.ap[0:96, :].rearrange("p (h t) -> p h t", h=4), ACT.Copy),
                    last)
                b.give(ev)
            return ev

        nt = C1.get(384)
        branch(0, vtm)
        columns(pr)
        P.barrier()
        normalize(vtm, qT, 96 ** -0.5)
        P.barrier()
        branch(3, ktm)
        P.barrier()
        normalize(ktm, kT, 1.0)
        branch(6, vtm)

        def gsink(t, c, n, b, tok):
            return act(lambda e: e.activation(gate[:, t, c:c + n], b[:, 0:n], ACT.Silu), tok)

        proj_tm(w, c0 + 1152, 384, gsink, range(8), banks=(0, 1, 2, 3))
        P.hT_live = False
        P.pending.append(h_sp)
        P.barrier()

        H1 = region(*hreg)
        C2 = region(C1.at - 384, M0 + 8192)
        C2.at = C2.lo = M0 + 3072 + TT
        lv = H1.get(2, 7, 128)
        lvt = load("gpar2", lv, A["c_lv"].rearrange("p (a b c) -> p a b c", a=2, b=7))
        oacc = H1.get(8, 384)
        odone = {}

        wsl = [W.slots[i] for i in range(4)]
        wfree = [f for s in wsl for f in s.take()]
        RW = region(ringm.lo, ringm.hi)
        order = ([8, 9] + list(range(8)), [9, 8] + list(range(7, -1, -1)))
        st = [0, 0]
        pstate = [None, None]
        Sd = []

        def scan(d, par_, ar):
            DT, LT, C = ar.get(512), ar.get(512), ar.get(512)
            X, XT_, M1 = ar.get(512), ar.get(512), ar.get(512)
            qe, vn = ar.get(512)[0:96, :], ar.get(384)
            S = Sd[d]
            pr = Ring([PSL[4 * d + 2 * par_ + i] for i in range(2)])
            tail = None
            for place in range(par_, 10, 2):
                c = order[d][place]
                lat = c < 8
                ts = slice(128 * c, 128 * c + 128)
                b, bf = pr.next()
                for h in range(4):
                    t = pe(lambda e, h=h, b=b: e.matmul(b.ap[:, 128 * h:128 * h + 128], sel[:, 4 * d + h, :], G[:, ts],
                                                       start=True, stop=True), bf)
                kb, kf = pr.next()
                for h in range(4):
                    tk = pe(lambda e, h=h, kb=kb: e.matmul(kb.ap[:, 128 * h:128 * h + 128], kT[:, h, ts], kT[:, h, ts],
                                                          start=True, stop=True), kf)
                yield
                for h in range(4):
                    last = dve(lambda e, h=h, b=b: e.scalar_tensor_tensor(
                        DT[:, 128 * h:128 * h + 128], b.ap[:, 128 * h:128 * h + 128],
                        ngc[:, c, 4 * d + h:4 * d + h + 1], mt[:, d, :], ALU.add, ALU.min), t, wfree)
                a1 = act(lambda e: e.activation(DT, DT, ACT.Exp), last)
                rel = [last]
                if lat:
                    a2 = act(lambda e, b=b: e.activation(qe, b.ap[0:96, :], ACT.Exp), tail)
                    qed = pool(lambda e: e.tensor_tensor(h4(qe, 128), h4(qe, 128), qT[:, :, ts], ALU.mult), a2)
                    rel.append(a2)
                b.give(*rel)
                yield
                for h in range(4):
                    last = dve(lambda e, h=h, kb=kb: e.scalar_tensor_tensor(
                        LT[:, 128 * h:128 * h + 128], kb.ap[:, 128 * h:128 * h + 128],
                        colg[:, c, 8 + 4 * d + h:8 + 4 * d + h + 1], DT[:, 128 * h:128 * h + 128], ALU.mult,
                        ALU.mult), tk, a1, tail)
                kb.give(last)
                mdone, ltok = tail, last
                for n in range(7):
                    s = 1 << n

                    def half(ap, k, s=s):
                        return ap.rearrange("p (n k s) -> p n k s", k=2, s=s)[:, :, k, :]

                    def part(ap, s=s):
                        return ap.rearrange("p (n s) -> p n s", s=s)

                    cm = pool(lambda e, n=n: e.tensor_tensor(
                        h4(C, 128), h4(LT, 128), lv[:, d, n, :].unsqueeze(1).to_broadcast([128, 4, 128]), ALU.mult),
                        ltok, lvt, mdone)
                    b, bf = pr.next()
                    for h in range(4):
                        sl = slice(128 * h, 128 * h + 128)
                        rhs = ident if n == 0 else X[:, sl]
                        t = pe(lambda e, b=b, sl=sl, rhs=rhs: e.matmul(b.ap[:, sl], C[:, sl], rhs, start=True,
                                                                       stop=True), cm, bf, last)
                    mdone = t
                    idb = ident.unsqueeze(1).to_broadcast([128, 4, 128])
                    if n == 0:
                        x1 = dve(lambda e, b=b: e.tensor_tensor(h4(X, 128), idb, h4(b.ap[:, :], 128), ALU.subtract), t)
                        last = dve(lambda e: e.tensor_tensor(h4(XT_, 128), idb, h4(C, 128), ALU.subtract))
                        mdone = last
                        b.give(x1)
                        yield
                        continue
                    m1 = act(lambda e, b=b: e.activation(M1, b.ap[:, :], ACT.Copy), t)
                    b.give(m1)
                    yield
                    b2, bf2 = pr.next()
                    for h in range(4):
                        sl = slice(128 * h, 128 * h + 128)
                        t2 = pe(lambda e, b2=b2, sl=sl, h=h: e.matmul(
                            part(b2.ap[:, 64 * h:64 * h + 64]), M1[:, sl], half(XT_[:, sl], 1 - d), start=True,
                            stop=True), m1, bf2)
                    if n < 6:
                        for h in range(4):
                            sl = slice(128 * h, 128 * h + 128)
                            t2 = pe(lambda e, b2=b2, sl=sl, h=h: e.matmul(
                                part(b2.ap[:, 256 + 64 * h:256 + 64 * h + 64]), XT_[:, sl], half(M1[:, sl], d),
                                start=True, stop=True))
                    last = dve(lambda e, b2=b2: e.tensor_tensor(
                        half(XT_, 1 - d), half(XT_, 1 - d), part(b2.ap[:, 0:256]), ALU.subtract), t2)
                    if n < 6:
                        last = dve(lambda e, b2=b2: e.tensor_tensor(
                            half(X, d), half(X, d), part(b2.ap[:, 256:512]), ALU.subtract))
                    b2.give(last)
                    yield
                ke, nw = M1[:, 0:384], LT[0:96, :]
                k1 = pool(lambda e: e.tensor_tensor(h4(ke, 96), h4(ktm[:, c, :], 96),
                                                    bc(egc[:, c, 4 * d:4 * d + 4], 96), ALU.mult), t2)
                b, bf = pr.next()
                for h in range(4):
                    t = pe(lambda e, b=b, h=h: e.matmul(b.ap[0:96, 128 * h:128 * h + 128], ke[:, 96 * h:96 * h + 96],
                                                       XT_[:, 128 * h:128 * h + 128], start=True, stop=True),
                           k1, last, bf)
                n1 = act(lambda e, b=b: e.activation(nw, b.ap[0:96, :], ACT.Copy, scale=-1.0), t)
                b.give(n1)
                if lat:
                    qb, qf = pr.next()
                    for h in range(4):
                        tq = pe(lambda e, qb=qb, h=h: e.matmul(qb.ap[:, 128 * h:128 * h + 128], kT[:, h, ts],
                                                              qT[:, h, ts], start=True, stop=True), qf)
                    at = dve(lambda e, qb=qb: e.tensor_tensor(C, qb.ap[:, :], DT, ALU.mult), tq)
                    qb.give(at)
                kd = X[:, 0:384]
                kdt = pool(lambda e: e.tensor_tensor(h4(kd, 96), h4(ktm[:, c, :], 96),
                                                     bc(kdE[:, c, 4 * d:4 * d + 4], 96), ALU.mult), mdone)
                yield
                while st[d] < place:
                    yield
                b, bf = pr.next()
                for h in range(4):
                    pe(lambda e, b=b, h=h: e.matmul(b.ap[:, 96 * h:96 * h + 96], XT_[:, 128 * h:128 * h + 128],
                                                    vtm[:, c, 96 * h:96 * h + 96], start=True, stop=False), bf, n1)
                    t = pe(lambda e, b=b, h=h: e.matmul(b.ap[:, 96 * h:96 * h + 96], nw[:, 128 * h:128 * h + 128],
                                                       S[:, 96 * h:96 * h + 96], start=False, stop=True),
                           n1, pstate[d])
                v1 = dve(lambda e, b=b: e.tensor_tensor(h4(vn, 96), h4(b.ap[:, 0:384], 96),
                                                        bc(colg[:, c, 8 + 4 * d:12 + 4 * d], 96), ALU.mult), t)
                b.give(v1)
                yield
                b, bf = pr.next()
                for h in range(4):
                    ts_ = pe(lambda e, b=b, h=h: e.matmul(b.ap[0:96, 96 * h:96 * h + 96], kd[:, 96 * h:96 * h + 96],
                                                         vn[:, 96 * h:96 * h + 96], start=True, stop=True), v1, kdt,
                             bf)
                tail = ts_
                if lat:
                    ob, of = pr.next()
                    for h in range(4):
                        pe(lambda e, ob=ob, h=h: e.matmul(ob.ap[:, 96 * h:96 * h + 96], C[:, 128 * h:128 * h + 128],
                                                          vn[:, 96 * h:96 * h + 96], start=True, stop=False), at, of)
                        to = pe(lambda e, ob=ob, h=h: e.matmul(
                            ob.ap[:, 96 * h:96 * h + 96], qe[:, 128 * h:128 * h + 128], S[:, 96 * h:96 * h + 96],
                            start=False, stop=True), qed)
                    tail = to
                    if c not in odone:
                        o1 = act(lambda e, ob=ob: e.activation(oacc[:, c, :], ob.ap[:, 0:384], ACT.Copy), to)
                        odone[c] = o1
                    else:
                        o1 = dve(lambda e, ob=ob: e.tensor_tensor(oacc[:, c, :], oacc[:, c, :], ob.ap[:, 0:384],
                                                                  ALU.add), to, odone[c])
                    ob.give(o1)
                dve(lambda e: e.tensor_tensor(h4(S, 96), h4(S, 96), bc(eGL[0:96, 4 * d:4 * d + 4, c], 96), ALU.mult),
                    tail)
                s1_ = dve(lambda e, b=b: e.tensor_tensor(S, S, b.ap[0:96, 0:384], ALU.add), ts_)
                b.give(s1_)
                pstate[d] = s1_
                st[d] = place + 1
                yield

        for d in range(2):
            Sd.append(C2.get(384)[0:96, :])
            pstate[d] = dve(lambda e: e.memset(Sd[d], 0.0))

        def late(g, k):
            for _ in range(k):
                yield
            for _ in g:
                yield

        g4 = [scan(d, q, ScanAr([RW, H1, C2, B1])) for q in range(2) for d in range(2)]
        interleave(g4[0:2] + [late(g, 9) for g in g4[2:4]])
        for s in wsl:
            s.give(*(P.q[e][-1] for e in ("pe", "act", "dve", "pool")))
        P.barrier()
        head_out(oacc, gate, "gdn_norm_g", 4, 96, cat, region(H1.lo + 1792 + 3072, H1.hi), CX)

    class ScanAr:
        def __init__(self, ars):
            self.ars = ars

        def get(self, n):
            for a in self.ars:
                if a.at + n <= a.hi:
                    return a.get(n)
            raise AssertionError("no room")

    def head_out(oacc, gate, gname, nh, dv, cat, ar, CX):
        nn = nh * dv
        gb = ar.get(dv)
        gl = load("gb", gb, A[gname][0].partition_broadcast(128))
        sq = ar.get(nn)
        s8 = CX.get(8, nh)
        for t in range(8):
            dve(lambda e, t=t: e.tensor_tensor(sq, oacc[:, t, :], oacc[:, t, :], ALU.mult))
            dve(lambda e, t=t: e.tensor_reduce(s8[:, t, :], h4(sq, dv), AXX, ALU.add))
        a = dve(lambda e: e.tensor_scalar(s8, s8, 1.0 / dv, 1e-6, ALU.mult, ALU.add))
        act(lambda e: e.activation(s8, s8, ACT.Ln), a)
        a = act(lambda e: e.activation(s8, s8, ACT.Exp, scale=-0.5))
        pr = Ring([PSL[i] for i in range(4)])
        for t in range(8):
            dve(lambda e, t=t: e.tensor_tensor(h4(oacc[:, t, :], dv), h4(oacc[:, t, :], dv), bc(s8[:, t, :], dv),
                                               ALU.mult), a)
            dve(lambda e, t=t: e.tensor_tensor(h4(oacc[:, t, :], dv), h4(oacc[:, t, :], dv),
                                               gb.unsqueeze(1).to_broadcast([128, nh, dv]), ALU.mult), gl)
            n = dve(lambda e, t=t: e.tensor_tensor(oacc[:, t, :], oacc[:, t, :], gate[:, t, :], ALU.mult))
            b, last = tr4([oacc[:, t, 128 * i:128 * i + 128] for i in range(nn // 128)], None, pr, n)
            ev = act(lambda e, t=t, b=b: e.activation(
                cat[:, :, 128 * t:128 * t + 128], b.ap[:, 0:nn].rearrange("p (m t) -> p m t", t=128), ACT.Copy), last)
            b.give(ev)
        P.barrier()

    def gla():
        w = A["w_in"][0]
        c0 = OFF["gla"]
        cat = CAT.t[:, M0 + 2 * T:M0 + 5 * T].rearrange("p (m t) -> p m t", m=3)
        C1 = region(M0, M0 + 5 * T)
        B1 = region(M0 + 8192, total - 10240)
        H1 = region(total - 10240, total)
        CX = region(CON.at, CON.hi)
        gate = B1.get(8, 384)
        qT, kT = B1.get(4, TT, parts=48), B1.get(4, TT, parts=48)
        vtm = B1.get(10, 384)
        aT = [B1.get(TT, parts=16), B1.get(TT, parts=16)]
        wa = C1.get(2, 192, parts=16)
        nba = CX.get(2, 4)[0:48, :, :]
        pl = load("gl1", wa, A["gla_w_a2"][0].rearrange("d r n -> r d n"))
        for d in range(2):
            for h in range(4):
                pl = load("gl1", nba[:, d, h:h + 1],
                          A["gla_b_a"][0, d, 48 * h:48 * h + 48].rearrange("(a b) -> a b", b=1))
        load_hT(hT)
        pr = Ring([PSL[i] for i in range(4)])

        def headed(c, m, nh, step, dst):
            hv_ = P.hT
            s, free = W.next()
            view = s.ap[:, 0:8 * nh * step].rearrange("p (k n) -> p k n", k=8)
            for g in range(nh):
                tok = P.dma(s.lane, lambda e: e.dma_start(view[:, :, step * g:step * g + step],
                                                          wcols(w, c + m * g, step)), free)
            per = min(128 // step, nh)
            for g0 in range(0, nh, per):
                for (t0, n) in BLKS:
                    b, bf = pr.next()
                    for k in range(8):
                        last = pe(lambda e: e.matmul(b.ap[0:per * step, 0:n],
                                                     view[:, k, step * g0:step * (g0 + per)],
                                                     hv_[:, k, t0:t0 + n], start=(k == 0), stop=(k == 7)), tok, bf,
                                  hx(t0))
                    for i in range(per):
                        o = dst(g0 + i, t0, n)
                        ev = act(lambda e: e.activation(o, b.ap[step * i:step * i + m, 0:n], ACT.Copy), last)
                    b.give(ev)
            s.give(last)

        headed(c0, 48, 4, 64, lambda g, t0, n: qT[:, g, t0:t0 + n])
        headed(c0 + 192, 48, 4, 64, lambda g, t0, n: kT[:, g, t0:t0 + n])
        headed(c0 + 1152, 16, 2, 32, lambda g, t0, n: aT[g][:, t0:t0 + n])

        def vsink(t, c, n, b, tok):
            return dve(lambda e: e.tensor_copy(vtm[:, t, c:c + n], b[:, 0:n]), tok)

        proj_tm(w, c0 + 384, 384, vsink, range(10))

        def gsink(t, c, n, b, tok):
            return act(lambda e: e.activation(gate[:, t, c:c + n], b[:, 0:n], ACT.Silu), tok)

        proj_tm(w, c0 + 768, 384, gsink, range(8))
        P.barrier()
        P.hT_live = False
        oacc = H1.get(8, 384)
        pm = H1.get(2, 512)
        H1.get(768)
        pmt = load("gl2", pm, A["c_pm"].bitcast(F32).rearrange("p (d x) -> p d x", d=2))
        odone = {}
        rem = ScanAr([H1, B1, C1])

        def scan(d):
            g48 = lambda: rem.get(512)[0:48, :]
            la, bb, e1, e2, qs, kd = g48(), g48(), g48(), g48(), g48(), g48()
            qd, kk = g48(), g48()
            At = rem.get(512)
            kdt, dec, S = CX.get(192), CX.get(4)[0:48, :], CXS(CX, d)[0:48, :]
            pr = Ring([PSL[4 * d + i] for i in range(3)])
            dve(lambda e: e.memset(At, 0.0))
            st = dve(lambda e: e.memset(S, 0.0))
            order = [8, 9] + list(range(8)) if d == 0 else [9, 8] + list(range(7, -1, -1))
            fin_pe = None

            def gate_in(c):
                b, bf = pr.next()
                for h in range(4):
                    t = pe(lambda e: e.matmul(b.ap[0:48, 128 * h:128 * h + 128], wa[:, d, 48 * h:48 * h + 48],
                                              aT[d][:, 128 * c:128 * c + 128], start=True, stop=True), bf, pl)
                y = dve(lambda e: e.tensor_tensor(h4(la, 128), h4(b.ap[0:48, :], 128),
                                                  bc(nba[:, d, :], 128), ALU.add), t, pl)
                b.give(y)
                return y

            def exp_in(y):
                act(lambda e: e.activation(e1, la, ACT.Abs), y)
                act(lambda e: e.activation(e1, e1, ACT.Exp, scale=-1.0))

            exp_in(gate_in(order[0]))
            yield
            ln = act(lambda e: e.activation(e1, e1, ACT.Ln, bias=1.0))
            yield
            for place, c in enumerate(order):
                lat = c < 8
                ts = slice(128 * c, 128 * c + 128)
                dve(lambda e: e.scalar_tensor_tensor(la, la, 0.0, e1, ALU.min, ALU.subtract), ln)
                dve(lambda e: e.tensor_scalar(la, la, 1.0 / 16.0, None, ALU.mult))
                ms = rst[0:48, d, 0:512]
                if d == 0:
                    dve(lambda e: e.tensor_tensor_scan(bb, ms, la, 0.0, ALU.mult, ALU.add))
                else:
                    dve(lambda e: e.tensor_tensor_scan(bb[:, ::-1], ms[:, ::-1], la[:, ::-1], 0.0, ALU.mult, ALU.add))
                b4 = h4(bb, 128)
                end = 127 if d == 0 else 0
                f1 = dve(lambda e: e.tensor_tensor(h4(e2, 128), b4[:, :, end:end + 1].to_broadcast([48, 4, 128]), b4,
                                                  ALU.subtract), fin_pe)
                a2 = act(lambda e: e.activation(e2, e2, ACT.Exp), f1)
                eL = act(lambda e: e.activation(dec, b4[:, :, end], ACT.Exp), f1)
                yn = gate_in(order[place + 1]) if place < 9 else None
                kdd = pool(lambda e: e.tensor_tensor(h4(kd, 128), h4(e2, 128), kT[:, :, ts], ALU.mult), a2,
                           fin_pe)
                yield
                kb, kf = pr.next()
                for h in range(4):
                    tk = pe(lambda e, h=h: e.transpose(kb.ap[:, 48 * h:48 * h + 48], kd[:, 128 * h:128 * h + 128],
                                                      ident[0:48, 0:48]), kdd, kf)
                if yn is not None:
                    exp_in(yn)
                kt1 = act(lambda e: e.activation(kdt, kb.ap[:, 0:192], ACT.Copy), tk)
                kb.give(kt1)
                sb_, sf = pr.next()
                for h in range(4):
                    tsn = pe(lambda e, h=h: e.matmul(sb_.ap[0:48, 96 * h:96 * h + 96], kdt[:, 48 * h:48 * h + 48],
                                                     vtm[:, c, 96 * h:96 * h + 96], start=True, stop=True), kt1, sf)
                if lat:
                    a3 = act(lambda e: e.activation(qs, bb, ACT.Exp))
                    q1 = pool(lambda e: e.tensor_tensor(h4(qs, 128), h4(qs, 128), qT[:, :, ts], ALU.mult), a3)
                    b5 = bb.rearrange("p (h f x) -> p (h f) x", h=4, f=2)
                    mid = b5[:, :, 31:32].to_broadcast([48, 8, 64])
                    dve(lambda e: e.tensor_tensor(qd.rearrange("p (g x) -> p g x", g=8), b5, mid, ALU.subtract),
                        fin_pe)
                    f2 = dve(lambda e: e.tensor_scalar(qd, qd, 80.0, -80.0, ALU.min, ALU.max))
                    act(lambda e: e.activation(kk, qd, ACT.Exp, scale=-1.0), f2)
                    a4 = act(lambda e: e.activation(qd, qd, ACT.Exp))
                    pool(lambda e: e.tensor_tensor(h4(kk, 128), h4(kk, 128), kT[:, :, ts], ALU.mult), a4)
                    q2 = pool(lambda e: e.tensor_tensor(h4(qd, 128), h4(qd, 128), qT[:, :, ts], ALU.mult), a4)
                    yield
                    ab, af = pr.next()
                    for h in range(4):
                        t1 = pe(lambda e, h=h: e.matmul(ab.ap[:, 128 * h:128 * h + 128], kk[:, 128 * h:128 * h + 128],
                                                       qd[:, 128 * h:128 * h + 128], start=True, stop=True), q2, af)
                    r = 63 if d == 0 else 64
                    qh = slice(64, 128) if d == 0 else slice(0, 64)
                    kh = slice(0, 64) if d == 0 else slice(64, 128)
                    ref = b4[:, :, r:r + 1].to_broadcast([48, 4, 64])
                    q4, k4 = h4(qd, 128), h4(kk, 128)
                    dve(lambda e: e.tensor_tensor(q4[:, :, qh], b4[:, :, qh], ref, ALU.subtract), t1)
                    f3 = dve(lambda e: e.tensor_tensor(k4[:, :, kh], ref, b4[:, :, kh], ALU.subtract))
                    act(lambda e: e.activation(q4[:, :, qh], q4[:, :, qh], ACT.Exp), f3)
                    a5 = act(lambda e: e.activation(k4[:, :, kh], k4[:, :, kh], ACT.Exp))
                    pool(lambda e: e.tensor_tensor(q4[:, :, qh], q4[:, :, qh],
                                                   qT[:, :, 128 * c + qh.start:128 * c + qh.stop], ALU.mult), a5)
                    q3 = pool(lambda e: e.tensor_tensor(k4[:, :, kh], k4[:, :, kh],
                                                        kT[:, :, 128 * c + kh.start:128 * c + kh.stop], ALU.mult))
                    yield
                    for h in range(4):
                        o = ab.ap[kh, 128 * h + qh.start:128 * h + qh.stop]
                        t2 = pe(lambda e, h=h, o=o: e.matmul(o, k4[:, h, kh], q4[:, h, qh], start=True, stop=True),
                                q3)
                    pmi = pm[:, d, :].bitcast(I32)
                    cp = dve(lambda e: e.copy_predicated(At, pmi, ab.ap[:, :]), t2, pmt, fin_pe)
                    ab.give(cp)
                    ob, of = pr.next()
                    for h in range(4):
                        pe(lambda e, h=h: e.matmul(ob.ap[:, 96 * h:96 * h + 96], At[:, 128 * h:128 * h + 128],
                                                   vtm[:, c, 96 * h:96 * h + 96], start=True, stop=False), cp, of)
                        to = pe(lambda e, h=h: e.matmul(ob.ap[:, 96 * h:96 * h + 96], qs[:, 128 * h:128 * h + 128],
                                                       S[:, 96 * h:96 * h + 96], start=False, stop=True), q1, st)
                    if c not in odone:
                        o1 = act(lambda e: e.activation(oacc[:, c, :], ob.ap[:, 0:384], ACT.Copy,
                                                        scale=48 ** -0.5), to)
                        odone[c] = o1
                    else:
                        o1 = dve(lambda e: e.scalar_tensor_tensor(oacc[:, c, :], ob.ap[:, 0:384], 48 ** -0.5,
                                                                  oacc[:, c, :], ALU.mult, ALU.add), to, odone[c])
                    ob.give(o1)
                fin_pe = P.q["pe"][-1]
                dve(lambda e: e.tensor_tensor(h4(S, 96), h4(S, 96), bc(dec, 96), ALU.mult), fin_pe, eL)
                st = dve(lambda e: e.tensor_tensor(S, S, sb_.ap[0:48, 0:384], ALU.add), tsn)
                sb_.give(st)
                if yn is not None:
                    ln = act(lambda e: e.activation(e1, e1, ACT.Ln, bias=1.0))
                yield

        def vectors():
            yield from modulation(A["w_mod"][0], 0, 16, 48, col("b_mod", 0, 48), modc, (3,), 1)
            yield from ada(0, 1)

        interleave([scan(0), vectors(), scan(1)])
        P.barrier()
        head_out(oacc, gate, "gla_norm_g", 4, 96, cat, region(H1.lo + 3072, H1.hi), CX)

    def CXS(CX, d):
        return big[:, total - 10240 + 3072 + 1024 + 384 * d:total - 10240 + 3072 + 1024 + 384 * (d + 1)]

    def hyena():
        w = A["w_in"][0]
        cat = CAT.t[:, M0:M0 + 2 * T].rearrange("p (m t) -> p m t", m=2)
        B1 = region(M0 + 8192, total - 10240)
        H1 = region(total - 10240, total)
        load_hT(hT, BLKS[0:2])
        u = B1.get(8, 768)
        mark = B1.at
        zr = Ring([Slot(B1.get(16 * 66)) for _ in range(2)])
        for s in zr.slots:
            s.free = [dve(lambda e, s=s: e.memset(s.ap, 0.0))]
        cr = Ring([Slot(B1.get(T)) for _ in range(2)])
        pr = Ring([PSL[i] for i in (4, 5, 6, 7)])
        hw, hr = offs["hy_conv_w"]

        def outs(m):
            s, f = cr.next()

            def fin(m, tok):
                sv = s.ap.rearrange("p (t two) -> p two t", two=2)
                for par in range(2):
                    b, last = tr4([sv[:, par, 128 * i:128 * i + 128] for i in range(4)], None, pr, tok)
                    ev = act(lambda e, b=b, par=par: e.activation(
                        u[:, 4 * par:4 * par + 4, 128 * m:128 * m + 128],
                        b.ap[:, :].rearrange("p (t c) -> p t c", t=4), ACT.Copy), last)
                    b.give(ev)
                s.give(last)
            return s.ap, f, fin

        conv_channels(w, 0, 6, 3, 64, lambda m, tap: vec[hw][:, hr + tap * 6 + m:hr + tap * 6 + m + 1],
                      lambda m: col("hy_conv_b", m, 1), zr, outs, fn=None, blks=BLKS[0:2])
        P.barrier()
        P.hT_live = False
        B1.at = mark
        CX = region(CON.at, CON.hi)
        hm = H1.at
        zc = H1.get(T)[0:33, :]
        fw1, fw2 = H1.get(64)[0:33, :], H1.get(64)[0:64, :]
        fw3 = H1.get(1024)[0:64, :]
        h1, rr, kf = H1.get(T)[0:64, :], H1.get(T)[0:64, :], H1.get(T)[0:64, :]
        fp = CX.get(8)[0:64, :]
        for dst, src in ((zc, A["c_z"]), (fw1, A["hy_f_w1"][0]), (fw2, A["hy_f_w2"][0]), (fw3, A["hy_f_w3"][0]),
                         (fp[:, 0:1], A["hy_f_b1"][0].rearrange("(a b) -> a b", b=1)),
                         (fp[:, 1:2], A["hy_f_b2"][0].rearrange("(a b) -> a b", b=1)),
                         (fp[:, 2:3], A["hy_sin_freq"][0, 0].rearrange("(a b) -> a b", b=1)),
                         (fp[:, 3:4], A["hy_sin_freq"][0, 1].rearrange("(a b) -> a b", b=1))):
            ld = load("hyl", dst, src)
        MAGIC = 12582912.0
        C1_, C2_ = 6.28125, 2 * math.pi - 6.28125
        prev = ld
        for n, (wt, inp) in enumerate(((fw1, zc), (fw2, h1))):
            evs = []
            for i in range(2):
                t = pe(lambda e, i=i: e.matmul(psum[i][0:64, :], wt, inp[:, 512 * i:512 * i + 512], start=True,
                                               stop=True), prev, ld)
                evs.append(dve(lambda e, i=i: e.tensor_scalar(rr[:, 512 * i:512 * i + 512], psum[i][0:64, :],
                                                             fp[:, n:n + 1], fp[:, 2 + n:3 + n], ALU.add, ALU.mult),
                               t))
            dve(lambda e: e.tensor_scalar(kf, rr, 1.0 / (2 * math.pi), MAGIC, ALU.mult, ALU.add))
            dve(lambda e: e.tensor_scalar(kf, kf, MAGIC, None, ALU.subtract))
            dve(lambda e: e.scalar_tensor_tensor(rr, kf, -C1_, rr, ALU.mult, ALU.add))
            dve(lambda e: e.scalar_tensor_tensor(rr, kf, -C2_, rr, ALU.mult, ALU.add))
            a = dve(lambda e: e.tensor_scalar(rr, rr, 3.1415925, -3.1415925, ALU.min, ALU.max))
            prev = act(lambda e: e.activation(h1, rr, ACT.Sin), a)
        dec = Ring([Slot(H1.get(256), lane=f"dec{i}") for i in range(2)])
        R2 = H1.at
        fr = Ring([Slot(B1.get(1024)) for _ in range(2)])
        hsm = B1.get(8, 512)
        hdf_ = B1.get(8, 512)
        pr = Ring([PSL[i] for i in range(2, 8)])
        hv = h1.rearrange("p (t two) -> p two t", two=2)
        for tt_ in range(8):
            par, i = tt_ // 4, tt_ % 4
            s, sf = dec.next()
            dl = load(s.lane, s.ap, A["c_dec"][128 * tt_:128 * tt_ + 128, :], sf)
            f, ff = fr.next()
            for half in range(2):
                b, bf = pr.next()
                t = pe(lambda e, half=half: e.matmul(b.ap[:, :], hv[:, par, 128 * i:128 * i + 128],
                                                     fw3[:, 512 * half:512 * half + 512], start=True, stop=True),
                       prev, bf)
                ev = dve(lambda e, half=half: e.tensor_tensor(
                    f.ap[:, 512 * half:512 * half + 512].rearrange("p (a c) -> p a c", a=2),
                    b.ap[:, :].rearrange("p (a c) -> p a c", a=2), s.ap.unsqueeze(1).to_broadcast([128, 2, 256]),
                    ALU.mult), t, dl, ff)
                b.give(ev)
            s.give(ev)
            fv = f.ap.rearrange("p (o d c) -> p o d c", o=2, d=2)
            if tt_ == 0:
                dve(lambda e: e.memset(fv[0:1, :, 1, :], 0.0))
            o1 = hsm[:, tt_, :].rearrange("p (o c) -> p o c", o=2)
            o2 = hdf_[:, tt_, :].rearrange("p (o c) -> p o c", o=2)
            dve(lambda e: e.tensor_tensor(o1, fv[:, :, 0, :], fv[:, :, 1, :], ALU.add))
            last = dve(lambda e: e.tensor_tensor(o2, fv[:, :, 0, :], fv[:, :, 1, :], ALU.subtract))
            f.give(last)
        fdone = last

        def mat(name, n):
            return wload(A[name][n].rearrange("(k p) n -> p k n", p=128), 4, 512)

        def dft(src_c, src_s, ncol, dst, ready, banks):
            for k_ in range(2):
                src = src_c if k_ == 0 else src_s
                re, rep = (dst[0], dst[2]) if k_ == 0 else (dst[1], dst[3])
                slE, vE, tE = mat("c_dft", k_)
                slO, vO, tO = mat("c_dft", 2 + k_)
                pe_last = None
                for k in range(4):
                    be, bef = banks.next()
                    bo, bof = banks.next()
                    for half, (b, bf, v, tk) in enumerate(((be, bef, vE, tE), (bo, bof, vO, tO))):
                        for t in range(4):
                            last = pe(lambda e, b=b, v=v, t=t, half=half: e.matmul(
                                b.ap[:, 0:ncol], v[:, t, 128 * k:128 * k + 128], src[:, 4 * half + t, :],
                                start=(t == 0), stop=(t == 3)), tk, bf, ready)
                    e1 = act(lambda e: e.activation(re[:, k, :], be.ap[:, 0:ncol], ACT.Copy), last)
                    be.give(e1)
                    d2 = dve(lambda e: e.tensor_tensor(rep[:, k, :], re[:, k, :], bo.ap[:, 0:ncol], ALU.subtract), e1,
                             last)
                    d1 = dve(lambda e: e.tensor_tensor(re[:, k, :], re[:, k, :], bo.ap[:, 0:ncol], ALU.add))
                    bo.give(d1)
                slE.give(last)
                slO.give(last)
            return dve(lambda e: e.tensor_scalar(dst[1], dst[1], -1.0, None, ALU.mult))

        banks = Ring([PSL[i] for i in range(8)])
        P.barrier()
        H1.at = hm
        HF = [H1.get(4, 512) for _ in range(4)]
        fh = dft(hsm, hdf_, 512, HF, fdone, banks)
        P.barrier()
        B1.at = mark
        Y = [B1.get(4, 256) for _ in range(4)]
        Z = [B1.get(4, 256) for _ in range(4)]
        tmp, tmp2 = H1.get(1024).rearrange("p (a b) -> p a b", a=4), H1.get(1024).rearrange("p (a b) -> p a b", a=4)
        dsk = B1.get(2, 256)
        dl = load("hyl", dsk, A["hy_d"][0].partition_broadcast(128))
        y = u[:, :, 0:256]
        ready = None
        for o in range(2):
            ready = dft(y, y, 256, Y, ready, banks)
            H = [x[:, :, 256 * o:256 * o + 256] for x in HF]
            for q in range(2):
                ar, ai, hr_, hi = Y[2 * q], Y[2 * q + 1], H[2 * q], H[2 * q + 1]
                zr_, zi = Z[2 * q], Z[2 * q + 1]
                dve(lambda e: e.tensor_tensor(zr_, ar, hr_, ALU.mult), ready)
                p1 = pool(lambda e: e.tensor_tensor(tmp, ai, hi, ALU.mult), ready, P.q["dve"][-2])
                dve(lambda e: e.tensor_tensor(zi, ar, hi, ALU.mult))
                p2 = pool(lambda e: e.tensor_tensor(tmp2, ai, hr_, ALU.mult))
                dve(lambda e: e.tensor_tensor(zr_, zr_, tmp, ALU.subtract), p1)
                dve(lambda e: e.tensor_tensor(zi, zi, tmp2, ALU.add), p2)
            dve(lambda e: e.tensor_tensor(Y[0], Z[0], Z[2], ALU.add))
            dve(lambda e: e.tensor_tensor(Y[1], Z[3], Z[1], ALU.subtract))
            dve(lambda e: e.tensor_tensor(Y[2], Z[0], Z[2], ALU.subtract))
            dve(lambda e: e.tensor_tensor(Y[3], Z[1], Z[3], ALU.add))
            rdy = dve(lambda e: e.tensor_scalar(Y[3], Y[3], -1.0, None, ALU.mult))
            gate = u[:, :, 256 * (o + 1):256 * (o + 2)]
            for par in range(2):
                slc, vc, tc = mat("c_idft", 2 * par)
                sls, vs, ts_ = mat("c_idft", 2 * par + 1)
                for i in range(4):
                    b, bf = banks.next()
                    for v, yy, tk in ((vc, Y[2 * par], tc), (vs, Y[2 * par + 1], ts_)):
                        for k in range(4):
                            last = pe(lambda e, v=v, yy=yy, k=k: e.matmul(
                                b.ap[:, 0:256], v[:, k, 128 * i:128 * i + 128], yy[:, k, :],
                                start=(v is vc and k == 0), stop=(v is vs and k == 3)), tk, bf, rdy)
                    tt_ = 4 * par + i
                    yv = y[:, tt_, :]
                    t_ = tmp[:, 0, :]
                    dve(lambda e: e.tensor_tensor(t_, yv, dsk[:, o, :], ALU.mult), dl)
                    dve(lambda e: e.tensor_tensor(t_, t_, b.ap[:, 0:256], ALU.add), last)
                    b.give(P.q["dve"][-1])
                    ready = dve(lambda e: e.tensor_tensor(y[:, tt_, :], t_, gate[:, tt_, :], ALU.mult))
                slc.give(last)
                sls.give(last)
        for m in range(2):
            cv = cat[:, m, :].rearrange("p (t two) -> p two t", two=2)
            for par in range(2):
                b, last = tr4([y[:, 4 * par + i, 128 * m:128 * m + 128] for i in range(4)], None, banks, ready)
                ev = act(lambda e: e.activation(cv[:, par, :], b.ap[:, :], ACT.Copy), last)
                b.give(ev)
        P.barrier()

    def out_proj(w, XT, cat, gates, blks):
        pr = Ring(PSL)
        for j in range(0, 8, 2):
            s, wv, tok = wload(wcols(w, 128 * j, 256), 8, 256)
            for m in range(2):
                for bi, (t0, n) in enumerate(blks):
                    b, bf = pr.next()
                    for k in range(8):
                        last = pe(lambda e: e.matmul(b.ap[:, 0:n], wv[:, k, 128 * m:128 * m + 128],
                                                     cat[:, k, t0:t0 + n], start=(k == 0), stop=(k == 7)), tok, bf)
                    g = gates[1 if t0 >= T else 0][:, j + m:j + m + 1]
                    x = XT[:, j + m, t0:t0 + n]
                    ev = dve(lambda e: e.scalar_tensor_tensor(x, b.ap[:, 0:n], g, x, ALU.mult, ALU.add), last)
                    b.give(ev)
            s.give(last)
        P.barrier()

    def restore_xT():
        BR.reset()
        x = BR.get(8, TT)
        it = load("xsl", x, xs)
        P.fence["dve"] = P.fence["dve"] + [it]
        P.fence["act"] = P.fence["act"] + [it]
        return x

    def mlp(XT):
        gcol = m6(5)
        hr = Ring([Slot(CAT.t[:, M0 + 4096 * i:M0 + 4096 * i + 4096].rearrange("p (a b) -> p a b", a=4))
                   for i in range(2)])
        pr = Ring(PSL)
        w1, w2 = A["w_mlp1"][0], A["w_mlp2"][0]
        hv_ = P.hT
        held = []

        def second(g, s, done):
            w2v = w2.rearrange("(k p) n -> p k n", p=128)
            for half in range(2):
                ws, wv, tok = wload(w2v[:, 4 * g:4 * g + 4, 512 * half:512 * half + 512], 4, 512)
                for m in range(4):
                    for (t0, n) in BLKS[0:2]:
                        b, bf = pr.next()
                        for k in range(4):
                            last = pe(lambda e: e.matmul(b.ap[:, :], wv[:, k, 128 * m:128 * m + 128],
                                                         s.ap[:, k, t0:t0 + n], start=(k == 0), stop=(k == 3)), tok,
                                      bf, done)
                        x = XT[:, 4 * half + m, t0:t0 + n]
                        g_ = gcol[:, 4 * half + m:4 * half + m + 1]
                        ev = dve(lambda e: e.scalar_tensor_tensor(x, b.ap[:, :], g_, x, ALU.mult, ALU.add), last)
                        b.give(ev)
                ws.give(last)
            s.give(last)

        for g in range(8):
            s, sf = hr.next()
            for half in range(2):
                ws, wv, tok = wload(wcols(w1, 512 * g + 256 * half, 256), 8, 256)
                for m in range(2):
                    for (t0, n) in BLKS[0:2]:
                        b, bf = pr.next()
                        for k in range(8):
                            last = pe(lambda e: e.matmul(b.ap[:, :], wv[:, k, 128 * m:128 * m + 128],
                                                         hv_[:, k, t0:t0 + n], start=(k == 0), stop=(k == 7)), tok,
                                      bf)
                        r1 = act(lambda e: e.activation(s.ap[:, 2 * half + m, t0:t0 + n], b.ap[:, :], ACT.Relu),
                                 last, sf)
                        b.give(r1)
                        done = pool(lambda e: e.tensor_tensor(
                            s.ap[:, 2 * half + m, t0:t0 + n], s.ap[:, 2 * half + m, t0:t0 + n],
                            s.ap[:, 2 * half + m, t0:t0 + n], ALU.mult), r1)
                ws.give(last)
            held.append((g, s, done))
            if len(held) == 2:
                second(*held.pop(0))
        second(*held.pop(0))
        P.barrier()

    def block1_end():
        CATV = CAT.t[:, M0:M0 + 8 * T].rearrange("p (a b) -> p a b", a=8)
        XT = restore_xT()
        out_proj(A["w_out"][0], XT, CATV, (m6(2), None), BLKS[0:2])
        c2 = norm_cols("norm2_g", 0, m6(4), m6(3))
        tmp = region(BR.lo + 10240, BR.hi)
        P.hT, P.hx = hT, []
        rms(XT, hT, BLKS[0:2], tmp, c2)
        P.barrier()
        mlp(XT)
        tmp.reset()
        rms(XT, XT, BLKS[0:2], tmp, None, g_only=col("final_norm_g", 0, 8))
        P.barrier()
        return XT

    C2 = {"aq": 0, "ak": 512, "av": 640, "az": 768, "mq": 1280, "mk": 1792, "mv": 2304, "mo": 2816, "mz": 3328,
          "mi": 3840, "mf": 3848}

    def mlstm(l, XT):
        w = A["w_in_2"][l]
        last_layer = l == 1
        lat_tiles = range(8) if last_layer else range(10)
        B1 = region(M0 + 10240, total - 10240)
        C1 = region(M0, M0 + 10240)
        CX = region(CON.at, CON.hi)
        vtm = C1.get(10, 4 * 129)
        U = C1.get(TT)
        colm, AB, par = CX.get(10, 4, 8), CX.get(8, 10), CX.get(2)
        B1.reset(B1.lo + 10240)
        G, I, Bc, M, t1 = B1.get(TT), B1.get(TT), B1.get(TT), B1.get(TT), B1.get(TT)
        MP, EN, BL = CX.get(10), CX.get(10), CX.get(10)
        R2, R3 = (C1.t[:, C1.at + TT * i:C1.at + TT * i + TT] for i in range(2))
        rows_proj(w, {0: (C2["mf"], 4), 1: (C2["mf"] + 4, 4), 2: (C2["mi"], 4), 3: (C2["mi"] + 4, 4)}, G)
        z0 = dve(lambda e: e.memset(par, 0.0))
        for q, off in enumerate((8, 12, 0, 4)):
            pl = load("mpar", par[32 * q:32 * q + 4, 0:1],
                      A["gate_b_2"][l, off:off + 4].rearrange("(a b) -> a b", b=1), z0)
        x_sp2 = store_late("xs", xs, XT, pl, P.rows_tok)
        h_sp2 = store_late("hs", hs, hT)
        dve(lambda e: e.tensor_scalar(G, G, par[:, 0:1], None, ALU.add), pl)
        dve(lambda e: e.tensor_copy(I[0:64, :], G[64:128, :]))
        F = G[0:64, :]
        dve(lambda e: e.tensor_scalar(F, F, -1.0, None, ALU.mult))
        softplus(F, t1[0:64, :], Bc[0:64, :])
        dve(lambda e: e.tensor_scalar(F, F, -1.0, None, ALU.mult), P.q["act"][-1])
        for d in range(2):
            q = slice(32 * d, 32 * d + 32)
            s = (lambda x: x[:, ::-1]) if d else (lambda x: x)
            dve(lambda e: e.tensor_tensor_scan(s(Bc[q, :]), s(rst[q, d, :]), s(G[q, :]), 0.0, ALU.mult, ALU.add))
            dve(lambda e: e.tensor_tensor_scan(s(M[q, T:TT]), s(G[q, T:TT]), s(I[q, T:TT]), NEG, ALU.add, ALU.max))
            e0 = TT - 1 if d == 0 else T
            dve(lambda e: e.tensor_tensor_scan(s(M[q, 0:T]), s(G[q, 0:T]), s(I[q, 0:T]), M[q, e0:e0 + 1], ALU.add,
                                               ALU.max))
            end = 127 if d == 0 else 0
            dve(lambda e: e.tensor_copy(EN[q, :], M[q, end:TT:128]))
            dve(lambda e: e.tensor_copy(BL[q, :], Bc[q, end:TT:128]))
            if d == 0:
                dve(lambda e: e.tensor_copy(MP[q, 1:10], EN[q, 0:9]))
                dve(lambda e: e.tensor_copy(MP[q, 0:1], EN[q, 9:10]))
                dve(lambda e: e.memset(MP[q, 8:9], NEG))
            else:
                dve(lambda e: e.tensor_copy(MP[q, 0:9], EN[q, 1:10]))
                dve(lambda e: e.memset(MP[q, 9:10], NEG))
        H = slice(0, 64)
        v10 = lambda x: x.rearrange("p (c t) -> p c t", c=10)
        b10 = lambda x: x.unsqueeze(2).to_broadcast([64, 10, 128])
        dve(lambda e: e.memset(U, 0.0))
        dve(lambda e: e.tensor_tensor(U[H, :], Bc[H, :], M[H, :], ALU.subtract))
        dve(lambda e: e.tensor_tensor(R2[H, :], I[H, :], Bc[H, :], ALU.subtract))
        dve(lambda e: e.tensor_tensor(v10(R2[64:128, :]), v10(U[H, :]), b10(MP[H, :]), ALU.add))
        dve(lambda e: e.tensor_scalar(R3[H, :], M[H, :], -1.0, None, ALU.mult))
        dve(lambda e: e.tensor_tensor(BL[H, :], BL[H, :], EN[H, :], ALU.subtract))
        dve(lambda e: e.tensor_tensor(v10(R3[64:128, :]), v10(R2[H, :]), b10(BL[H, :]), ALU.add))
        dve(lambda e: e.memset(EN, 0.0))
        rd = dve(lambda e: e.tensor_tensor(EN[H, :], BL[H, :], MP[H, :], ALU.add))

        def columns(pr):
            for c in range(10):
                b, bf = pr.next()
                pe(lambda e: e.transpose(b.ap[:, 0:128], R2[:, 128 * c:128 * c + 128], ident), rd, bf)
                t = pe(lambda e: e.transpose(b.ap[:, 128:256], R3[:, 128 * c:128 * c + 128], ident))
                src = b.ap[:, 0:256].rearrange("p (q r) -> p q r", q=8)[:, :, 0:4]
                ev = dve(lambda e: e.tensor_copy(colm[:, c, :, :].rearrange("p a b -> p (a b)").rearrange(
                    "p (q r) -> p q r", q=8), src), t)
                b.give(ev)
            ex = act(lambda e: e.activation(colm[:, :, 1:4, :], colm[:, :, 1:4, :], ACT.Exp), ev)
            dve(lambda e: e.tensor_scalar(colm[:, :, 3, :], colm[:, :, 3, :], 128 ** -0.5, None, ALU.mult), ex)
            b, bf = pr.next()
            for r in range(8):
                t = pe(lambda e: e.matmul(b.ap[:, 16 * r:16 * r + 10], sel[:, r, :], EN, start=True, stop=True), rd, bf)
            ab = act(lambda e: e.activation(AB, b.ap[:, 0:128].rearrange("p (a b) -> p a b", a=8)[:, :, 0:10], ACT.Exp), t)
            b.give(ab)

        P.fence["dve"] = P.fence["dve"] + [x_sp2]
        B1.reset()
        qT, kT, ktm = B1.get(4, TT), B1.get(4, TT), B1.get(10, 512)
        zr = Ring([Slot(B1.get(1028 + 260)) for _ in range(2)])
        for s in zr.slots:
            s.free = [dve(lambda e: e.memset(s.ap, 0.0))]
        cw, cwr = offs["conv_w_2"]
        pt = Ring([PSL[i] for i in (4, 5, 6, 7)])

        def outs(m):
            dst = (qT if m < 4 else kT)[:, m % 4, :]

            def fin(m, tok):
                if m < 4:
                    return
                for t0 in (0, 4, 8):
                    k = min(4, 10 - t0)
                    b, last = tr4([dst[:, 128 * (t0 + i):128 * (t0 + i) + 128] for i in range(k)], None, pt, tok)
                    o = ktm[:, t0:t0 + k, 128 * (m - 4):128 * (m - 4) + 128]
                    ev = dve(lambda e: e.tensor_copy(o, b.ap[:, 0:128 * k].rearrange("p (t c) -> p t c", t=k)), last)
                    b.give(ev)
            return dst, None, fin

        conv_channels(w, C2["mq"], 8, 5, T, lambda m, tap: vec[cw][:, cwr + 40 * l + 8 * tap + m:
                      cwr + 40 * l + 8 * tap + m + 1], lambda m: col("conv_b_2", 8 * l + m, 1), zr, outs,
                      fn=ACT.Silu)
        columns(pt)
        v5 = vtm.rearrange("p t (h x) -> p t h x", h=4)
        dve(lambda e: e.memset(v5[:, :, :, 128:129].rearrange("p t h x -> p (t h) x"), 1.0))

        def vsink(t, c, n, b, tok):
            o = v5[:, t, c // 128:c // 128 + 2, 0:128]
            return dve(lambda e: e.tensor_copy(o, b[:, 0:n].rearrange("p (h x) -> p h x", h=2)), tok)

        proj_tm(w, C2["mv"], 512, vsink, range(10))
        P.pending.append(h_sp2)
        P.barrier()
        H1 = region(total - 10240, total)
        hacc = H1.get(10, 512)
        B1.at = B1.lo + 3 * 5120
        hdone = {}

        def scan(d):
            E, Pm, wv, hn = H1.get(512), H1.get(512), H1.get(516), H1.get(516)
            Cs, dn = B1.get(516), B1.get(8)
            pr = Ring([PSL[4 * d + i] for i in range(3 if d and l == 0 else 4)])
            st = dve(lambda e: e.memset(Cs, 0.0))
            order = [8, 9] + list(range(8)) if d == 0 else [9, 8] + list(range(7, -1, -1))
            pe_last = None
            for c in order:
                want = c < 8 or not last_layer
                ts = slice(128 * c, 128 * c + 128)
                cc = lambda g, h, c=c: colm[:, c, g, 4 * d + h:4 * d + h + 1]
                wvd = pool(lambda e: e.tensor_tensor(h4(wv, 129), v5[:, c, :, :],
                                                     bc(colm[:, c, 3, 4 * d:4 * d + 4], 129), ALU.mult), pe_last)
                if want:
                    b, bf = pr.next()
                    for h in range(4):
                        t = pe(lambda e: e.matmul(b.ap[:, 128 * h:128 * h + 128], sel[:, 4 * d + h, :], U[:, ts],
                                                  start=True, stop=True), bf)
                    sb_, sf = pr.next()
                    for h in range(4):
                        t_s = pe(lambda e: e.matmul(sb_.ap[:, 128 * h:128 * h + 128], kT[:, h, ts], qT[:, h, ts],
                                                    start=True, stop=True), sf)
                    yield
                    for h in range(4):
                        a = dve(lambda e: e.scalar_tensor_tensor(
                            E[:, 128 * h:128 * h + 128], b.ap[:, 128 * h:128 * h + 128], cc(0, h), mt[:, d, :],
                            ALU.add, ALU.min), t)
                    b.give(a)
                    ex = act(lambda e: e.activation(E, E, ACT.Exp), a)
                    yield
                    pm_ = dve(lambda e: e.scalar_tensor_tensor(Pm, sb_.ap[:, :], 128 ** -0.5, E, ALU.mult, ALU.mult),
                              t_s, ex, pe_last)
                    sb_.give(pm_)
                    for hh in range(2):
                        xb, xf = pr.next()
                        yb, yf = pr.next()
                        for j in range(2):
                            h = 2 * hh + j
                            sl = slice(129 * h, 129 * h + 129)
                            tx = pe(lambda e: e.matmul(xb.ap[:, 129 * j:129 * j + 129], Pm[:, 128 * h:128 * h + 128],
                                                       vtm[:, c, sl], start=True, stop=True), pm_, xf)
                            ty = pe(lambda e: e.matmul(yb.ap[:, 129 * j:129 * j + 129], qT[:, h, ts], Cs[:, sl],
                                                       start=True, stop=True), st, yf)
                        cp = act(lambda e: e.activation(hn[:, 258 * hh:258 * hh + 258], xb.ap[:, 0:258], ACT.Copy),
                                 tx)
                        xb.give(cp)
                        for j in range(2):
                            h = 2 * hh + j
                            o = hn[:, 129 * h:129 * h + 129]
                            a = dve(lambda e: e.scalar_tensor_tensor(o, yb.ap[:, 129 * j:129 * j + 129], cc(1, h), o,
                                                                     ALU.mult, ALU.add), ty, cp)
                        yb.give(a)
                    yield
                    den = h4(hn, 129)[:, :, 128]
                    dve(lambda e: e.scalar_tensor_tensor(dn[:, 0:4], den, -1.0, den, ALU.mult, ALU.max))
                    dve(lambda e: e.tensor_tensor(dn[:, 0:4], dn[:, 0:4], colm[:, c, 2, 4 * d:4 * d + 4], ALU.max))
                    dve(lambda e: e.reciprocal(dn[:, 4:8], dn[:, 0:4]))
                    o = h4(hacc[:, c, :], 128)
                    num = h4(hn, 129)[:, :, 0:128]
                    if c not in hdone:
                        hdone[c] = dve(lambda e: e.tensor_tensor(o, num, bc(dn[:, 4:8], 128), ALU.mult))
                    else:
                        dve(lambda e: e.tensor_tensor(num, num, bc(dn[:, 4:8], 128), ALU.mult))
                        hdone[c] = dve(lambda e: e.tensor_tensor(o, o, num, ALU.add), hdone[c])
                yield
                bs = []
                for hh in range(2):
                    b, bf = pr.next()
                    for j in range(2):
                        h = 2 * hh + j
                        t = pe(lambda e: e.matmul(b.ap[:, 129 * j:129 * j + 129], ktm[:, c, 128 * h:128 * h + 128],
                                                  wv[:, 129 * h:129 * h + 129], start=True, stop=True), wvd, bf)
                    bs.append((b, t))
                pe_last = t
                for hh in range(2):
                    b, t = bs[hh]
                    for j in range(2):
                        h = 2 * hh + j
                        o = Cs[:, 129 * h:129 * h + 129]
                        st = dve(lambda e: e.scalar_tensor_tensor(o, o, AB[:, 4 * d + h, c:c + 1],
                                                                  b.ap[:, 129 * j:129 * j + 129], ALU.mult, ALU.add),
                                 t, pe_last)
                    b.give(st)
                yield

        interleave([scan(0), scan(1)] + ([ada(1, 2)] if l == 0 else []))
        P.barrier()
        B1.reset()
        load_hT(B1.get(8, TT))
        gb = B1.get(512)
        gl = load("gb", gb, A["head_g_2"][l].partition_broadcast(128))
        tr = Ring([Slot(B1.get(256)) for _ in range(4)])
        sq, s10 = B1.get(512), B1.get(10, 4)

        def osink(t, c, n, b, tok):
            s, sf = tr.next()
            a = act(lambda e: e.activation(s.ap, b[:, 0:n], ACT.Sigmoid), tok, sf)
            y = pool(lambda e: e.tensor_tensor(hacc[:, t, c:c + n], hacc[:, t, c:c + n], s.ap, ALU.mult), a)
            s.give(y)
            return a

        proj_tm(w, C2["mo"], 512, osink, lat_tiles)
        pl = P.q["pool"][-1]
        for t in lat_tiles:
            dve(lambda e: e.tensor_tensor(sq, hacc[:, t, :], hacc[:, t, :], ALU.mult), pl)
            a = dve(lambda e: e.tensor_reduce(s10[:, t, :], h4(sq, 128), AXX, ALU.add))
        nt = len(lat_tiles)
        a = dve(lambda e: e.tensor_scalar(s10[:, 0:nt, :], s10[:, 0:nt, :], 1.0 / 128, 1e-6, ALU.mult, ALU.add))
        act(lambda e: e.activation(s10[:, 0:nt, :], s10[:, 0:nt, :], ACT.Ln), a)
        a = act(lambda e: e.activation(s10[:, 0:nt, :], s10[:, 0:nt, :], ACT.Exp, scale=-0.5))
        for t in lat_tiles:
            dve(lambda e: e.tensor_tensor(h4(hacc[:, t, :], 128), h4(hacc[:, t, :], 128), bc(s10[:, t, :], 128),
                                          ALU.mult), a)
            nd = dve(lambda e: e.tensor_tensor(hacc[:, t, :], hacc[:, t, :], gb, ALU.mult), gl)
        catm = CAT.t[:, M0 + 5120:M0 + 10240].rearrange("p (m t) -> p m t", m=4)
        pt = Ring([PSL[i] for i in range(4)])

        late = []

        def turn():
            s, y, t, c = late.pop(0)
            b2, last = tr4([s.ap[:, 0:128], s.ap[:, 128:256]], None, pt, y)
            s.give(last)
            o = catm[:, c // 128:c // 128 + 2, 128 * t:128 * t + 128]
            b2.give(dve(lambda e: e.tensor_copy(o, b2.ap[:, 0:256].rearrange("p (m t) -> p m t", m=2)), last))

        def zsink(t, c, n, b, tok):
            s, sf = tr.next()
            a = act(lambda e: e.activation(s.ap, b[:, 0:n], ACT.Silu), tok, sf)
            y = pool(lambda e: e.tensor_tensor(s.ap, hacc[:, t, c:c + n], s.ap, ALU.mult), a, nd)
            late.append((s, y, t, c))
            if len(late) > 2:
                turn()
            return a

        proj_tm(w, C2["mz"], 512, zsink, lat_tiles)
        while late:
            turn()
        P.barrier()

    def attention(l):
        w = A["w_in_2"][l]
        last_layer = l == 1
        H1 = region(total - 10240, total)
        B1 = region(M0 + 10240 + 10240, total - 10240)
        cata = CAT.t[:, M0:M0 + 5120].rearrange("p (m t) -> p m t", m=4)
        hv_ = P.hT
        qT, kT, vtm = H1.get(4, TT), H1.get(TT), H1.get(10, 128)
        cos, sin, rot, wm = H1.get(T), H1.get(T), H1.get(128), H1.get(384)
        CX = region(CON.at, CON.hi)
        snk = CX.get(8)
        for dst, src in ((cos, A["c_cos"]), (sin, A["c_sin"]), (rot, A["c_rot"]), (wm, A["c_wm"]),
                         (snk, A["sink_2"][l].partition_broadcast(128))):
            cl = load("att", dst, src)
        t1 = Ring([Slot(B1.get(512)) for _ in range(2)])
        t2 = Ring([Slot(B1.get(512)) for _ in range(2)])
        pr = Ring([PSL[i] for i in range(4)])
        p2 = Ring([PSL[i] for i in range(4, 8)])

        def rope_sink(dst, t0, n, b, tok):
            if t0 >= T:
                return act(lambda e: e.activation(dst, b.ap[:, 0:n], ACT.Copy), tok)
            s, sf = t1.next()
            a = act(lambda e: e.activation(s.ap, b.ap[:, :], ACT.Copy), tok, sf)
            b2, bf2 = p2.next()
            r = pe(lambda e: e.matmul(b2.ap[:, :], rot, s.ap, start=True, stop=True), a, bf2, cl)
            u, uf = t2.next()
            rs = dve(lambda e: e.tensor_tensor(u.ap, b2.ap[:, :], sin[:, t0:t0 + n], ALU.mult), r, uf, cl)
            b2.give(rs)
            m = pool(lambda e: e.tensor_tensor(s.ap, s.ap, cos[:, t0:t0 + n], ALU.mult), r, a, cl)
            f = dve(lambda e: e.tensor_tensor(dst, s.ap, u.ap, ALU.add), m)
            s.give(f)
            u.give(f)
            return a

        for j in range(0, 6, 2):
            s, free = W.next()
            nt = 2 if j < 4 else 1
            view = s.ap[:, 0:8 * 128 * nt].rearrange("p (k n) -> p k n", k=8)
            if j < 4:
                for m in range(2):
                    for hf in range(2):
                        c0 = 64 * (j + m + 4 * hf)
                        tok = P.dma(s.lane, lambda e: e.dma_start(
                            view[:, :, 128 * m + 64 * hf:128 * m + 64 * hf + 64], wcols(w, c0, 64)), free)
            else:
                tok = P.dma(s.lane, lambda e: e.dma_start(view, wcols(w, C2["ak"], 128)), free)
            for m in range(nt):
                for (t0, n) in BLKS:
                    b, bf = pr.next()
                    for k in range(8):
                        last = pe(lambda e: e.matmul(b.ap[:, 0:n], view[:, k, 128 * m:128 * m + 128],
                                                     hv_[:, k, t0:t0 + n], start=(k == 0), stop=(k == 7)), tok, bf,
                                  hx(t0))
                    dst = qT[:, j + m, t0:t0 + n] if j < 4 else kT[:, t0:t0 + n]
                    b.give(rope_sink(dst, t0, n, b, last))
            s.give(last)

        def vsink(t, c, n, b, tok):
            return act(lambda e: e.activation(vtm[:, t, :], b[:, 0:n], ACT.Copy), tok)

        proj_tm(w, C2["av"], 128, vsink, range(10))
        P.barrier()
        B1.reset()
        zs = [wload(wcols(w, C2["az"] + 256 * i, 256), 8, 256) for i in range(2)]
        Sr = Ring([Slot(B1.get(4, 640)) for _ in range(2)])
        Pr = Ring([Slot(B1.get(640)) for _ in range(2)])
        og, zg = B1.get(512), H1.t[:, H1.lo + 7680:H1.lo + 8192]
        st = CX.get(2, 24)
        sb_ = Ring([PSL[i] for i in (0, 1, 2, 3)])
        tb = Ring([PSL[i] for i in (4, 5)])
        ob = Ring([PSL[i] for i in (6, 7)])
        scale = 64 ** -0.5
        blocks = range(8) if last_layer else range(10)
        NB = {n: [] if n >= 8 else [k for k in (n - 1, n, n + 1) if 0 <= k < 8] for n in blocks}
        state = {"og": None, "zg": None}

        def scores(n, g):
            kb = NB[n]
            S, Sf = Sr.next()
            for h in range(4):
                q = qT[64 * g:64 * g + 64, h, 128 * n:128 * n + 128]
                if kb:
                    b, bf = sb_.next()
                    c0, c1 = 128 * (kb[0] - n + 1), 128 * (kb[-1] - n + 2)
                    t = pe(lambda e: e.matmul(b.ap[:, c0:c1], q, kT[64 * g:64 * g + 64,
                                                                   128 * kb[0]:128 * kb[-1] + 128],
                                              start=True, stop=True), bf)
                    ev1 = dve(lambda e: e.scalar_tensor_tensor(S.ap[:, h, c0:c1], b.ap[:, c0:c1], scale,
                                                               wm[:, c0:c1], ALU.mult, ALU.add), t, Sf)
                    b.give(ev1)
                    if n == 7:
                        dve(lambda e: e.memset(S.ap[:, h, 256:384], NEG))
                b, bf = sb_.next()
                t = pe(lambda e: e.matmul(b.ap[:, 0:256], q, kT[64 * g:64 * g + 64, T:TT], start=True,
                                          stop=True), bf)
                ev2 = act(lambda e: e.activation(S.ap[:, h, 384:640], b.ap[:, 0:256], ACT.Copy, scale=scale), t,
                          Sf)
                b.give(ev2)
            return S, ev2

        def largest(n, g, S, ev2):
            lo = 384 if n >= 8 else (128 if n == 0 else 0)
            mx, nm, es = (st[:, g, 4 * i:4 * i + 4] for i in (0, 1, 3))
            dve(lambda e: e.tensor_reduce(mx, S.ap[:, :, lo:640], AXX, ALU.max), ev2)
            dve(lambda e: e.tensor_tensor(mx, mx, snk[:, 4 * g:4 * g + 4], ALU.max), cl)
            dve(lambda e: e.tensor_scalar(nm, mx, -1.0, None, ALU.mult))
            dd = dve(lambda e: e.tensor_tensor(es, snk[:, 4 * g:4 * g + 4], mx, ALU.subtract))
            return dd

        def exponentials(n, g, S, dd):
            lo = 384 if n >= 8 else (128 if n == 0 else 0)
            nm, sm, es = (st[:, g, 4 * i:4 * i + 4] for i in (1, 2, 3))
            exs = []
            for h in range(4):
                exs.append(act(lambda e: e.activation(S.ap[:, h, lo:640], S.ap[:, h, lo:640], ACT.Exp,
                                                      bias=nm[:, h:h + 1], accum_out=sm[:, h:h + 1]), dd))
            ea = act(lambda e: e.activation(es, es, ACT.Exp))
            return S, exs, ea

        def values(n, g, S, exs, ea, o_, of, between):
            sm, es = st[:, g, 8:12], st[:, g, 12:16]
            kt = [(k - n + 1, k) for k in NB[n]] + [(3, 8), (4, 9)]
            prev = None

            def pv(h, p, evs):
                hd = 4 * g + h
                for i, (slot, k) in enumerate(kt):
                    t = pe(lambda e: e.matmul(o_.ap[:, 64 * hd:64 * hd + 64], p.ap[:, 128 * i:128 * i + 128],
                                              vtm[:, k, 64 * g:64 * g + 64], start=(i == 0),
                                              stop=(i == len(kt) - 1)), evs, of)
                p.give(t)
                return t

            for h in range(4):
                p, pf = Pr.next()
                evs = []
                for i0 in range(0, len(kt), 4):
                    b, bf = tb.next()
                    grp = kt[i0:i0 + 4]
                    for i, (slot, k) in enumerate(grp):
                        t = pe(lambda e: e.transpose(b.ap[:, 128 * i:128 * i + 128],
                                                     S.ap[:, h, 128 * slot:128 * slot + 128], ident), exs[h], bf)
                    o = p.ap[:, 128 * i0:128 * (i0 + len(grp))]
                    if i0 == 0 and h % 2:
                        ev = dve(lambda e: e.tensor_copy(o, b.ap[:, 0:128 * len(grp)]), t, pf)
                    else:
                        ev = act(lambda e: e.activation(o, b.ap[:, 0:128 * len(grp)], ACT.Copy), t, pf)
                    b.give(ev)
                    evs.append(ev)
                if h == 1:
                    dd = between()
                if prev is not None:
                    pv(*prev)
                prev = (h, p, evs)
            t = pv(*prev)
            S.give(t)
            dve(lambda e: e.tensor_tensor(sm, sm, es, ALU.add), ea)
            dve(lambda e: e.reciprocal(sm, sm))
            o4 = o_.ap[:, 256 * g:256 * g + 256].rearrange("p (h x) -> p h x", h=4)
            return dve(lambda e: e.tensor_tensor(h4(og[:, 256 * g:256 * g + 256], 64), o4, bc(sm, 64), ALU.mult), t,
                       state["og"]), dd

        def gates(n):
            for i in range(2):
                b, bf = sb_.next()
                wv, tok = zs[i][1], zs[i][2]
                for k in range(8):
                    t = pe(lambda e: e.matmul(b.ap[:, 0:256], hv_[:, k, 128 * n:128 * n + 128], wv[:, k, :],
                                              start=(k == 0), stop=(k == 7)), tok, bf)
                a = act(lambda e: e.activation(zg[:, 256 * i:256 * i + 256], b.ap[:, 0:256], ACT.Silu), t,
                        state["zg"])
                b.give(a)
            return a, t

        def finish(n, a):
            m = dve(lambda e: e.tensor_tensor(og, og, zg, ALU.mult), a)
            state["zg"] = m
            b, last = tr4([og[:, 128 * i:128 * i + 128] for i in range(4)], None, tb, m)
            state["og"] = last
            ev = act(lambda e: e.activation(cata[:, :, 128 * n:128 * n + 128],
                                            b.ap[:, :].rearrange("p (m t) -> p m t", m=4), ACT.Copy), last)
            b.give(ev)

        units = [(n, g) for n in blocks for g in range(2)]
        S0 = scores(*units[0])
        pend = exponentials(*units[0], S0[0], largest(*units[0], *S0))
        for u, (n, g) in enumerate(units):
            o_, of = ob.next()
            more = units[u + 1] if u + 1 < len(units) else None
            nxt = scores(*more) if more else None
            if g == 1:
                a, zlast = gates(n)
            ev, dd = values(n, g, *pend, o_, of, lambda: largest(*more, *nxt) if more else None)
            o_.give(ev)
            if g == 1:
                finish(n, a)
            pend = exponentials(*more, nxt[0], dd) if more else None
        for z_ in zs:
            z_[0].give(zlast)
        P.barrier()

    def block2(XT):
        R1.reset()
        load_xT(XT, [(A["ctx_2"][0], T)])
        P.barrier()
        for l in range(2):
            md = adac[:, l, :, :]
            c = norm_cols("norm_g_2", 8 * l, md[:, 8:16, 0], md[:, 0:8, 0], md[:, 8:16, 1], md[:, 0:8, 1])
            tmp = region(BR.lo + 10240, BR.hi)
            P.barrier()
            P.hT, P.hx = hT, []
            rms(XT, hT, BLKS, tmp, c)
            P.barrier()
            mlstm(l, XT)
            attention(l)
            XT = restore_xT()
            CATV = CAT.t[:, M0:M0 + 8 * TT].rearrange("p (a b) -> p a b", a=8)
            out_proj(A["w_out_2"][l], XT, CATV, (md[:, 16:24, 0], md[:, 16:24, 1]), BLKS if l == 0 else BLKS[0:2])
        tmp = region(BR.lo + 10240, BR.hi)
        rms(XT, XT, BLKS[0:2], tmp, None, g_only=col("final_g_2", 0, 8))
        P.barrier()
        st = Ring([Slot(R1.t[:, R1.lo + 1024 * i:R1.lo + 1024 * i + 1024], lane=f"o{i}") for i in range(3)])
        pr = Ring(PSL)
        for t in range(8):
            s, sf = st.next()
            evs = []
            for half in range(2):
                b, last = tr4([XT[:, 4 * half + k, 128 * t:128 * t + 128] for k in range(4)], None, pr, None)
                dst = s.ap[:, 512 * half:512 * half + 512]
                if half:
                    ev = dve(lambda e: e.tensor_copy(dst, b.ap[:, :]), last, sf)
                else:
                    ev = act(lambda e: e.activation(dst, b.ap[:, :], ACT.Copy), last, sf)
                b.give(ev)
                evs.append(ev)
            it = P.dma(s.lane, lambda e: e.dma_start(out[0, 128 * t:128 * t + 128, :], s.ap), *evs, eng="pool")
            s.give(it)
            P.outs = [x for x in P.outs if x.lane != s.lane] + [it]

    gdn()
    gla()
    hyena()
    XT = block1_end()
    block2(XT)

_OUTS = [((1, 1024, 1024), "float32")]


def kernel(**inputs):
    import numpy as _np
    import concourse.bacc as _bacc
    from concourse import mybir as _mybir
    from concourse.bass_utils import run_bass_kernel_spmd as _run

    nc = _bacc.Bacc("TRN2", target_bir_lowering=False, num_devices=1)
    arrays = {f"in_{k}": _np.ascontiguousarray(v) for k, v in inputs.items()}
    arrays.update(constants())
    A = {}
    for name, a in arrays.items():
        A[name.removeprefix("in_")] = nc.dram_tensor(name, a.shape, _mybir.dt.from_np(a.dtype), kind="ExternalInput").ap()
    o = nc.dram_tensor("out_0", _OUTS[0][0], F32, kind="ExternalOutput").ap()
    build(nc, A, o)
    r = _run(nc, [arrays], core_ids=[0])
    return r.results[0]["out_0"]
```
